# Optimizing a Trainium2 kernel written in Bass

```python
import math
import jax
import jax.numpy as jnp
from jax import lax
import numpy as np

D_MODEL = 1024
BATCH = 1
SEQ = 128
DEPTH = 2
DEC_BATCH = 1
DEC_SEQ = 512
PAST_LEN = 128

GRID_W = 64
N_BRANCH = 4
BR_W = 512
H_A = 4
DK_A = 128
DV_A = 128
CHUNK = 64
CONV_K = 3
HY_BANDS = 16
HY_EMB = 1 + 2 * HY_BANDS
HY_FF = 64
H_C = 4
DH_C = 128
WIN_R = 8
WIN_C = 16
H_D = 4
DQK_D = 64
DV_D = 128
Q_BLOCK = 128
ROPE_BASE = 10000.0
EPS = 1e-6

N_A = 4 * BR_W + 4 * H_A
N_B = 4 * BR_W
N_C = 4 * BR_W
N_D = 4 * BR_W
N_IN = N_A + N_B + N_C + N_D

kernel_name = 'hybrid_prefix_diffusion_trunk_step'

def rmsnorm(x, g):
    xf = x.astype(jnp.float32)
    xf = xf * lax.rsqrt(jnp.mean(xf * xf, axis=-1, keepdims=True) + EPS)
    return (xf * g.astype(jnp.float32)).astype(x.dtype)

def l2norm(x):
    xf = x.astype(jnp.float32)
    return xf * lax.rsqrt(jnp.sum(xf * xf, axis=-1, keepdims=True) + EPS)

def dwconv(x, w):
    k = w.shape[0]
    return lax.conv_general_dilated(x, w[:, None, :].astype(x.dtype), window_strides=(1,),
                                    padding=[(k // 2, k // 2)],
                                    dimension_numbers=('NWC', 'WIO', 'NWC'),
                                    feature_group_count=x.shape[-1])

def heads(x, n):
    b, l, _ = x.shape
    return x.reshape(b, l, n, -1).transpose(0, 2, 1, 3)

def merge_heads(x):
    b, n, l, d = x.shape
    return x.transpose(0, 2, 1, 3).reshape(b, l, n * d)

def split_maps(t):
    b, h, l, _ = t.shape
    return t.reshape(b, h, l, 2, DQK_D).transpose(0, 1, 3, 2, 4)

def axial_rope(x):
    l, d = x.shape[-2], x.shape[-1]
    half = d // 2
    nf = half // 2
    t = jnp.arange(l)
    row = (t // GRID_W).astype(jnp.float32)
    col = (t % GRID_W).astype(jnp.float32)
    inv = ROPE_BASE ** (-jnp.arange(nf, dtype=jnp.float32) / nf)
    ang = jnp.concatenate([row[:, None] * inv, col[:, None] * inv], axis=-1)
    cos, sin = jnp.cos(ang), jnp.sin(ang)
    xf = x.astype(jnp.float32)
    x1, x2 = xf[..., :half], xf[..., half:]
    return jnp.concatenate([x1 * cos - x2 * sin, x2 * cos + x1 * sin], axis=-1).astype(x.dtype)

def gdn_chunked(q, k, v, g, beta, s0):
    b, h, l, dk = q.shape
    dv = v.shape[-1]
    n = l // CHUNK
    q = q.astype(jnp.float32).reshape(b, h, n, CHUNK, dk)
    k = k.astype(jnp.float32).reshape(b, h, n, CHUNK, dk)
    v = v.astype(jnp.float32).reshape(b, h, n, CHUNK, dv)
    beta = beta.astype(jnp.float32).reshape(b, h, n, CHUNK, 1)
    gc = jnp.cumsum(g.astype(jnp.float32).reshape(b, h, n, CHUNK), axis=-1)
    incl = jnp.tril(jnp.ones((CHUNK, CHUNK), dtype=bool))
    strict = jnp.tril(jnp.ones((CHUNK, CHUNK), dtype=bool), -1)
    rel = gc[..., :, None] - gc[..., None, :]
    decay = jnp.where(incl, jnp.exp(jnp.where(incl, rel, 0.0)), 0.0)
    kb = k * beta
    lower = jnp.where(strict, jnp.einsum('bhnid,bhnjd->bhnij', kb, k) * decay, 0.0)
    rhs = jnp.concatenate([v * beta, kb * jnp.exp(gc)[..., None]], axis=-1)
    sol = lax.linalg.triangular_solve(lower + jnp.eye(CHUNK, dtype=jnp.float32), rhs,
                                      left_side=True, lower=True, unit_diagonal=True)
    u, w = sol[..., :dv], sol[..., dv:]
    a_intra = jnp.where(incl, jnp.einsum('bhnid,bhnjd->bhnij', q, k) * decay, 0.0)
    q_dec = q * jnp.exp(gc)[..., None]
    k_dec = k * jnp.exp(gc[..., -1:] - gc)[..., None]
    g_last = jnp.exp(gc[..., -1])

    def step(s, xs):
        u_i, w_i, q_i, k_i, a_i, gl_i = xs
        v_new = u_i - jnp.einsum('bhik,bhkv->bhiv', w_i, s)
        o_i = jnp.einsum('bhik,bhkv->bhiv', q_i, s) + jnp.einsum('bhij,bhjv->bhiv', a_i, v_new)
        s = s * gl_i[..., None, None] + jnp.einsum('bhik,bhiv->bhkv', k_i, v_new)
        return s, o_i

    xs = tuple(jnp.moveaxis(t, 2, 0) for t in (u, w, q_dec, k_dec, a_intra, g_last))
    s_fin, o = lax.scan(step, s0.astype(jnp.float32), xs)
    return jnp.moveaxis(o, 0, 2).reshape(b, h, l, dv), s_fin

def gdn_branch(pa, conv_w, a_log, dt_bias, norm_g, s0):
    b, l, _ = pa.shape
    qkv = jax.nn.silu(dwconv(pa[..., :3 * BR_W], conv_w))
    q = l2norm(heads(qkv[..., :BR_W], H_A)) * (DK_A ** -0.5)
    k = l2norm(heads(qkv[..., BR_W:2 * BR_W], H_A))
    v = heads(qkv[..., 2 * BR_W:], H_A)
    z = pa[..., 3 * BR_W:4 * BR_W]
    ab = pa[..., 4 * BR_W:].astype(jnp.float32).reshape(b, l, 2, 2, H_A).transpose(2, 3, 0, 4, 1)
    g_all = -jnp.exp(a_log.astype(jnp.float32))[:, None, :, None] * jax.nn.softplus(
        ab[:, 0] + dt_bias.astype(jnp.float32)[:, None, :, None])
    beta_all = jax.nn.sigmoid(ab[:, 1])
    o_f, s_f = gdn_chunked(q, k, v, g_all[0], beta_all[0], s0[:, 0])
    rev = lambda t: jnp.flip(t, axis=2)
    o_b, s_b = gdn_chunked(rev(q), rev(k), rev(v), rev(g_all[1]), rev(beta_all[1]), s0[:, 1])
    o = rmsnorm(o_f + rev(o_b), norm_g)
    y = merge_heads(o) * jax.nn.silu(z.astype(jnp.float32))
    return y.astype(pa.dtype), jnp.stack([s_f, s_b], axis=1)

def hyena_filters(l, w1, b1, w2, b2, w3, b3, decay):
    pos = jnp.arange(l, dtype=jnp.float32)
    t = pos / l
    ang = (2.0 * math.pi) * t[:, None] * jnp.arange(1, HY_BANDS + 1, dtype=jnp.float32)
    feat = jnp.concatenate([t[:, None], jnp.cos(ang), jnp.sin(ang)], axis=-1)
    hid = jnp.sin(feat @ w1 + b1)
    hid = jnp.sin(hid @ w2 + b2)
    filt = (hid @ w3 + b3).astype(jnp.float32)
    dist = jnp.abs(pos - l // 2) / l
    return filt * jnp.exp(-dist[:, None] * jnp.abs(decay.astype(jnp.float32)))

def fft_conv_centred(u, h, skip):
    l = u.shape[1]
    uf = jnp.fft.rfft(u.astype(jnp.float32), n=2 * l, axis=1)
    hf = jnp.fft.rfft(h, n=2 * l, axis=0)
    y = jnp.fft.irfft(uf * hf[None], n=2 * l, axis=1)[:, l // 2:l // 2 + l]
    return y + u.astype(jnp.float32) * skip.astype(jnp.float32)

def hyena_branch(pb, conv_w, w1, b1, w2, b2, w3, b3, decay, skip):
    l = pb.shape[1]
    proj = dwconv(pb[..., :3 * BR_W], conv_w)
    v, x1, x2 = proj[..., :BR_W], proj[..., BR_W:2 * BR_W], proj[..., 2 * BR_W:]
    filt = hyena_filters(l, w1, b1, w2, b2, w3, b3, decay)
    z = x1.astype(jnp.float32) * fft_conv_centred(v, filt[:, :BR_W], skip[0])
    z = x2.astype(jnp.float32) * fft_conv_centred(z, filt[:, BR_W:], skip[1])
    return (z * jax.nn.silu(pb[..., 3 * BR_W:].astype(jnp.float32))).astype(pb.dtype)

def blocked_attn(q, k, v):
    b, h, lq, d = q.shape
    qb = jnp.moveaxis(q.reshape(b, h, lq // Q_BLOCK, Q_BLOCK, d), 2, 0)

    def block(q_i):
        s = jnp.einsum('bhqd,bhkd->bhqk', q_i, k).astype(jnp.float32) * (d ** -0.5)
        pr = jax.nn.softmax(s, axis=-1).astype(v.dtype)
        return jnp.einsum('bhqk,bhkd->bhqd', pr, v)

    o = lax.map(block, qb)
    return jnp.moveaxis(o, 0, 2).reshape(b, h, lq, v.shape[-1])

def nat_latent(q, k, v, ck, cv, rpb):
    b, h, l, d = q.shape
    rows = l // GRID_W
    kr = min(WIN_R, rows)
    cols = jnp.arange(GRID_W)
    col_idx = jnp.clip(cols - WIN_C // 2, 0, GRID_W - WIN_C)[:, None] + jnp.arange(WIN_C)[None, :]
    dc = col_idx - cols[:, None] + (WIN_C - 1)
    qg = q.reshape(b, h, rows, GRID_W, d)
    kg = k.reshape(b, h, rows, GRID_W, d)
    vg = v.reshape(b, h, rows, GRID_W, d)
    scale = d ** -0.5

    def row_block(r):
        rs = jnp.clip(r - kr // 2, 0, rows - kr)
        q_r = lax.dynamic_index_in_dim(qg, r, axis=2, keepdims=False)
        k_w = lax.dynamic_slice_in_dim(kg, rs, kr, axis=2)[:, :, :, col_idx]
        v_w = lax.dynamic_slice_in_dim(vg, rs, kr, axis=2)[:, :, :, col_idx]
        dr = rs + jnp.arange(kr) - r + (WIN_R - 1)
        bias = rpb[:, dr[None, :, None], dc[:, None, :]].astype(jnp.float32)
        s_lat = jnp.einsum('bhqd,bhjqcd->bhqjc', q_r, k_w).astype(jnp.float32) * scale + bias[None]
        s_ctx = jnp.einsum('bhqd,bhsd->bhqs', q_r, ck).astype(jnp.float32) * scale
        pr = jax.nn.softmax(jnp.concatenate([s_lat.reshape(b, h, GRID_W, kr * WIN_C), s_ctx], axis=-1),
                            axis=-1).astype(v.dtype)
        p_lat = pr[..., :kr * WIN_C].reshape(b, h, GRID_W, kr, WIN_C)
        return (jnp.einsum('bhqjc,bhjqcd->bhqd', p_lat, v_w)
                + jnp.einsum('bhqs,bhsd->bhqd', pr[..., kr * WIN_C:], cv))

    o = lax.map(row_block, jnp.arange(rows))
    return jnp.transpose(o, (1, 2, 0, 3, 4)).reshape(b, h, l, d)

def diff_attn(q, k, v, lam):
    b, h, _, lq, dq = q.shape
    qb = jnp.moveaxis(q.reshape(b, h, 2, lq // Q_BLOCK, Q_BLOCK, dq), 3, 0)

    def block(q_i):
        s = jnp.einsum('bhmqd,bhmkd->bhmqk', q_i, k).astype(jnp.float32) * (dq ** -0.5)
        pr = jax.nn.softmax(s, axis=-1)
        a = (pr[:, :, 0] - lam * pr[:, :, 1]).astype(v.dtype)
        return jnp.einsum('bhqk,bhkd->bhqd', a, v)

    o = lax.map(block, qb)
    return jnp.moveaxis(o, 0, 2).reshape(b, h, lq, v.shape[-1])

def trunk_layer(x, mod, p, layer, ctx):
    b, l, _ = x.shape
    latent = ctx is not None
    shift, scale, gate = jnp.split(mod, 3, axis=-1)
    h = rmsnorm(x, p['g_pre']) * (1.0 + scale) + shift
    proj = h @ p['w_in']
    pa = proj[..., :N_A]
    pb = proj[..., N_A:N_A + N_B]
    pc = proj[..., N_A + N_B:N_A + N_B + N_C]
    pd = proj[..., N_A + N_B + N_C:]

    s0 = ctx['gdn'] if latent else jnp.zeros((b, 2, H_A, DK_A, DV_A), jnp.float32)
    ya, s_fin = gdn_branch(pa, p['gdn_conv'], p['gdn_a_log'], p['gdn_dt_bias'], p['gdn_norm'], s0)

    yb = hyena_branch(pb, p['hy_conv'], p['hy_w1'], p['hy_b1'], p['hy_w2'], p['hy_b2'],
                      p['hy_w3'], p['hy_b3'], p['hy_decay'], p['hy_skip'])

    qc = heads(pc[..., :BR_W], H_C)
    kc = heads(pc[..., BR_W:2 * BR_W], H_C)
    vc = heads(pc[..., 2 * BR_W:3 * BR_W], H_C)
    if latent:
        oc = nat_latent(qc, kc, vc, ctx['nat_k'], ctx['nat_v'], p['nat_rpb'])
    else:
        oc = blocked_attn(qc, kc, vc)
    yc = merge_heads(oc) * jax.nn.silu(pc[..., 3 * BR_W:])

    qd = pd[..., :BR_W].reshape(b, l, H_D, 2, DQK_D).transpose(0, 2, 3, 1, 4)
    kd_flat = heads(pd[..., BR_W:2 * BR_W], H_D)
    vd = heads(pd[..., 2 * BR_W:3 * BR_W], H_D)
    lam_init = 0.8 - 0.6 * math.exp(-0.3 * layer)
    lam_p = p['diff_lam'].astype(jnp.float32)
    lam = jnp.exp(jnp.sum(lam_p[0] * lam_p[1])) - jnp.exp(jnp.sum(lam_p[2] * lam_p[3])) + lam_init
    if latent:
        keys = jnp.concatenate([axial_rope(split_maps(kd_flat)), split_maps(ctx['diff_k'])], axis=3)
        vals = jnp.concatenate([vd, ctx['diff_v']], axis=2)
        od = diff_attn(axial_rope(qd), keys, vals, lam)
    else:
        od = diff_attn(qd, split_maps(kd_flat), vd, lam)
    yd = merge_heads(rmsnorm(od, p['diff_norm']) * (1.0 - lam_init)) * jax.nn.silu(pd[..., 3 * BR_W:])

    ys = jnp.stack([t.astype(x.dtype) for t in (ya, yb, yc, yd)], axis=2)
    br = jnp.einsum('blkw,kwd->blkd', ys, p['w_branch'])
    gates = jax.nn.sigmoid((h @ p['w_merge'] + p['b_merge']).astype(jnp.float32)).reshape(b, l, N_BRANCH, D_MODEL)
    y = jnp.sum(gates * br.astype(jnp.float32), axis=2).astype(x.dtype) @ p['w_out']
    x = x + gate * rmsnorm(y, p['g_post'])
    if latent:
        return x, None
    return x, (s_fin, jnp.stack([kc, vc], axis=1), jnp.stack([kd_flat, vd], axis=1))

def setup_inputs(seed: int = 0) -> dict:
    key = jax.random.key(seed)
    ks = jax.random.split(key, 32)
    f32 = jnp.float32
    nrm = lambda i, shape, s: jax.random.normal(ks[i], shape, f32) * s
    dt = jnp.exp(jax.random.uniform(ks[14], (DEPTH, 2, H_A), f32, math.log(1e-3), math.log(1e-1)))
    return {
        'x_prompt': nrm(0, (BATCH, SEQ, D_MODEL), 1.0),
        'x_sample': nrm(1, (DEC_BATCH, DEC_SEQ, D_MODEL), 1.0),
        'state_gdn': nrm(2, (DEC_BATCH, DEPTH, 2, H_A, DK_A, DV_A), 0.5),
        'cache_nat_kv': nrm(3, (DEC_BATCH, DEPTH, 2, H_C, PAST_LEN, DH_C), 1.0),
        'cache_diff_kv': nrm(4, (DEC_BATCH, DEPTH, 2, H_D, PAST_LEN, 2 * DQK_D), 1.0),
        'c': nrm(5, (DEC_BATCH, D_MODEL), 1.0),
        'c_ctx': nrm(6, (D_MODEL,), 1.0),
        'w_mod': nrm(7, (DEPTH, D_MODEL, 3 * D_MODEL), D_MODEL ** -0.5),
        'b_mod': nrm(8, (DEPTH, 3 * D_MODEL), 0.02),
        'g_pre': 1.0 + nrm(9, (DEPTH, D_MODEL), 0.02),
        'g_post': 1.0 + nrm(10, (DEPTH, D_MODEL), 0.02),
        'w_in': nrm(11, (DEPTH, D_MODEL, N_IN), D_MODEL ** -0.5),
        'gdn_conv': nrm(12, (DEPTH, CONV_K, 3 * BR_W), CONV_K ** -0.5),
        'gdn_a_log': jnp.log(jax.random.uniform(ks[13], (DEPTH, 2, H_A), f32, 1.0, 16.0)),
        'gdn_dt_bias': dt + jnp.log(-jnp.expm1(-dt)),
        'gdn_norm': 1.0 + nrm(15, (DEPTH, DV_A), 0.02),
        'hy_conv': nrm(16, (DEPTH, CONV_K, 3 * BR_W), CONV_K ** -0.5),
        'hy_w1': nrm(17, (DEPTH, HY_EMB, HY_FF), HY_EMB ** -0.5),
        'hy_b1': nrm(18, (DEPTH, HY_FF), 0.1),
        'hy_w2': nrm(19, (DEPTH, HY_FF, HY_FF), HY_FF ** -0.5),
        'hy_b2': nrm(20, (DEPTH, HY_FF), 0.1),
        'hy_w3': nrm(21, (DEPTH, HY_FF, 2 * BR_W), 0.1 * HY_FF ** -0.5),
        'hy_b3': nrm(22, (DEPTH, 2 * BR_W), 0.01),
        'hy_decay': jax.random.uniform(ks[23], (DEPTH, 2 * BR_W), f32, 3.0, 30.0),
        'hy_skip': nrm(24, (DEPTH, 2, BR_W), 0.5),
        'nat_rpb': nrm(25, (DEPTH, H_C, 2 * WIN_R - 1, 2 * WIN_C - 1), 0.1),
        'diff_lam': nrm(26, (DEPTH, 4, DQK_D), 0.1),
        'diff_norm': 1.0 + nrm(27, (DEPTH, DV_D), 0.02),
        'w_branch': nrm(28, (DEPTH, N_BRANCH, BR_W, D_MODEL), BR_W ** -0.5),
        'w_merge': nrm(29, (DEPTH, D_MODEL, N_BRANCH * D_MODEL), D_MODEL ** -0.5),
        'b_merge': nrm(30, (DEPTH, N_BRANCH * D_MODEL), 0.02),
        'w_out': nrm(31, (DEPTH, D_MODEL, D_MODEL), D_MODEL ** -0.5),
    }

def reference(x_prompt, x_sample, state_gdn, cache_nat_kv, cache_diff_kv, c, c_ctx,
              w_mod, b_mod, g_pre, g_post, w_in, gdn_conv, gdn_a_log, gdn_dt_bias, gdn_norm,
              hy_conv, hy_w1, hy_b1, hy_w2, hy_b2, hy_w3, hy_b3, hy_decay, hy_skip,
              nat_rpb, diff_lam, diff_norm, w_branch, w_merge, b_merge, w_out):
    stacked = {
        'w_mod': w_mod, 'b_mod': b_mod, 'g_pre': g_pre, 'g_post': g_post, 'w_in': w_in,
        'gdn_conv': gdn_conv, 'gdn_a_log': gdn_a_log, 'gdn_dt_bias': gdn_dt_bias, 'gdn_norm': gdn_norm,
        'hy_conv': hy_conv, 'hy_w1': hy_w1, 'hy_b1': hy_b1, 'hy_w2': hy_w2, 'hy_b2': hy_b2,
        'hy_w3': hy_w3, 'hy_b3': hy_b3, 'hy_decay': hy_decay, 'hy_skip': hy_skip,
        'nat_rpb': nat_rpb, 'diff_lam': diff_lam, 'diff_norm': diff_norm,
        'w_branch': w_branch, 'w_merge': w_merge, 'b_merge': b_merge, 'w_out': w_out,
    }

    y_prompt = x_prompt
    gdn_states, nat_kvs, diff_kvs = [], [], []
    for layer in range(DEPTH):
        p = {name: arr[layer] for name, arr in stacked.items()}
        mod = jax.nn.silu(c_ctx) @ p['w_mod'] + p['b_mod']
        y_prompt, (s_l, nat_l, diff_l) = trunk_layer(y_prompt, mod, p, layer, None)
        gdn_states.append(s_l)
        nat_kvs.append(nat_l)
        diff_kvs.append(diff_l)
    new_state_gdn = jnp.stack(gdn_states, axis=1)
    new_cache_nat_kv = jnp.stack(nat_kvs, axis=1)
    new_cache_diff_kv = jnp.stack(diff_kvs, axis=1)

    y_sample = x_sample
    for layer in range(DEPTH):
        p = {name: arr[layer] for name, arr in stacked.items()}
        mod = (jax.nn.silu(c) @ p['w_mod'] + p['b_mod'])[:, None, :]
        ctx = {
            'gdn': state_gdn[:, layer],
            'nat_k': cache_nat_kv[:, layer, 0], 'nat_v': cache_nat_kv[:, layer, 1],
            'diff_k': cache_diff_kv[:, layer, 0], 'diff_v': cache_diff_kv[:, layer, 1],
        }
        y_sample, _ = trunk_layer(y_sample, mod, p, layer, ctx)

    return (y_prompt, y_sample, new_state_gdn, new_cache_nat_kv, new_cache_diff_kv)


_drawn_inputs = setup_inputs


def setup_inputs(seed=0):
    import zlib

    import numpy as np

    out = dict(_drawn_inputs(seed))
    spreads = {}
    factors = {'g_post': 3.452,
     'gdn_norm': 18.893,
     'nat_rpb': 23.515,
     'diff_lam': 3.589,
     'diff_norm': 22.966,
     'b_merge': 8.0,
     'cache_nat_kv': 4.546}
    for name, (base, spread) in spreads.items():
        noise = np.random.default_rng([zlib.crc32(name.encode()), seed]).standard_normal(out[name].shape)
        drawn = base * np.exp(spread * noise) if base else spread * noise
        out[name] = jnp.asarray(drawn.astype(out[name].dtype))
    for name, factor in factors.items():
        out[name] = (out[name] * factor).astype(out[name].dtype)
    return out
```

```python
import concourse.bass as bass
from concourse import mybir
from contextlib import ExitStack
import math
import numpy as np

DEPTH, D, NT, SAMPLE, PROMPT = 2, 1024, 640, 512, 128
TILES, KT, HEADS, W = 5, 8, 4, 128
GRID_W, WIN_R, WIN_C = 64, 8, 16
BANDS, HY_EMB, HY_FF = 16, 33, 64
EPS = 1e-6
LEVELS = 7
SP1 = NT + 1
CONV_TILE = [0, 128, 256, 384, 513]
BIAS_W = 14 * GRID_W
RING, SPLITS = 2, 2
MOD_BLOCKS, BRANCH_BLOCKS, OUT_BLOCKS = 24, 24, 8
SPLIT_BLOCKS = 4 * BRANCH_BLOCKS + OUT_BLOCKS
RAW_BLOCKS = MOD_BLOCKS + SPLIT_BLOCKS
NSMALL = 20
V_PRE, V_POST, V_BMOD, V_GDN, V_DIFF, V_HB1, V_HB2, V_LAM, V_DT, V_ALOG, V_BMERGE, NVEC = (
    0, 8, 16, 40, 41, 42, 43, 44, 45, 53, 61, 93)
MAGIC = 1.5 * 2.0 ** 23


def program(nc, I, O):
    f32, f32r, u8 = mybir.dt.float32, mybir.dt.float32r, mybir.dt.uint8
    ALU, ACT, AX = mybir.AluOpType, mybir.ActivationFunctionType, mybir.AxisListType
    ctx = ExitStack()
    with ctx:
        def sb(name, shape, dt=f32):
            return ctx.enter_context(nc.sbuf_tensor(name, [shape[0], int(np.prod(shape[1:]))], dt))

        def view(t, *dims, at=0):
            n = int(np.prod(dims))
            names = "abcd"[:len(dims)]
            return t[:, at:at + n].rearrange(
                "p (" + " ".join(names) + ") -> p " + " ".join(names),
                **{x: d for x, d in zip(names[:-1], dims[:-1])}) if len(dims) > 1 else t[:, at:at + n]

        h_hi, h_lo = (sb(n, [128, KT, NT], f32r) for n in ("h_hi", "h_lo"))
        h_hi_v, h_lo_v = view(h_hi, KT, NT), view(h_lo, KT, NT)
        raw_t = sb("raw", [128, RING, 12, 128])
        raw = view(raw_t, RING, 12, 128)
        w_hi_t, w_lo_t = (sb(n, [128, SPLITS, 12, 128], f32r) for n in ("w_hi", "w_lo"))
        w_hi, w_lo = view(w_hi_t, SPLITS, 12, 128), view(w_lo_t, SPLITS, 12, 128)
        y_hi_t, y_lo_t = (sb(n, [128, HEADS, NT], f32r) for n in ("y_hi", "y_lo"))
        y_hi, y_lo = view(y_hi_t, HEADS, NT), view(y_lo_t, HEADS, NT)
        merged_t = sb("merged", [128, KT, NT])
        merged = view(merged_t, KT, NT)
        tmp640 = sb("tmp640", [128, NT])
        ident, ones = sb("ident", [128, 128]), sb("ones", [128, 128])
        tri_t, strict_t = sb("tri", [128, 2, 128]), sb("strict", [128, 2, 128])
        tri, strict = view(tri_t, 2, 128), view(strict_t, 2, 128)
        level_t, level_now = sb("level", [128, LEVELS, 384], u8), sb("level_now", [128, 384], u8)
        level, level_v = view(level_t, LEVELS, 384), view(level_now, 3, 128)
        swap = sb("swap", [128, 128])
        dist = sb("dist", [128, TILES])
        neg_half = sb("neg_half", [128, 16])
        small_t = sb("small", [128, DEPTH * HEADS, NSMALL])
        small = view(small_t, DEPTH * HEADS, NSMALL)
        vecs_t = sb("vecs", [128, DEPTH, NVEC])
        vecs = view(vecs_t, DEPTH, NVEC)
        cond_raw, cond = sb("cond_raw", [128, KT * 2]), sb("cond", [128, KT * 2])
        mod_t = sb("mod", [128, 24, 2])
        mod = view(mod_t, 24, 2)
        g_scale_t = sb("g_scale", [128, KT, 2])
        g_scale = view(g_scale_t, KT, 2)
        lam_in = sb("lam_in", [128, 256])
        lam_s = sb("lam_s", [128, 8])
        ab_w = sb("ab_w", [128, KT, 16])
        ab_s = sb("ab_s", [128, 10, 40])
        hid_t = sb("hid", [65, NT])
        gate_sg_t = sb("gate_sg", [128, 2, NT])
        gate_sg = view(gate_sg_t, 2, NT)
        exp_alog = sb("exp_alog", [128, 8])
        gate_post_t = sb("gate_post", [128, 2, KT])
        gate_post = view(gate_post_t, 2, KT)
        stat = sb("stat", [128, 64])

        AREA = 16800
        area = sb("area", [128, AREA])

        class Area:
            def __init__(self, at=0):
                self.at = at

            def take(self, *dims):
                n = int(np.prod(dims))
                v = view(area, *dims, at=self.at)
                self.at += n
                assert self.at <= AREA, self.at
                return v

        psum_a = [ctx.enter_context(nc.psum_tensor(f"proj{i}", [128, 1024], f32)) for i in range(2)]
        M = ctx.enter_context(nc.psum_tensor("mix", [128, 2048], f32))

        passed = {n: ctx.enter_context(nc.semaphore(f"passed_{n}")) for n in ("SP", "Pool", "PE", "Activation", "DVE")}

        class Signal:
            all = []

            def __init__(self, name, per_layer, first=0, step=1):
                self.sem = ctx.enter_context(nc.semaphore(name))
                self.per, self.step = per_layer, step
                self.first = max(first, 1) if step == 1 else 0
                Signal.all.append(self)

            def at(self, layer, n):
                return layer * (self.per * self.step) + n * self.step + self.first

        def held(eng):
            eng.sem_inc(passed[eng.engine.name], 1)

        def per_unit(name, k=1, step=1, first=0):
            return Signal(name, HEADS * k, step=step, first=first)

        raw_in = [Signal(f"raw_in{s}", RAW_BLOCKS // RING, step=16) for s in range(RING)]
        hi_ready = Signal("weight_hi_ready", SPLIT_BLOCKS, first=RING)
        lo_ready = Signal("weight_lo_ready", SPLIT_BLOCKS, first=RING)
        block_done = Signal("block_done", SPLIT_BLOCKS, first=SPLITS)
        proj_taken = Signal("proj_taken", SPLIT_BLOCKS, first=2)
        mod_mm = Signal("mod_mm", MOD_BLOCKS, first=RING)
        raw_zero = Signal("raw_zero", 0)
        pad_zero = Signal("pad_zero", 1)
        level_cast = Signal("level_cast", 0)
        x_ss, y_ss = Signal("x_ss", 1), Signal("y_ss", 1)
        rope_in = [Signal(f"rope_in{i}", 1, step=16) for i in range(2)]
        consts_in = Signal("consts_in", 0, step=16)
        layer_in2 = [Signal(f"layer_in{i}", 1, step=16) for i in range(6)]
        cond_ready = Signal("cond_ready", 0)
        mod_ready = Signal("mod_ready", 1)
        x_in = Signal("x_in", 1, step=16)
        x_sq = Signal("x_sq", 1)
        x_rn = Signal("x_rn", 1)
        x_n = Signal("x_n", 1)
        xt_mm = Signal("xt_mm", KT)
        ht_raw = Signal("ht_raw", KT)
        h_ready = Signal("h_ready", KT)
        ab_mm = Signal("ab_mm", 1)
        ab_l = Signal("ab_l", 1)
        ab_v = Signal("ab_v", 3)
        gc_mm = Signal("gc_mm", 1)
        gc_e = Signal("gc_e", 1)
        ab_done = Signal("ab_done", 1)
        lam_v = Signal("lam_v", 2)
        lam_e = Signal("lam_e", 1)
        hid_mm = Signal("hid_mm", 2)
        hid_arg = Signal("hid_arg", 2)
        hid_sin = Signal("hid_sin", 2)
        dec_ready_l = Signal("decay_abs_ready", 1)
        A_conv, A_qkv = per_unit("A_conv", 3), per_unit("A_qkv")
        A_tr, A_tm, A_ss, A_rn = per_unit("A_tr"), per_unit("A_tm"), per_unit("A_ss", 2), per_unit("A_rn", 2)
        A_g1, A_rel, A_dec, A_kqn = per_unit("A_g1"), per_unit("A_rel", 2), per_unit("A_dec", 2), per_unit("A_kqn")
        A_kqt_mm, A_kqt, A_gram = per_unit("A_kqt_mm"), per_unit("A_kqt"), per_unit("A_gram")
        A_x0, A_lat = per_unit("A_x0"), per_unit("A_lat")
        A_q, A_qn, A_d = per_unit("A_q", 3 * LEVELS), per_unit("A_qn", 3 * LEVELS), per_unit("A_d", 3 * LEVELS)
        A_x = per_unit("A_x", 3 * LEVELS, first=3)
        A_wt_mm, A_wt, A_s_in = per_unit("A_wt_mm"), per_unit("A_wt"), per_unit("A_s_in", step=16)
        A_va, A_vn, A_sb, A_su = per_unit("A_va", 5), per_unit("A_vn", 5), per_unit("A_sb", 5), per_unit("A_su", 5)
        A_s_out, A_stored = per_unit("A_s_out", step=16), per_unit("A_stored")
        A_o, A_ot, A_y = per_unit("A_o"), per_unit("A_ot"), per_unit("A_y")
        B_const = [Signal(f"B_const{i}", 1, step=16) for i in range(4)]
        B_conv = per_unit("B_conv", 3)
        B_win, B_filt_mm, B_filt = per_unit("B_win"), per_unit("B_filt_mm"), per_unit("B_filt")
        B_h_mm, B_h = per_unit("B_h_mm"), per_unit("B_h")
        B_tr, B_vt, B_u, B_y0, B_inv = (per_unit(n, 2) for n in ("B_tr", "B_vt", "B_u", "B_yf", "B_inv"))
        B_z1, B_y = per_unit("B_z1"), per_unit("B_y")
        def attention(n, dma, once, each):
            return {**{k: per_unit(f"{n}_{k}", step=16) for k in dma}, **{k: per_unit(f"{n}_{k}") for k in once},
                    **{k: per_unit(f"{n}_{k}", 5) for k in each}}

        C = attention("C", ("in0", "in1", "in2", "kv0", "kv1"), ("tr", "vt", "pv", "y", "stored"),
                      ("s", "mx", "p", "pn", "pt_mm", "pt"))
        Dd = attention("D", ("in0", "in1", "kv0", "kv1"), ("tr", "vt", "rope", "ss", "rn", "on", "ot", "y", "stored"),
                       ("s", "mx", "p", "pn", "pt_mm", "pt", "pv", "o"))
        br_mm, merged_step = Signal("branch_mm", 32), Signal("merged_step", 32, first=2)
        m_split = Signal("merged_split", 1)
        yt_mm, ytm = Signal("y_t", OUT_BLOCKS), Signal("y_tm", OUT_BLOCKS)
        gate_diag, gate_mm, gate_bc = Signal("gate_diag", 1), Signal("gate_mm", 1), Signal("gate_bc", 1)
        y_sq, y_rn, x_new = Signal("y_sq", 1), Signal("y_rn", 1), Signal("x_new", 1)
        x_back = Signal("x_back", 1, step=16)
        x_reload = Signal("x_reload", 1, step=16)
        x_out = Signal("x_out", 0, step=16)

        pre = Area()
        x_tm = pre.take(TILES, D)
        x_n_v = pre.take(TILES, D)
        feat = pre.take(NT)[0:HY_EMB]
        hy_w12 = pre.take(2 * HY_FF)[0:HY_FF]
        hid_tmp = pre.take(2, NT)[0:HY_FF]
        end = Area(TILES * D)
        y_tm = end.take(TILES, D)
        gate_b = end.take(2, D)
        y_cm = end.take(2, NT)
        diag = end.take(16, 128)
        a = Area()
        pad = a.take(643)
        A_c = a.take(3, SP1)
        A_L0 = a.at
        A_zb = a.take(NT)
        A_tmv = a.take(3, TILES, 128)
        kqn = a.take(TILES, 2, 128)
        kqT = a.take(TILES, 2, 128)
        g1 = a.take(2, TILES, 128)
        dec = a.take(2, TILES, 128)
        decT = a.take(2, TILES, 128)
        X = a.take(2, TILES, 128)
        XT = a.take(2, TILES, 128)
        Qn = a.take(2, TILES, 128)
        vn = a.take(2, 128)
        S = a.take(2, 128)
        S_out = a.take(2, 128)
        Rv = g1
        Rk = view(area, 2, TILES, 128, at=643)
        o_tm = view(area, TILES, 128, at=643 + 2 * NT)
        kd = view(area, 2, TILES, 128, at=A_L0 + NT)
        sq_a = view(area, 2 * NT, at=A_L0 + NT + 3 * NT + 4 * NT + 6 * NT)
        b_ = Area(643)
        F_s, F_p = b_.take(4, 6, 128), b_.take(2, 128)
        Fi_s, Fi_p = b_.take(6, 512), b_.take(2, 128)
        B_c = b_.take(3, SP1)
        B_gb = b_.take(SP1)
        Hf = b_.take(8, 2, 128)
        w3, dec_abs = b_.take(HEADS, 256), b_.take(HEADS, 256)
        B_over = b_.at
        filt, win = b_.take(TILES, 256), b_.take(TILES, 256)
        bo = Area(B_over)
        vt_b, Yf, z1 = bo.take(TILES, 128), bo.take(8, 128), bo.take(NT)
        t1, t2 = view(tmp640, 4, 128), view(gate_sg_t, 4, 128)
        c_ = Area()
        qT, kT, vT, gT = c_.take(NT), c_.take(NT), c_.take(NT), c_.take(NT)
        v_t = c_.take(TILES, 128)
        k_p = c_.take(128)
        ctx_k, ctx_v = c_.take(128), c_.take(128)
        bias = c_.take(BIAS_W)
        s_buf = c_.take(2, NT)
        PT = c_.take(TILES, 512)
        PTp = c_.take(128)
        d_o = c_.take(TILES, 128)
        d_sq = c_.take(NT)
        cosT, sinT = c_.take(512), c_.take(512)
        rope_tmp = c_.take(512)

        def raw_uses(n, static):
            if isinstance(n, int):
                return (MOD_BLOCKS + n) // RING + 1
            return n // RING + (MOD_BLOCKS // RING + 1)

        def base(b):
            return b * BRANCH_BLOCKS

        N_CONST = 10 * 16
        started = ctx.enter_context(nc.semaphore("started"))

        def start(eng):
            eng.wait_ge(started, 1)

        block = ctx.enter_context(nc.Block())

        @block.sync
        def _(sp):
            for s in Signal.all:
                if s.per and s.first:
                    sp.sem_inc(s.sem, s.first)
            sp.drain().then_inc(started, 1)
            start(sp)
            sp.wait_ge(raw_zero.sem, 1)
            with sp.Fori(0, DEPTH) as layer:
                def load(slot, nth, src, n):
                    sp.dma_start(raw[:, slot, 0:n, :], src).then_inc(raw_in[slot].sem, raw_in[slot].step)

                sp.wait_ge(hi_ready.sem, hi_ready.at(layer, 0))
                held(sp)
                sp.wait_ge(lo_ready.sem, lo_ready.at(layer, 0))
                held(sp)
                with sp.Fori(0, MOD_BLOCKS // RING) as i:
                    for s in range(RING):
                        sp.wait_ge(mod_mm.sem, mod_mm.at(layer, i * RING + (s - 1)))
                        held(sp)
                        load(s, MOD_BLOCKS // RING, I["w_mod"][layer, i * RING + s, :, :].rearrange("p (k c) -> p k c", k=8), 8)
                sp.wait_ge(mod_mm.sem, mod_mm.at(layer, MOD_BLOCKS))
                held(sp)
                for b in range(4):
                    with sp.Fori(0, HEADS) as h:
                        for s in range(4):
                            n = h * 4 + (base(b) + s)
                            sp.wait_ge(hi_ready.sem, hi_ready.at(layer, n - RING + 1))
                            held(sp)
                            sp.wait_ge(lo_ready.sem, lo_ready.at(layer, n - RING + 1))
                            held(sp)
                            load(s % RING, HEADS, I["w_in"][layer, b, h * 4 + s, :, :].rearrange("p (k c) -> p k c", k=8), 8)
                    with sp.Fori(0, 2) as i:
                        for s in range(4):
                            n = i * 4 + (base(b) + 16 + s)
                            sp.wait_ge(hi_ready.sem, hi_ready.at(layer, n - RING + 1))
                            held(sp)
                            sp.wait_ge(lo_ready.sem, lo_ready.at(layer, n - RING + 1))
                            held(sp)
                            load(s % RING, 2, I["w_mb"][layer, b, i * 4 + s, :, :].rearrange("p (k c) -> p k c", k=12), 12)
                with sp.Fori(0, OUT_BLOCKS // RING) as i:
                    for s in range(RING):
                        n = i * RING + (base(4) + s)
                        sp.wait_ge(hi_ready.sem, hi_ready.at(layer, n - RING + 1))
                        held(sp)
                        sp.wait_ge(lo_ready.sem, lo_ready.at(layer, n - RING + 1))
                        held(sp)
                        load(s, OUT_BLOCKS // RING, I["w_out"][layer, i * RING + s, :, :].rearrange("p (k c) -> p k c", k=8), 8)

        @block.gpsimd
        def _(pool):
            P = nc.gpsimd
            start(pool)
            for dst, src in ((ident, I["ident"]), (ones, I["ones"]), (tri_t, I["tri"]), (strict_t, I["strict"]),
                             (area, I["level"]), (swap, I["swap"]), (dist, I["dist"]), (small_t, I["small"]),
                             (vecs_t, I["vecs"]), (cond_raw, I["cond"])):
                pool.dma_start(dst[:, :] if dst is not area else dst[:, 0:LEVELS * 384], src).then_inc(consts_in.sem, 16)
            P.memset(neg_half[:, :], -0.5)
            P.memset(raw_t[:, :], 0.0).then_inc(raw_zero.sem, raw_zero.step)
            pool.dma_start(O["x"][0:SAMPLE, :], I["x_sample"]).then_inc(x_out.sem, 16)
            pool.dma_start(O["x"][SAMPLE:NT, :], I["x_prompt"]).then_inc(x_out.sem, 16)
            pool.wait_ge(x_out.sem, 32)
            pool.wait_ge(consts_in.sem, N_CONST)
            pool.wait_ge(level_cast.sem, 1)

            def power(layer, start_sig, n_wait, done_sig, cols, times):
                pool.wait_ge(start_sig.sem, start_sig.at(layer, n_wait))
                held(pool)
                P.tensor_tensor(stat[:, 0:cols], stat[:, 0:cols], neg_half[:, 0:cols], ALU.pow).then_inc(done_sig.sem, done_sig.step)

            with pool.Fori(0, DEPTH) as layer:
                if True:
                    pool.dma_start(x_tm, O["x"].rearrange("(t p) d -> p t d", p=128)).then_inc(x_in.sem, x_in.step)
                    pool.dma_start(lam_in[:, :], I["lam"][layer, :, :].to_broadcast([128, 256])).then_inc(layer_in2[0].sem, layer_in2[0].step)
                    pool.dma_start(ab_w[:, :], I["ab_w"][layer, :, :]).then_inc(layer_in2[1].sem, layer_in2[1].step)
                    pool.dma_start(hy_w12[0:HY_FF, :], I["w12"][layer, :, :]).then_inc(layer_in2[2].sem, layer_in2[2].step)
                    pool.dma_start(feat[:, :], I["feat"]).then_inc(layer_in2[3].sem, layer_in2[3].step)
                power(layer, x_sq, 1, x_rn, 5, 1)
                pool.wait_ge(ab_done.sem, ab_done.at(layer, 1))
                held(pool)
                pool.wait_ge(h_ready.sem, h_ready.at(layer, KT))
                held(pool)
                pool.wait_ge(hid_sin.sem, hid_sin.at(layer, 2))
                held(pool)
                P.memset(pad, 0.0).then_inc(pad_zero.sem, pad_zero.step)
                with pool.Fori(0, HEADS) as h:
                    it = layer * HEADS + h
                    if True:
                        pool.wait_ge(A_su.sem, A_su.at(layer, h * 5))
                        held(pool)
                        pool.dma_start(S, I["state"][layer, h, :, :].rearrange("p (a b) -> p a b", a=2)).then_inc(A_s_in.sem, A_s_in.step)
                    power(layer, A_ss, h * 2 + 1, A_rn, 10, HEADS)
                    pool.wait_ge(A_tm.sem, A_tm.at(layer, h + 1))
                    held(pool)
                    for dst in (X, XT):
                        for d in range(2):
                            last = P.tensor_copy(dst[:, d, :, :], ident[:, :].unsqueeze(1).to_broadcast([128, TILES, 128]))
                    last.then_inc(A_x0.sem, A_x0.step)
                    pool.wait_ge(A_su.sem, A_su.at(layer, h * 5 + 5))
                    held(pool)
                    pool.dma_start(O["state"][layer, h, :, :], S_out.rearrange("p a b -> p (a b)")).then_inc(A_s_out.sem, A_s_out.step)
                    power(layer, A_ss, h * 2 + 2, A_rn, 5, HEADS)
                    pool.wait_ge(A_s_out.sem, A_s_out.at(layer, h + 1))
                    held(pool)
                    P.drain().then_inc(A_stored.sem, A_stored.step)
                pool.wait_ge(A_y.sem, A_y.at(layer, HEADS))
                held(pool)
                for i, (dst, src) in enumerate(((F_s, "F_s"), (F_p, "F_p"), (Fi_s, "Fi_s"), (Fi_p, "Fi_p"))):
                    pool.dma_start(dst, I[src].rearrange("p (a b) -> p a b", b=dst.shape[-1]) if len(dst.shape) == 3
                                                 else I[src].rearrange("p (a b c) -> p a b c", b=6, c=128)).then_inc(B_const[i].sem, B_const[i].step)
                pool.dma_start(w3[0:65], I["w3"][layer, :, :].rearrange("p (a b) -> p a b", a=4)).then_inc(layer_in2[4].sem, layer_in2[4].step)
                pool.dma_start(dec_abs, I["decay"][layer, :, :].rearrange("o (a b) -> o a b", a=4).to_broadcast([128, 4, 256])).then_inc(layer_in2[5].sem, layer_in2[5].step)
                pool.wait_ge(B_y.sem, B_y.at(layer, HEADS))
                held(pool)
                with pool.Fori(0, HEADS) as h:
                    pool.wait_ge(C["y"].sem, C["y"].at(layer, h))
                    held(pool)
                    pool.dma_start(ctx_k, I["nat_kT"][layer, h, :, :]).then_inc(C["in0"].sem, C["in0"].step)
                    pool.dma_start(ctx_v, I["nat_v"][layer, h, :, :]).then_inc(C["in1"].sem, C["in1"].step)
                    pool.dma_start(bias, I["bias"][layer, h, :, :]).then_inc(C["in2"].sem, C["in2"].step)
                    pool.wait_ge(C["vt"].sem, C["vt"].at(layer, h + 1))
                    held(pool)
                    pool.dma_start(O["nat"][layer, 0, h, :, :], k_p).then_inc(C["kv0"].sem, C["kv0"].step)
                    pool.dma_start(O["nat"][layer, 1, h, :, :], v_t[:, 4, :]).then_inc(C["kv1"].sem, C["kv1"].step)
                    pool.wait_ge(C["kv0"].sem, C["kv0"].at(layer, h + 1))
                    held(pool)
                    pool.wait_ge(C["kv1"].sem, C["kv1"].at(layer, h + 1))
                    held(pool)
                    P.drain().then_inc(C["stored"].sem, C["stored"].step)
                pool.wait_ge(C["y"].sem, C["y"].at(layer, HEADS))
                held(pool)
                pool.dma_start(cosT, I["cos"]).then_inc(rope_in[0].sem, rope_in[0].step)
                pool.dma_start(sinT, I["sin"]).then_inc(rope_in[1].sem, rope_in[1].step)
                with pool.Fori(0, HEADS) as h:
                    pool.wait_ge(Dd["y"].sem, Dd["y"].at(layer, h))
                    held(pool)
                    pool.dma_start(ctx_k, I["diff_kT"][layer, h, :, :]).then_inc(Dd["in0"].sem, Dd["in0"].step)
                    pool.dma_start(ctx_v, I["diff_v"][layer, h, :, :]).then_inc(Dd["in1"].sem, Dd["in1"].step)
                    pool.wait_ge(Dd["vt"].sem, Dd["vt"].at(layer, h + 1))
                    held(pool)
                    pool.dma_start(O["diff"][layer, 0, h, :, :], k_p).then_inc(Dd["kv0"].sem, Dd["kv0"].step)
                    pool.dma_start(O["diff"][layer, 1, h, :, :], v_t[:, 4, :]).then_inc(Dd["kv1"].sem, Dd["kv1"].step)
                    pool.wait_ge(Dd["kv0"].sem, Dd["kv0"].at(layer, h + 1))
                    held(pool)
                    pool.wait_ge(Dd["kv1"].sem, Dd["kv1"].at(layer, h + 1))
                    held(pool)
                    P.drain().then_inc(Dd["stored"].sem, Dd["stored"].step)
                    power(layer, Dd["ss"], h + 1, Dd["rn"], 5, HEADS)
                pool.wait_ge(Dd["y"].sem, Dd["y"].at(layer, HEADS))
                held(pool)
                pool.dma_start(x_tm, O["x"].rearrange("(t p) d -> p t d", p=128)).then_inc(x_reload.sem, x_reload.step)
                power(layer, y_sq, 1, y_rn, 5, 1)
                pool.wait_ge(x_new.sem, x_new.at(layer, 1))
                held(pool)
                pool.dma_start(O["x"].rearrange("(t p) d -> p t d", p=128), x_tm).then_inc(x_back.sem, x_back.step)
                pool.wait_ge(x_back.sem, x_back.at(layer, 1))
                held(pool)

        @block.tensor
        def _(pe):
            T = nc.tensor
            start(pe)
            pe.wait_ge(consts_in.sem, N_CONST)

            def mm(out, l, r, start=True, stop=True):
                return T.matmul(out, l, r, start=start, stop=stop)

            def tr(out, src):
                return T.transpose(out, src, ident[:, :])

            def product(layer, n, static, act_hi, act_lo, kts, w0, out, times):
                s = static % SPLITS
                pairs = ((w_hi, act_hi), (w_hi, act_lo), (w_lo, act_hi))
                for k in range(kts):
                    for j, (w, t) in enumerate(pairs):
                        a, z = (k == 0 and j == 0), (k == kts - 1 and j == 2)
                        mm(out[:, 0:SAMPLE], w[:, s, w0 + k, :], t[:, k, 0:SAMPLE], a, z)
                        last = mm(out[:, SAMPLE:NT], w[:, s, w0 + k, :], t[:, k, SAMPLE:NT], a, z)
                return last

            def project(layer, n, static, times):
                pe.wait_ge(hi_ready.sem, hi_ready.at(layer, n + 1))
                pe.wait_ge(lo_ready.sem, lo_ready.at(layer, n + 1))
                pe.wait_ge(proj_taken.sem, proj_taken.at(layer, n - 1))
                product(layer, n, static, h_hi_v, h_lo_v, KT, 0, psum_a[static % 2], times).then_inc(block_done.sem, block_done.step)

            with pe.Fori(0, DEPTH) as layer:
                if True:
                    pe.wait_ge(cond_ready.sem, 1)
                    pe.wait_ge(gate_bc.sem, gate_bc.at(layer, 0))
                    held(pe)
                    with pe.Fori(0, MOD_BLOCKS // RING) as i:
                        for s in range(RING):
                            pe.wait_ge(raw_in[s].sem, raw_in[s].at(layer, i + 1))
                            for k in range(KT):
                                last = mm(M[:, bass.ds((i * RING + s) * 2, 2)], raw[:, s, k, :], cond[:, 2 * k:2 * k + 2],
                                          k == 0, k == KT - 1)
                            last.then_inc(mod_mm.sem, mod_mm.step)
                for i in (2, 3):
                    pe.wait_ge(layer_in2[i].sem, layer_in2[i].at(layer, 1))
                pe.wait_ge(mod_ready.sem, mod_ready.at(layer, 1))
                for j in range(2):
                    src = feat[0:HY_EMB, :] if j == 0 else hid_tmp[0:HY_FF, 0, :]
                    w = hy_w12[0:HY_EMB, 0:HY_FF] if j == 0 else hy_w12[0:HY_FF, HY_FF:2 * HY_FF]
                    if j:
                        pe.wait_ge(hid_sin.sem, hid_sin.at(layer, 1))
                    held(pe)
                    mm(M[0:HY_FF, 0:SAMPLE], w, src[:, 0:SAMPLE])
                    mm(M[0:HY_FF, SAMPLE:NT], w, src[:, SAMPLE:NT]).then_inc(hid_mm.sem, hid_mm.step)
                pe.wait_ge(x_n.sem, x_n.at(layer, 1))
                pe.wait_ge(hid_arg.sem, hid_arg.at(layer, 2))
                for k in range(KT):
                    at = 1024 * (k % 2)
                    if k >= 2:
                        pe.wait_ge(ht_raw.sem, ht_raw.at(layer, k - 1))
                    for t in range(TILES):
                        last = tr(M[:, at + 128 * t:at + 128 * (t + 1)], x_n_v[:, t, 128 * k:128 * (k + 1)])
                    last.then_inc(xt_mm.sem, xt_mm.step)
                pe.wait_ge(h_ready.sem, h_ready.at(layer, KT))
                pe.wait_ge(layer_in2[1].sem, layer_in2[1].at(layer, 1))
                for t in range(TILES):
                    for k in range(KT):
                        for j, x in enumerate((h_hi_v, h_lo_v)):
                            last = mm(M[:, 16 * t:16 * t + 16], x[:, k, 128 * t:128 * t + 128].bitcast(f32),
                                      ab_w[:, 16 * k:16 * k + 16], k == 0 and j == 0, k == KT - 1 and j == 1)
                last.then_inc(ab_mm.sem, ab_mm.step)
                pe.wait_ge(ab_v.sem, ab_v.at(layer, 2))
                g = ab_s[:, 0:40]
                for d in range(2):
                    mm(M[:, 512 + 20 * d:512 + 20 * d + 20], tri[:, d, :], ab_s[:, 20 * d:20 * d + 20])
                mm(M[:, 576:616], ones[:, :], g).then_inc(gc_mm.sem, gc_mm.step)

                pe.wait_ge(ab_done.sem, ab_done.at(layer, 1))
                held(pe)
                with pe.Fori(0, HEADS) as h:
                    for j in range(4):
                        project(layer, h * 4 + (base(0) + j), j, HEADS)
                    pe.wait_ge(A_y.sem, A_y.at(layer, h))
                    pe.wait_ge(A_qkv.sem, A_qkv.at(layer, h + 1))
                    for w in range(3):
                        for t in range(TILES):
                            col = 512 * w + 128 * t if t < 4 else 1536 + 128 * w
                            last = tr(M[:, col:col + 128], A_c[:, w, CONV_TILE[t]:CONV_TILE[t] + 128])
                    last.then_inc(A_tr.sem, A_tr.step)
                    pe.wait_ge(A_tm.sem, A_tm.at(layer, h + 1))
                    pe.wait_ge(A_g1.sem, A_g1.at(layer, h + 1))
                    for d in range(2):
                        if d:
                            pe.wait_ge(A_dec.sem, A_dec.at(layer, h * 2 + 1))
                        mm(M[:, 0:512], tri[:, d, :], g1[:, d, 0:4, :])
                        mm(M[:, 512:640], tri[:, d, :], g1[:, d, 4, :])
                        for t in range(TILES):
                            last = mm(M[:, 1024 + 128 * t:1152 + 128 * t], g1[:, d, t, :], tri[:, d, :])
                        last.then_inc(A_rel.sem, A_rel.step)
                    pe.wait_ge(A_kqn.sem, A_kqn.at(layer, h + 1))
                    pe.wait_ge(A_dec.sem, A_dec.at(layer, h * 2 + 2))
                    for t in range(TILES):
                        for j in range(2):
                            last = tr(M[:, 256 * t + 128 * j:256 * t + 128 * j + 128], kqn[:, t, j, :])
                    last.then_inc(A_kqt_mm.sem, A_kqt_mm.step)
                    pe.wait_ge(A_kqt.sem, A_kqt.at(layer, h + 1))
                    for t in range(TILES):
                        last = mm(M[:, 256 * t:256 * t + 256], kqT[:, t, 0, :], kqT[:, t, :, :])
                    last.then_inc(A_gram.sem, A_gram.step)
                    pe.wait_ge(A_x0.sem, A_x0.at(layer, h + 1))
                    pe.wait_ge(A_lat.sem, A_lat.at(layer, h + 1))
                    held(pe)
                    groups = ([(0, t) for t in range(4)], [(1, t) for t in range(4)], [(0, 4), (1, 4)])
                    with pe.Fori(0, LEVELS) as lv:
                        e = h * (3 * LEVELS) + lv * 3
                        for gi, grp in enumerate(groups):
                            pe.wait_ge(A_x.sem, A_x.at(layer, e + (gi + 1 - 3)))
                            for j, (d, t) in enumerate(grp):
                                last = mm(M[:, 512 * gi + 128 * j:512 * gi + 128 * j + 128], dec[:, d, t, :], XT[:, d, t, :])
                            last.then_inc(A_q.sem, A_q.step)
                        for gi, grp in enumerate(groups):
                            pe.wait_ge(A_qn.sem, A_qn.at(layer, e + (1, 3, 3)[gi]))
                            if gi == 2:
                                pe.wait_ge(A_x.sem, A_x.at(layer, e + 1))
                            a0, b0 = ((1536, 0), (512, 1024), (1536, 1792))[gi]
                            for j, (d, t) in enumerate(grp):
                                mm(M[:, a0 + 128 * j:a0 + 128 * j + 128], Qn[:, d, t, :], X[:, d, t, :])
                            for j, (d, t) in enumerate(grp):
                                last = mm(M[:, b0 + 128 * j:b0 + 128 * j + 128], X[:, d, t, :], Qn[:, d, t, :])
                            last.then_inc(A_d.sem, A_d.step)
                    pe.wait_ge(A_x.sem, A_x.at(layer, h * (3 * LEVELS) + 3 * LEVELS))
                    for d in range(2):
                        for t in range(4):
                            last = mm(M[:, 512 * d + 128 * t:512 * d + 128 * t + 128], Rk[:, d, t, :], XT[:, d, t, :])
                    last.then_inc(A_wt_mm.sem, A_wt_mm.step)
                    pe.wait_ge(A_s_in.sem, A_s_in.at(layer, h + 1))
                    pe.wait_ge(A_wt.sem, A_wt.at(layer, h + 1))
                    for n in range(5):
                        ts = (n, 3 - n) if n < 4 else (4, 4)
                        if n:
                            pe.wait_ge(A_su.sem, A_su.at(layer, h * 5 + n))
                        for d, t in enumerate(ts):
                            o = M[:, 1024 + 128 * d:1152 + 128 * d]
                            last = mm(o, XT[:, d, t, :], Rv[:, d, t, :], True, n == 4)
                            if n < 4:
                                mm(o, Qn[:, d, t, :], S[:, d, :], False, True)
                        if n < 4:
                            for d, t in enumerate(ts):
                                last = mm(M[:, 1280 + 128 * d:1408 + 128 * d], kqT[:, t, 1, :], S[:, d, :])
                        last.then_inc(A_va.sem, A_va.step)
                        pe.wait_ge(A_vn.sem, A_vn.at(layer, h * 5 + (n + 1)))
                        for d, t in enumerate(ts):
                            mm(M[:, 1536 + 128 * d:1664 + 128 * d], decT[:, d, t, :], vn[:, d, :])
                        for d, t in enumerate(ts):
                            last = mm(M[:, 1792 + 128 * d:1920 + 128 * d], kd[:, d, t, :], vn[:, d, :])
                        last.then_inc(A_sb.sem, A_sb.step)
                    pe.wait_ge(A_o.sem, A_o.at(layer, h + 1))
                    for t in range(TILES):
                        last = tr(M[:, 128 * t:128 * t + 128], o_tm[:, t, :])
                    last.then_inc(A_ot.sem, A_ot.step)

                def merge(b, y_sig):
                    pe.wait_ge(y_sig.sem, y_sig.at(layer, HEADS))
                    held(pe)
                    with pe.Fori(0, 2) as i:
                        for s in range(4):
                            n = i * 4 + (base(b) + 16 + s)
                            step = i * 4 + (8 * b + s)
                            pe.wait_ge(hi_ready.sem, hi_ready.at(layer, n + 1))
                            pe.wait_ge(lo_ready.sem, lo_ready.at(layer, n + 1))
                            pe.wait_ge(merged_step.sem, merged_step.at(layer, step - 1))
                            product(layer, n, s, y_hi, y_lo, HEADS, 8, M[:, 1024 * (s % 2):1024 * (s % 2) + NT], 2).then_inc(br_mm.sem, br_mm.step)
                            project(layer, n, s, 2)

                merge(0, A_y)

                def dft(src_s, src_p, out_w, at):
                    for f in range(6):
                        o = at + (f + f // 3) * out_w
                        for t in range(4):
                            mm(M[:, o:o + out_w], F_s[:, t, f, :], src_s(t), t == 0, t == 3)
                    for j in range(2):
                        o = at + (3 + 4 * j) * out_w
                        last = mm(M[:, o:o + out_w], F_p[:, j, :], src_p)
                    return last

                for i in range(4):
                    pe.wait_ge(B_const[i].sem, B_const[i].at(layer, 1))
                pe.wait_ge(layer_in2[4].sem, layer_in2[4].at(layer, 1))
                held(pe)
                with pe.Fori(0, HEADS) as h:
                    for j in range(4):
                        project(layer, h * 4 + (base(1) + j), j, HEADS)
                    pe.wait_ge(B_y.sem, B_y.at(layer, h))
                    pe.wait_ge(merged_step.sem, merged_step.at(layer, 8))
                    for t in range(TILES):
                        last = mm(M[:, 256 * t:256 * t + 256], hid_t[:, 128 * t:128 * t + 128], w3[0:65, h, :])
                    last.then_inc(B_filt_mm.sem, B_filt_mm.step)
                    pe.wait_ge(B_filt.sem, B_filt.at(layer, h + 1))
                    dft(lambda t: filt[:, t, :], filt[:, 4, :], 256, 0).then_inc(B_h_mm.sem, B_h_mm.step)
                    pe.wait_ge(B_h.sem, B_h.at(layer, h + 1))
                    for r in range(2):
                        if r == 0:
                            pe.wait_ge(B_conv.sem, B_conv.at(layer, h * 3 + 1))
                            src = [B_c[:, 0, x:x + 128] for x in CONV_TILE]
                        else:
                            pe.wait_ge(B_z1.sem, B_z1.at(layer, h + 1))
                            src = [z1[:, 128 * t:128 * t + 128] for t in range(TILES)]
                        for t in range(TILES):
                            last = tr(M[:, 1024 + 128 * t:1152 + 128 * t], src[t])
                        last.then_inc(B_tr.sem, B_tr.step)
                        pe.wait_ge(B_vt.sem, B_vt.at(layer, h * 2 + (r + 1)))
                        dft(lambda t: vt_b[:, t, :], vt_b[:, 4, :], 128, 1024).then_inc(B_u.sem, B_u.step)
                        pe.wait_ge(B_y0.sem, B_y0.at(layer, h * 2 + (r + 1)))
                        for f in range(6):
                            mm(M[:, 0:512], Yf[:, f + f // 3, :], Fi_s[:, f, :], f == 0, f == 5)
                        for j in range(2):
                            last = mm(M[:, 512:640], Yf[:, 3 + 4 * j, :], Fi_p[:, j, :], j == 0, j == 1)
                        last.then_inc(B_inv.sem, B_inv.step)
                merge(1, B_y)

                with pe.Fori(0, HEADS) as h:
                    for j in range(4):
                        project(layer, h * 4 + (base(2) + j), j, HEADS)
                    pe.wait_ge(C["y"].sem, C["y"].at(layer, h))
                    pe.wait_ge(merged_step.sem, merged_step.at(layer, 16))
                    pe.wait_ge(proj_taken.sem, proj_taken.at(layer, h * 4 + (base(2) + 4)))
                    for t in range(TILES):
                        tr(M[:, 1024 + 128 * t:1152 + 128 * t], vT[:, 128 * t:128 * t + 128])
                    tr(M[:, 1664:1792], kT[:, SAMPLE:NT]).then_inc(C["tr"].sem, C["tr"].step)
                    for i in range(3):
                        pe.wait_ge(C[f"in{i}"].sem, C[f"in{i}"].at(layer, h + 1))

                    def scores(m):
                        if m:
                            pe.wait_ge(C["mx"].sem, C["mx"].at(layer, h * 5 + m))
                        q = qT[:, 128 * m:128 * m + 128]
                        if m < 4:
                            mm(M[:, 0:512], q, kT[:, 0:SAMPLE])
                            mm(M[:, 512:640], q, ctx_k).then_inc(C["s"].sem, C["s"].step)
                        else:
                            mm(M[:, 512:640], q, kT[:, SAMPLE:NT]).then_inc(C["s"].sem, C["s"].step)

                    scores(0)
                    pe.wait_ge(C["vt"].sem, C["vt"].at(layer, h + 1))
                    for m in range(5):
                        if m < 4:
                            scores(m + 1)
                        pe.wait_ge(C["pn"].sem, C["pn"].at(layer, h * 5 + (m + 1)))
                        if m:
                            pe.wait_ge(C["pt"].sem, C["pt"].at(layer, h * 5 + m))
                        for t in range(0 if m < 4 else 4, TILES):
                            last = tr(M[:, 1024 + 128 * t:1152 + 128 * t], s_buf[:, m % 2, 128 * t:128 * t + 128])
                        last.then_inc(C["pt_mm"].sem, C["pt_mm"].step)
                    pe.wait_ge(C["pt"].sem, C["pt"].at(layer, h * 5 + 5))
                    pe.wait_ge(C["mx"].sem, C["mx"].at(layer, h * 5 + 5))
                    for t in range(TILES):
                        mm(M[:, 0:512], v_t[:, t, :] if t < 4 else ctx_v, PT[:, t, :], t == 0, t == 4)
                    mm(M[:, 512:640], v_t[:, 4, :], PTp).then_inc(C["pv"].sem, C["pv"].step)
                merge(2, C["y"])

                with pe.Fori(0, HEADS) as h:
                    for j in range(4):
                        project(layer, h * 4 + (base(3) + j), j, HEADS)
                    pe.wait_ge(Dd["y"].sem, Dd["y"].at(layer, h))
                    pe.wait_ge(merged_step.sem, merged_step.at(layer, 24))
                    pe.wait_ge(proj_taken.sem, proj_taken.at(layer, h * 4 + (base(3) + 4)))
                    mm(M[:, 0:512], swap[:, :], qT[:, 0:SAMPLE])
                    mm(M[:, 512:1024], swap[:, :], kT[:, 0:SAMPLE])
                    for t in range(TILES):
                        tr(M[:, 1024 + 128 * t:1152 + 128 * t], vT[:, 128 * t:128 * t + 128])
                    tr(M[:, 1664:1792], kT[:, SAMPLE:NT]).then_inc(Dd["tr"].sem, Dd["tr"].step)
                    for i in range(2):
                        pe.wait_ge(Dd[f"in{i}"].sem, Dd[f"in{i}"].at(layer, h + 1))
                    pe.wait_ge(Dd["rope"].sem, Dd["rope"].at(layer, h + 1))
                    pe.wait_ge(Dd["vt"].sem, Dd["vt"].at(layer, h + 1))
                    for m in range(5):
                        if m:
                            pe.wait_ge(Dd["o"].sem, Dd["o"].at(layer, h * 5 + m))
                        for i in range(2):
                            rows = slice(64 * i, 64 * i + 64)
                            q = qT[rows, 128 * m:128 * m + 128]
                            if m < 4:
                                mm(M[:, 1024 * i:1024 * i + 512], q, kT[rows, 0:SAMPLE])
                            last = mm(M[:, 1024 * i + 512:1024 * i + 640], q, ctx_k[rows, :] if m < 4 else kT[rows, SAMPLE:NT])
                        last.then_inc(Dd["s"].sem, Dd["s"].step)
                        pe.wait_ge(Dd["pn"].sem, Dd["pn"].at(layer, h * 5 + (m + 1)))
                        first = 0 if m < 4 else 4
                        for t in range(first, TILES):
                            last = tr(M[:, 128 * t:128 * t + 128], s_buf[:, 0, 128 * t:128 * t + 128])
                        last.then_inc(Dd["pt_mm"].sem, Dd["pt_mm"].step)
                        pe.wait_ge(Dd["pt"].sem, Dd["pt"].at(layer, h * 5 + (m + 1)))
                        for t in range(first, TILES):
                            v = ctx_v if (t == 4 and m < 4) else v_t[:, t, :]
                            last = mm(M[:, 1024:1152], PT[:, t, 0:128], v, t == first, t == 4)
                        last.then_inc(Dd["pv"].sem, Dd["pv"].step)
                    pe.wait_ge(Dd["on"].sem, Dd["on"].at(layer, h + 1))
                    for t in range(TILES):
                        last = tr(M[:, 128 * t:128 * t + 128], d_o[:, t, :])
                    last.then_inc(Dd["ot"].sem, Dd["ot"].step)
                merge(3, Dd["y"])

                def back(n):
                    pe.wait_ge(proj_taken.sem, proj_taken.at(layer, base(4) + n + 1))
                    if n >= 2:
                        pe.wait_ge(ytm.sem, ytm.at(layer, n - 1))
                    for t in range(TILES):
                        last = tr(M[:, 1024 * (n % 2) + 128 * t:1024 * (n % 2) + 128 * t + 128],
                                  y_cm[:, n % 2, 128 * t:128 * t + 128])
                    last.then_inc(yt_mm.sem, yt_mm.step)

                pe.wait_ge(m_split.sem, m_split.at(layer, 1))
                for n in range(OUT_BLOCKS):
                    project(layer, base(4) + n, n, 1)
                    if n:
                        back(n - 1)
                back(OUT_BLOCKS - 1)
                pe.wait_ge(ytm.sem, ytm.at(layer, OUT_BLOCKS))
                pe.wait_ge(gate_diag.sem, gate_diag.at(layer, 1))
                for n in range(4):
                    last = mm(M[:, 512 * n:512 * n + 512], ones[:, :], diag[:, 4 * n:4 * n + 4, :])
                last.then_inc(gate_mm.sem, gate_mm.step)

        @block.scalar
        def _(act):
            A = nc.scalar
            start(act)
            act.wait_ge(consts_in.sem, N_CONST)
            act.wait_ge(raw_zero.sem, 1)
            A.activation(cond[:, :], cond_raw[:, :], ACT.Silu).then_inc(cond_ready.sem, cond_ready.step)

            def copy(out, x, scale=1.0):
                return A.activation(out, x, ACT.Copy, scale=scale)

            def split_hi(layer, n, static, width, times):
                r, s = static % RING, static % SPLITS
                act.wait_ge(raw_in[r].sem, raw_in[r].at(layer, raw_uses(n, static)))
                act.wait_ge(block_done.sem, block_done.at(layer, n - SPLITS + 1))
                copy(w_hi[:, s, 0:width, :], raw[:, r, 0:width, :]).then_inc(hi_ready.sem, hi_ready.step)

            def taken(instruction, times):
                instruction.then_inc(proj_taken.sem, proj_taken.step)

            with act.Fori(0, DEPTH) as layer:
                act.wait_ge(x_in.sem, x_in.at(layer, 1))
                for t in range(TILES):
                    last = A.activation(x_n_v[:, t, :], x_tm[:, t, :], ACT.Square, accum_out=stat[:, t:t + 1])
                last.then_inc(x_ss.sem, x_ss.step)
                act.wait_ge(lam_v.sem, lam_v.at(layer, 1))
                A.activation(lam_s[:, 2:4], lam_s[:, 0:2], ACT.Exp).then_inc(lam_e.sem, lam_e.step)
                for j in range(2):
                    act.wait_ge(hid_arg.sem, hid_arg.at(layer, j + 1))
                    out = hid_tmp[0:HY_FF, 0, :] if j == 0 else hid_t[0:HY_FF, :]
                    A.activation(out, hid_tmp[0:HY_FF, 0, :], ACT.Sin).then_inc(hid_sin.sem, hid_sin.step)
                act.wait_ge(mod_ready.sem, mod_ready.at(layer, 1))
                for k in range(KT):
                    at = 1024 * (k % 2)
                    act.wait_ge(xt_mm.sem, xt_mm.at(layer, k + 1))
                    if k >= 2:
                        act.wait_ge(h_ready.sem, h_ready.at(layer, k - 1))
                    A.activation(gate_sg[:, k % 2, 0:SAMPLE], M[:, at:at + SAMPLE], ACT.Identity,
                                 scale=g_scale[:, k, 0:1], bias=mod[:, k, 0:1])
                    A.activation(gate_sg[:, k % 2, SAMPLE:NT], M[:, at + SAMPLE:at + NT], ACT.Identity,
                                           scale=g_scale[:, k, 1:2], bias=mod[:, k, 1:2]).then_inc(ht_raw.sem, ht_raw.step)
                ab = lambda i: ab_s[:, 40 * i:40 * i + 40]
                act.wait_ge(ab_v.sem, ab_v.at(layer, 1))
                A.activation(ab(9), ab(7), ACT.Exp, scale=-1.0)
                A.activation(exp_alog[:, :], vecs[:, layer, V_ALOG:V_ALOG + 8], ACT.Exp)
                A.activation(ab(8), ab(8), ACT.Exp, scale=-1.0)
                A.drain()
                A.activation(ab(8), ab(8), ACT.Ln, bias=1.0).then_inc(ab_l.sem, ab_l.step)
                act.wait_ge(ab_v.sem, ab_v.at(layer, 3))
                A.activation(ab(2), ab(8), ACT.Exp)
                A.activation(ab(3), ab(3), ACT.Exp)
                A.activation(ab(4), ab(7), ACT.Exp).then_inc(gc_e.sem, gc_e.step)
                split_hi(layer, 0, 0, 8, 1)

                act.wait_ge(pad_zero.sem, pad_zero.at(layer, 1))

                def to_pad(conv, h, j, p):
                    act.wait_ge(conv.sem, conv.at(layer, h * 3 + j))
                    copy(pad[:, 1:1 + SAMPLE], p[:, 0:SAMPLE])
                    taken(copy(pad[:, 2 + SAMPLE:2 + NT], p[:, SAMPLE:NT]), HEADS)

                def head_block(b, h, j):
                    n = h * 4 + (base(b) + j)
                    split_hi(layer, n + 1, j + 1, 8 if j < 3 else 12, HEADS)
                    act.wait_ge(block_done.sem, block_done.at(layer, n + 1))
                    return psum_a[j % 2]

                with act.Fori(0, HEADS) as h:
                    for j in range(4):
                        p = head_block(0, h, j)
                        if j < 3:
                            to_pad(A_conv, h, j, p)
                        else:
                            act.wait_ge(A_y.sem, A_y.at(layer, h))
                            taken(A.activation(A_zb, p[:, 0:NT], ACT.Silu), HEADS)
                    act.wait_ge(A_conv.sem, A_conv.at(layer, h * 3 + 3))
                    A.activation(A_c, A_c, ACT.Silu).then_inc(A_qkv.sem, A_qkv.step)
                    act.wait_ge(A_tr.sem, A_tr.at(layer, h + 1))
                    copy(A_tmv[:, :, 0:4, :], M[:, 0:1536].rearrange("p (w t c) -> p w t c", w=3, t=4))
                    copy(A_tmv[:, :, 4, :], M[:, 1536:1920].rearrange("p (w c) -> p w c", w=3)).then_inc(A_tm.sem, A_tm.step)
                    for d in range(2):
                        act.wait_ge(A_rel.sem, A_rel.at(layer, h * 2 + (d + 1)))
                        A.activation(dec[:, d, :, :], M[:, 0:NT].rearrange("p (t c) -> p t c", t=5), ACT.Exp)
                        A.activation(decT[:, d, :, :], M[:, 1024:1024 + NT].rearrange("p (t c) -> p t c", t=5), ACT.Exp).then_inc(A_dec.sem, A_dec.step)
                    act.wait_ge(A_kqt_mm.sem, A_kqt_mm.at(layer, h + 1))
                    copy(kqT, M[:, 0:1280].rearrange("p (t j c) -> p t j c", t=5, j=2)).then_inc(A_kqt.sem, A_kqt.step)
                    with act.Fori(0, LEVELS) as lv:
                        e = h * (3 * LEVELS) + lv * 3
                        outs = (Qn[:, 0, 0:4, :], Qn[:, 1, 0:4, :], Qn[:, :, 4, :])
                        for gi in range(3):
                            act.wait_ge(A_q.sem, A_q.at(layer, e + (gi + 1)))
                            src = M[:, 512 * gi:512 * gi + (512 if gi < 2 else 256)].rearrange("p (t c) -> p t c", c=128)
                            copy(outs[gi], src, -1.0).then_inc(A_qn.sem, A_qn.step)
                    act.wait_ge(A_wt_mm.sem, A_wt_mm.at(layer, h + 1))
                    copy(Qn[:, :, 0:4, :], M[:, 0:1024].rearrange("p (d t c) -> p d t c", d=2, t=4), -1.0).then_inc(A_wt.sem, A_wt.step)
                    for n in range(5):
                        act.wait_ge(A_va.sem, A_va.at(layer, h * 5 + (n + 1)))
                        copy(vn, M[:, 1024:1280].rearrange("p (d c) -> p d c", d=2)).then_inc(A_vn.sem, A_vn.step)

                def merge(b):
                    with act.Fori(0, 2) as i:
                        for s in range(4):
                            n = i * 4 + (base(b) + 16 + s)
                            step = i * 4 + (8 * b + s)
                            split_hi(layer, n + 1, s + 1, 12, 2)
                            act.wait_ge(block_done.sem, block_done.at(layer, n + 1))
                            act.wait_ge(merged_step.sem, merged_step.at(layer, step - 1))
                            taken(A.activation(gate_sg[:, s % 2, :], psum_a[s % 2][:, 0:NT], ACT.Sigmoid,
                                               bias=vecs[:, layer, bass.ds(i * 4 + (V_BMERGE + 8 * b + s), 1)]), 2)

                merge(0)

                with act.Fori(0, HEADS) as h:
                    for j in range(4):
                        p = head_block(1, h, j)
                        if j < 3:
                            to_pad(B_conv, h, j, p)
                        else:
                            act.wait_ge(B_y.sem, B_y.at(layer, h))
                            A.activation(B_gb[:, 0:SAMPLE + 1], p[:, 0:SAMPLE + 1], ACT.Silu)
                            A.drain()
                            taken(A.activation(B_gb[:, SAMPLE + 1:SP1], p[:, SAMPLE:NT], ACT.Silu), HEADS)
                    act.wait_ge(dec_ready_l.sem, dec_ready_l.at(layer, 1))
                    for t in range(TILES):
                        last = A.activation(win[:, t, :], dec_abs[:, h, :], ACT.Exp, scale=dist[:, t:t + 1])
                    last.then_inc(B_win.sem, B_win.step)
                    act.wait_ge(B_h_mm.sem, B_h_mm.at(layer, h + 1))
                    copy(Hf, M[:, 0:2048].rearrange("p (f o c) -> p f o c", f=8, o=2)).then_inc(B_h.sem, B_h.step)
                    for r in range(2):
                        act.wait_ge(B_tr.sem, B_tr.at(layer, h * 2 + (r + 1)))
                        copy(vt_b, M[:, 1024:1664].rearrange("p (t c) -> p t c", t=5)).then_inc(B_vt.sem, B_vt.step)
                merge(1)

                def evacuate(b, X_, h):
                    for j, dst in enumerate((qT, kT, vT, gT)):
                        p = head_block(b, h, j)
                        if j == 3:
                            act.wait_ge(X_["y"].sem, X_["y"].at(layer, h))
                            taken(A.activation(gT, p[:, 0:NT], ACT.Silu), HEADS)
                        else:
                            taken(copy(dst, p[:, 0:NT], (128.0 if b == 2 else 64.0) ** -0.5 if j == 0 else 1.0), HEADS)
                    act.wait_ge(X_["tr"].sem, X_["tr"].at(layer, h + 1))
                    act.wait_ge(X_["stored"].sem, X_["stored"].at(layer, h))
                    copy(v_t, M[:, 1024:1664].rearrange("p (t c) -> p t c", t=5))
                    copy(k_p, M[:, 1664:1792]).then_inc(X_["vt"].sem, X_["vt"].step)

                with act.Fori(0, HEADS) as h:
                    evacuate(2, C, h)

                    def probs(m):
                        act.wait_ge(C["mx"].sem, C["mx"].at(layer, h * 5 + (m + 1)))
                        cols = slice(0 if m < 4 else SAMPLE, NT)
                        A.activation(s_buf[:, m % 2, cols], s_buf[:, m % 2, cols], ACT.Exp, bias=stat[:, m:m + 1],
                                               accum_out=stat[:, 8 + m:9 + m]).then_inc(C["p"].sem, C["p"].step)

                    probs(0)
                    for m in range(5):
                        if m < 4:
                            probs(m + 1)
                        act.wait_ge(C["pt_mm"].sem, C["pt_mm"].at(layer, h * 5 + (m + 1)))
                        if m < 4:
                            copy(PT[:, :, 128 * m:128 * m + 128], M[:, 1024:1664].rearrange("p (t c) -> p t c", t=5)).then_inc(C["pt"].sem, C["pt"].step)
                        else:
                            copy(PTp, M[:, 1536:1664]).then_inc(C["pt"].sem, C["pt"].step)
                merge(2)
                act.wait_ge(C["stored"].sem, C["stored"].at(layer, HEADS))
                with act.Fori(0, HEADS) as h:
                    evacuate(3, Dd, h)
                    for m in range(5):
                        act.wait_ge(Dd["mx"].sem, Dd["mx"].at(layer, h * 5 + (m + 1)))
                        cols = slice(0 if m < 4 else SAMPLE, NT)
                        for i in range(2):
                            last = A.activation(s_buf[:, i, cols], M[:, 1024 * i + cols.start:1024 * i + NT], ACT.Exp,
                                                bias=stat[:, 2 * m + i:2 * m + i + 1], accum_out=stat[:, 16 + 2 * m + i:17 + 2 * m + i])
                        last.then_inc(Dd["p"].sem, Dd["p"].step)
                        act.wait_ge(Dd["pt_mm"].sem, Dd["pt_mm"].at(layer, h * 5 + (m + 1)))
                        f = 0 if m < 4 else 4
                        copy(PT[:, f:TILES, 0:128], M[:, 128 * f:NT].rearrange("p (t c) -> p t c", c=128)).then_inc(Dd["pt"].sem, Dd["pt"].step)
                merge(3)

                for n in range(OUT_BLOCKS):
                    if n < OUT_BLOCKS - 1:
                        split_hi(layer, base(4) + n + 1, n + 1, 8, 1)
                    act.wait_ge(block_done.sem, block_done.at(layer, base(4) + n + 1))
                    if n >= 2:
                        act.wait_ge(yt_mm.sem, yt_mm.at(layer, n - 1))
                    taken(copy(y_cm[:, n % 2, :], psum_a[n % 2][:, 0:NT]), 1)
                act.wait_ge(gate_mm.sem, gate_mm.at(layer, 1))
                copy(gate_b, M[:, 0:2048].rearrange("p (g c) -> p g c", g=2)).then_inc(gate_bc.sem, gate_bc.step)
                for t in range(TILES):
                    A.drain()
                    last = A.activation(psum_a[0][:, :], y_tm[:, t, :], ACT.Square, accum_out=stat[:, t:t + 1])
                last.then_inc(y_ss.sem, y_ss.step)

        @block.vector
        def _(dve):
            V = nc.vector
            V.memset(hid_t[64:65, :], 1.0)
            start(dve)
            dve.wait_ge(consts_in.sem, N_CONST)
            dve.wait_ge(raw_zero.sem, 1)
            V.tensor_copy(level_t[:, :], area[:, 0:LEVELS * 384]).then_inc(level_cast.sem, level_cast.step)

            def tt(out, a_, b_, op):
                return V.tensor_tensor(out, a_, b_, op)

            def mul(out, a_, b_):
                return tt(out, a_, b_, ALU.mult)

            def add(out, a_, b_):
                return tt(out, a_, b_, ALU.add)

            def fence():
                held(dve)
                dve.drain()

            def over(v, *shape):
                return v.to_broadcast([128, *shape])

            def per_tile(cols):
                return over(cols.unsqueeze(2), TILES, 128)

            def all_tiles(mask):
                return over(mask.unsqueeze(1), TILES, 128)

            def split_lo(layer, n, static, width, times):
                r, s = static % RING, static % SPLITS
                dve.wait_ge(raw_in[r].sem, raw_in[r].at(layer, raw_uses(n, static)))
                dve.wait_ge(hi_ready.sem, hi_ready.at(layer, n + 1))
                tt(w_lo[:, s, 0:width, :], raw[:, r, 0:width, :], w_hi[:, s, 0:width, :].bitcast(f32), ALU.subtract).then_inc(lo_ready.sem, lo_ready.step)

            def split_y(h, sig):
                fence()
                V.tensor_copy(y_hi[:, h, :], tmp640[:, :])
                fence()
                tt(y_lo[:, h, :], tmp640[:, :], y_hi[:, h, :].bitcast(f32), ALU.subtract).then_inc(sig.sem, sig.step)

            def head_block(layer, b, h, j):
                split_lo(layer, h * 4 + (base(b) + j + 1), j + 1, 8 if j < 3 else 12, HEADS)

            def rms(layer, tile, sq, ss, rn, n_ss, times, done):
                mul(sq, tile, tile)
                fence()
                V.tensor_reduce(stat[:, 0:5], sq, AX.X, ALU.add)
                fence()
                V.tensor_scalar(stat[:, 0:5], stat[:, 0:5], 1.0 / 128, EPS, ALU.mult, ALU.add).then_inc(ss.sem, ss.step)
                dve.wait_ge(rn.sem, rn.at(layer, n_ss))
                mul(tile, tile, per_tile(stat[:, 0:5])).then_inc(done.sem, done.step)

            with dve.Fori(0, DEPTH) as layer:
                vec = lambda c, n=1: vecs[:, layer, c:c + n]
                dve.wait_ge(layer_in2[0].sem, layer_in2[0].at(layer, 1))
                lv4 = lam_in[:, :].rearrange("p (a b c) -> p a b c", a=2, b=2)
                mul(tmp640[:, 0:128].rearrange("p (a c) -> p a c", a=2), lv4[:, :, 0, :], lv4[:, :, 1, :])
                fence()
                V.tensor_reduce(lam_s[:, 0:2], tmp640[:, 0:128].rearrange("p (a c) -> p a c", a=2), AX.X, ALU.add).then_inc(lam_v.sem, lam_v.step)
                dve.wait_ge(x_ss.sem, x_ss.at(layer, 1))
                V.tensor_scalar(stat[:, 0:5], stat[:, 0:5], 1.0 / D, EPS, ALU.mult, ALU.add).then_inc(x_sq.sem, x_sq.step)
                dve.wait_ge(x_rn.sem, x_rn.at(layer, 1))
                for t in range(TILES):
                    last = V.tensor_scalar(x_n_v[:, t, :], x_tm[:, t, :], stat[:, t:t + 1], None, ALU.mult)
                last.then_inc(x_n.sem, x_n.step)
                dve.wait_ge(lam_e.sem, lam_e.at(layer, 1))
                tt(lam_s[:, 4:5], lam_s[:, 3:4], lam_s[:, 2:3], ALU.subtract)
                V.tensor_scalar(lam_s[:, 5:6], vec(V_LAM), -1.0, 1.0, ALU.mult, ALU.add)
                fence()
                tt(lam_s[:, 4:5], lam_s[:, 4:5], vec(V_LAM), ALU.subtract)
                mul(lam_s[:, 5:6], lam_s[:, 5:6], vec(V_DIFF)).then_inc(lam_v.sem, lam_v.step)
                dve.wait_ge(mod_mm.sem, mod_mm.at(layer, MOD_BLOCKS))
                add(mod, M[:, 0:48].rearrange("p (k g) -> p k g", g=2), over(vec(V_BMOD, 24).unsqueeze(2), 24, 2))
                fence()
                V.scalar_tensor_tensor(g_scale, mod[:, 8:16, :], 1.0, over(vec(V_PRE, 8).unsqueeze(2), 8, 2), ALU.add, ALU.mult)
                mul(gate_post, mod[:, 16:24, :].rearrange("p k g -> p g k"), over(vec(V_POST, 8).unsqueeze(1), 2, 8)).then_inc(mod_ready.sem, mod_ready.step)
                x, turns = hid_tmp[0:HY_FF, 0, :], tmp640[0:HY_FF, :]
                for j in range(2):
                    dve.wait_ge(hid_mm.sem, hid_mm.at(layer, j + 1))
                    V.tensor_scalar(x, M[0:HY_FF, 0:NT], vecs[0:HY_FF, layer, V_HB1 + j:V_HB1 + j + 1], None, ALU.add)
                    fence()
                    V.tensor_scalar(turns, x, 1.0 / (2 * math.pi), MAGIC, ALU.mult, ALU.add)
                    fence()
                    V.tensor_scalar(turns, turns, MAGIC, None, ALU.subtract)
                    fence()
                    V.scalar_tensor_tensor(x, turns, -6.28125, x, ALU.mult, ALU.add)
                    fence()
                    V.scalar_tensor_tensor(x, turns, -(2 * math.pi - 6.28125), x, ALU.mult, ALU.add)
                    fence()
                    V.tensor_scalar(x, x, 3.1415925, -3.1415925, ALU.min, ALU.max).then_inc(hid_arg.sem, hid_arg.step)
                for k in range(KT):
                    dve.wait_ge(ht_raw.sem, ht_raw.at(layer, k + 1))
                    V.tensor_copy(h_hi_v[:, k, :], gate_sg[:, k % 2, :])
                    fence()
                    tt(h_lo_v[:, k, :], gate_sg[:, k % 2, :], h_hi_v[:, k, :].bitcast(f32), ALU.subtract).then_inc(h_ready.sem, h_ready.step)
                ab = lambda i: ab_s[:, 40 * i:40 * i + 40]
                dht = lambda v: v.rearrange("p (d h t) -> p d h t", d=2, h=4)
                dve.wait_ge(ab_mm.sem, ab_mm.at(layer, 1))
                src = M[:, 0:80].rearrange("p (t d k h) -> p k d h t", t=5, d=2, k=2)
                for d in range(2):
                    add(dht(ab(6))[:, d], src[:, 0, d], over(vecs[:, layer, V_DT + 4 * d:V_DT + 4 * d + 4].unsqueeze(2), 4, 5))
                    V.tensor_copy(dht(ab(7))[:, d], src[:, 1, d])
                fence()
                V.scalar_tensor_tensor(ab(8), ab(6), -1.0, ab(6), ALU.mult, ALU.max).then_inc(ab_v.sem, ab_v.step)
                dve.wait_ge(ab_l.sem, ab_l.at(layer, 1))
                V.scalar_tensor_tensor(ab(6), ab(6), 0.0, ab(8), ALU.max, ALU.add)
                V.tensor_scalar(ab(9), ab(9), 1.0, None, ALU.add)
                fence()
                V.reciprocal(ab(1), ab(9))
                V.scalar_tensor_tensor(ab(0).rearrange("p (a t) -> p a t", t=5), ab(6).rearrange("p (a t) -> p a t", t=5), -1.0,
                                               over(exp_alog[:, :].unsqueeze(2), 8, 5), ALU.mult, ALU.mult).then_inc(ab_v.sem, ab_v.step)
                dve.wait_ge(gc_mm.sem, gc_mm.at(layer, 1))
                V.tensor_copy(ab(8), M[:, 512:552])
                V.tensor_copy(ab(7), M[:, 576:616])
                fence()
                tt(ab(3), ab(7), ab(8), ALU.subtract).then_inc(ab_v.sem, ab_v.step)
                dve.wait_ge(gc_e.sem, gc_e.at(layer, 1))
                mul(ab(5), ab(1), ab(2)).then_inc(ab_done.sem, ab_done.step)
                split_lo(layer, 0, 0, 8, 1)

                def convolve(out, h, first, sig):
                    w = lambda i: small[:, layer * HEADS + h, first + i:first + i + 1]
                    V.tensor_scalar(out, pad[:, 1:1 + SP1], w(1), None, ALU.mult)
                    fence()
                    V.scalar_tensor_tensor(out, pad[:, 0:SP1], w(0), out, ALU.mult, ALU.add)
                    fence()
                    V.scalar_tensor_tensor(out, pad[:, 2:2 + SP1], w(2), out, ALU.mult, ALU.add).then_inc(sig.sem, sig.step)

                with dve.Fori(0, HEADS) as h:
                    def col(i, d, t=None):
                        if t is None:
                            return ab_s[:, bass.ds(h * 5 + (40 * i + 20 * d), 5)]
                        return ab_s[:, bass.ds(h * 5 + (40 * i + 20 * d + t), 1)]

                    for j in range(4):
                        head_block(layer, 0, h, j)
                        if j < 3:
                            dve.wait_ge(proj_taken.sem, proj_taken.at(layer, h * 4 + (base(0) + j + 1)))
                            convolve(A_c[:, j, :], h, 3 * j, A_conv)
                    for d in range(2):
                        last = mul(g1[:, d, :, :], per_tile(col(0, d)), all_tiles(strict[:, d, :]))
                    last.then_inc(A_g1.sem, A_g1.step)
                    dve.wait_ge(A_tm.sem, A_tm.at(layer, h + 1))
                    mul(sq_a.rearrange("p (a c) -> p a c", c=128), A_tmv[:, 0:2, :, :].rearrange("p w t c -> p (w t) c"),
                        A_tmv[:, 0:2, :, :].rearrange("p w t c -> p (w t) c"))
                    fence()
                    V.tensor_reduce(stat[:, 0:10], sq_a.rearrange("p (a c) -> p a c", c=128), AX.X, ALU.add)
                    fence()
                    V.tensor_scalar(stat[:, 0:10], stat[:, 0:10], EPS, None, ALU.add).then_inc(A_ss.sem, A_ss.step)
                    for d in range(2):
                        dve.wait_ge(A_dec.sem, A_dec.at(layer, h * 2 + (d + 1)))
                        mul(dec[:, d, :, :], dec[:, d, :, :], all_tiles(strict[:, d, :]))
                        mul(decT[:, d, :, :], decT[:, d, :, :], all_tiles(tri[:, d, :]))
                        fence()
                        mul(dec[:, d, :, :], dec[:, d, :, :], per_tile(col(1, d)))
                    dve.wait_ge(A_rn.sem, A_rn.at(layer, h * 2 + 1))
                    V.tensor_scalar(stat[:, 0:5], stat[:, 0:5], 128.0 ** -0.5, None, ALU.mult)
                    mul(kqn[:, :, 0, :], A_tmv[:, 1, :, :], per_tile(stat[:, 5:10]))
                    fence()
                    mul(kqn[:, :, 1, :], A_tmv[:, 0, :, :], per_tile(stat[:, 0:5])).then_inc(A_kqn.sem, A_kqn.step)
                    fence()
                    for d in range(2):
                        mul(Rv[:, d, :, :], A_tmv[:, 2, :, :], per_tile(col(1, d)))
                        mul(Rk[:, d, :, :], kqn[:, :, 0, :], per_tile(col(5, d)))
                        mul(kd[:, d, :, :], kqn[:, :, 0, :], per_tile(col(3, d)))
                    V.memset(o_tm, 0.0)
                    dve.wait_ge(A_gram.sem, A_gram.at(layer, h + 1))
                    gram = M[:, 0:1280].rearrange("p (t j c) -> p t j c", t=5, j=2)
                    for d in range(2):
                        mul(dec[:, d, :, :], dec[:, d, :, :], gram[:, :, 0, :])
                        last = mul(decT[:, d, :, :], decT[:, d, :, :], gram[:, :, 1, :])
                    last.then_inc(A_lat.sem, A_lat.step)
                    with dve.Fori(0, LEVELS) as lv:
                        e = h * (3 * LEVELS) + lv * 3
                        fence()
                        V.tensor_copy(level_now[:, :], level[:, lv, :])
                        fence()
                        lower, upper = (over(level_v[:, i, :].unsqueeze(1), 4, 128) for i in range(2))
                        quad = lambda at: M[:, at:at + 512].rearrange("p (t c) -> p t c", c=128)
                        pair = lambda at: M[:, at:at + 256].rearrange("p (t c) -> p t c", c=128)
                        jobs = (((X[:, 0, 0:4, :], lower, quad(1536)), (XT[:, 0, 0:4, :], upper, quad(0))),
                                ((X[:, 1, 0:4, :], upper, quad(512)), (XT[:, 1, 0:4, :], lower, quad(1024))),
                                ((X[:, :, 4, :], level_v[:, 0:2, :], pair(1536)), (XT[:, :, 4, :], level_v[:, 1:3, :], pair(1792))))
                        for gi, job in enumerate(jobs):
                            dve.wait_ge(A_d.sem, A_d.at(layer, e + (gi + 1)))
                            held(dve)
                            for out, mask, data in job:
                                last = V.copy_predicated(out, mask, data)
                            last.then_inc(A_x.sem, A_x.step)
                    for n in range(5):
                        ts = (n, 3 - n) if n < 4 else (4, 4)
                        dve.wait_ge(A_sb.sem, A_sb.at(layer, h * 5 + (n + 1)))
                        fence()
                        oa = [M[:, 1536 + 128 * d:1664 + 128 * d] for d in range(2)]
                        if n < 4:
                            for d, t in enumerate(ts):
                                V.scalar_tensor_tensor(S[:, d, :], S[:, d, :], col(4, d, t), M[:, 1792 + 128 * d:1920 + 128 * d], ALU.mult, ALU.add)
                                V.scalar_tensor_tensor(o_tm[:, t, :], M[:, 1280 + 128 * d:1408 + 128 * d], col(2, d, t), o_tm[:, t, :], ALU.mult, ALU.add)
                            fence()
                            for d, t in enumerate(ts):
                                last = add(o_tm[:, t, :], o_tm[:, t, :], oa[d])
                        else:
                            dve.wait_ge(A_stored.sem, A_stored.at(layer, h))
                            V.tensor_copy(S_out, M[:, 1792:2048].rearrange("p (d c) -> p d c", d=2))
                            V.tensor_copy(o_tm[:, 4, :], oa[0])
                            fence()
                            last = add(o_tm[:, 4, :], o_tm[:, 4, :], oa[1])
                        last.then_inc(A_su.sem, A_su.step)
                    fence()
                    rms(layer, o_tm, sq_a[:, 0:NT].rearrange("p (t c) -> p t c", t=5), A_ss, A_rn, h * 2 + 2, HEADS, A_o)
                    dve.wait_ge(A_ot.sem, A_ot.at(layer, h + 1))
                    fence()
                    V.scalar_tensor_tensor(tmp640[:, :], M[:, 0:NT], vec(V_GDN), A_zb, ALU.mult, ALU.mult)
                    split_y(h, A_y)

                def merge(b):
                    with dve.Fori(0, 2) as i:
                        for s in range(4):
                            n = i * 4 + (base(b) + 16 + s)
                            step = i * 4 + (8 * b + s)
                            split_lo(layer, n + 1, s + 1, 12, 2)
                            dve.wait_ge(br_mm.sem, br_mm.at(layer, step + 1))
                            dve.wait_ge(proj_taken.sem, proj_taken.at(layer, n + 1))
                            br, out = M[:, 1024 * (s % 2):1024 * (s % 2) + NT], merged[:, i * 4 + s, :]
                            if b == 0:
                                last = mul(out, gate_sg[:, s % 2, :], br)
                            else:
                                fence()
                                mul(tmp640[:, :], gate_sg[:, s % 2, :], br)
                                fence()
                                last = add(out, out, tmp640[:, :])
                            last.then_inc(merged_step.sem, merged_step.step)

                merge(0)

                dve.wait_ge(layer_in2[5].sem, layer_in2[5].at(layer, 1))
                V.scalar_tensor_tensor(dec_abs, dec_abs, -1.0, dec_abs, ALU.mult, ALU.max).then_inc(dec_ready_l.sem, dec_ready_l.step)
                parts = ((slice(0, SAMPLE), slice(0, SAMPLE)), (slice(SAMPLE, NT), slice(SAMPLE + 1, SP1)))
                with dve.Fori(0, HEADS) as h:
                    skip = lambda r: small[:, layer * HEADS + h, 18 + r:19 + r]
                    for j in range(4):
                        head_block(layer, 1, h, j)
                        dve.wait_ge(proj_taken.sem, proj_taken.at(layer, h * 4 + (base(1) + j + 1)))
                        if j < 3:
                            convolve(B_c[:, j, :], h, 9 + 3 * j, B_conv)
                        else:
                            fence()
                            mul(B_c[:, 2, :], B_c[:, 2, :], B_gb)
                    dve.wait_ge(B_win.sem, B_win.at(layer, h + 1))
                    dve.wait_ge(B_filt_mm.sem, B_filt_mm.at(layer, h + 1))
                    mul(filt, M[:, 0:1280].rearrange("p (t c) -> p t c", t=5), win).then_inc(B_filt.sem, B_filt.step)
                    re, im = (M[:, x:x + 512].rearrange("p (f c) -> p f c", f=4) for x in (1024, 1536))
                    for r in range(2):
                        dve.wait_ge(B_u.sem, B_u.at(layer, h * 2 + (r + 1)))
                        Hr, Hi = Hf[:, 0:4, r, :], Hf[:, 4:8, r, :]
                        fence()
                        mul(t1, re, Hr)
                        mul(t2, im, Hi)
                        fence()
                        tt(Yf[:, 0:4, :], t1, t2, ALU.subtract)
                        fence()
                        mul(t1, re, Hi)
                        mul(t2, im, Hr)
                        fence()
                        add(Yf[:, 4:8, :], t1, t2).then_inc(B_y0.sem, B_y0.step)
                        dve.wait_ge(B_inv.sem, B_inv.at(layer, h * 2 + (r + 1)))
                        if r == 0:
                            for o, c in parts:
                                V.scalar_tensor_tensor(z1[:, o], B_c[:, 0, c], skip(0), M[:, o], ALU.mult, ALU.add)
                            fence()
                            for o, c in parts:
                                last = mul(z1[:, o], z1[:, o], B_c[:, 1, c])
                            last.then_inc(B_z1.sem, B_z1.step)
                        else:
                            fence()
                            V.scalar_tensor_tensor(tmp640[:, :], z1, skip(1), M[:, 0:NT], ALU.mult, ALU.add)
                            fence()
                            for o, c in parts:
                                mul(tmp640[:, o], tmp640[:, o], B_c[:, 2, c])
                            split_y(h, B_y)
                merge(1)

                with dve.Fori(0, HEADS) as h:
                    for j in range(4):
                        head_block(layer, 2, h, j)
                    dve.wait_ge(C["in2"].sem, C["in2"].at(layer, h + 1))

                    def logits(m):
                        dve.wait_ge(C["s"].sem, C["s"].at(layer, h * 5 + (m + 1)))
                        if m >= 2:
                            dve.wait_ge(C["pt_mm"].sem, C["pt_mm"].at(layer, h * 5 + (m - 1)))
                        s = s_buf[:, m % 2, :]
                        if m < 4:
                            add(s[:, 0:SAMPLE], M[:, 0:SAMPLE], bias[:, (6 - 2 * m) * GRID_W:(6 - 2 * m) * GRID_W + SAMPLE])
                        V.tensor_copy(s[:, SAMPLE:NT], M[:, SAMPLE:NT])
                        fence()
                        V.tensor_reduce(stat[:, m:m + 1], s if m < 4 else s[:, SAMPLE:NT], AX.X, ALU.max, negate=True).then_inc(C["mx"].sem, C["mx"].step)

                    logits(0)
                    for m in range(5):
                        if m < 4:
                            logits(m + 1)
                        dve.wait_ge(C["p"].sem, C["p"].at(layer, h * 5 + (m + 1)))
                        V.reciprocal(stat[:, 16 + m:17 + m], stat[:, 8 + m:9 + m])
                        fence()
                        cols = slice(0 if m < 4 else SAMPLE, NT)
                        V.tensor_scalar(s_buf[:, m % 2, cols], s_buf[:, m % 2, cols], stat[:, 16 + m:17 + m], None, ALU.mult).then_inc(C["pn"].sem, C["pn"].step)
                    dve.wait_ge(C["pv"].sem, C["pv"].at(layer, h + 1))
                    fence()
                    mul(tmp640[:, :], M[:, 0:NT], gT)
                    split_y(h, C["y"])
                merge(2)

                with dve.Fori(0, HEADS) as h:
                    for j in range(4):
                        head_block(layer, 3, h, j)
                    dve.wait_ge(rope_in[0].sem, rope_in[0].at(layer, 1))
                    dve.wait_ge(rope_in[1].sem, rope_in[1].at(layer, 1))
                    dve.wait_ge(Dd["tr"].sem, Dd["tr"].at(layer, h + 1))
                    for i, x_ in enumerate((qT, kT)):
                        mul(rope_tmp, M[:, 512 * i:512 * i + 512], sinT)
                        mul(x_[:, 0:SAMPLE], x_[:, 0:SAMPLE], cosT)
                        fence()
                        last = add(x_[:, 0:SAMPLE], x_[:, 0:SAMPLE], rope_tmp)
                        if i == 0:
                            fence()
                    last.then_inc(Dd["rope"].sem, Dd["rope"].step)
                    for m in range(5):
                        dve.wait_ge(Dd["s"].sem, Dd["s"].at(layer, h * 5 + (m + 1)))
                        first = 0 if m < 4 else SAMPLE
                        V.tensor_reduce(stat[:, 2 * m:2 * m + 2],
                                                    M[:, 0:2048].rearrange("p (i c) -> p i c", i=2)[:, :, first:NT],
                                                    AX.X, ALU.max, negate=True).then_inc(Dd["mx"].sem, Dd["mx"].step)
                        dve.wait_ge(Dd["p"].sem, Dd["p"].at(layer, h * 5 + (m + 1)))
                        sums, rec = stat[:, 16 + 2 * m:18 + 2 * m], stat[:, 32 + 2 * m:34 + 2 * m]
                        V.reciprocal(rec, sums)
                        fence()
                        V.scalar_tensor_tensor(stat[:, 48 + m:49 + m], sums[:, 0:1], rec[:, 1:2], lam_s[:, 4:5], ALU.mult, ALU.mult)
                        fence()
                        V.scalar_tensor_tensor(s_buf[:, 0, first:NT], s_buf[:, 1, first:NT], stat[:, 48 + m:49 + m],
                                                           s_buf[:, 0, first:NT], ALU.mult, ALU.add).then_inc(Dd["pn"].sem, Dd["pn"].step)
                        dve.wait_ge(Dd["pv"].sem, Dd["pv"].at(layer, h * 5 + (m + 1)))
                        V.tensor_scalar(d_o[:, m, :], M[:, 1024:1152], rec[:, 0:1], None, ALU.mult).then_inc(Dd["o"].sem, Dd["o"].step)
                    fence()
                    rms(layer, d_o, d_sq.rearrange("p (t c) -> p t c", t=5), Dd["ss"], Dd["rn"], h + 1, HEADS, Dd["on"])
                    dve.wait_ge(Dd["ot"].sem, Dd["ot"].at(layer, h + 1))
                    fence()
                    V.scalar_tensor_tensor(tmp640[:, :], M[:, 0:NT], lam_s[:, 5:6], gT, ALU.mult, ALU.mult)
                    split_y(h, Dd["y"])
                merge(3)

                dve.wait_ge(block_done.sem, block_done.at(layer, base(4)))
                fence()
                V.tensor_copy(h_hi[:, :], merged_t[:, :])
                fence()
                tt(h_lo[:, :], merged_t[:, :], h_hi[:, :].bitcast(f32), ALU.subtract).then_inc(m_split.sem, m_split.step)
                mul(diag, over(ident[:, :].unsqueeze(1), 16, 128),
                                 over(gate_post_t[:, :].unsqueeze(2), 16, 128)).then_inc(gate_diag.sem, gate_diag.step)
                for n in range(OUT_BLOCKS):
                    if n < OUT_BLOCKS - 1:
                        split_lo(layer, base(4) + n + 1, n + 1, 8, 1)
                    dve.wait_ge(yt_mm.sem, yt_mm.at(layer, n + 1))
                    V.tensor_copy(y_tm[:, :, 128 * n:128 * n + 128],
                                         M[:, 1024 * (n % 2):1024 * (n % 2) + NT].rearrange("p (t c) -> p t c", t=5)).then_inc(ytm.sem, ytm.step)
                dve.wait_ge(y_ss.sem, y_ss.at(layer, 1))
                V.tensor_scalar(stat[:, 0:5], stat[:, 0:5], 1.0 / D, EPS, ALU.mult, ALU.add).then_inc(y_sq.sem, y_sq.step)
                dve.wait_ge(y_rn.sem, y_rn.at(layer, 1))
                dve.wait_ge(gate_bc.sem, gate_bc.at(layer, 1))
                for t in range(TILES):
                    V.scalar_tensor_tensor(y_tm[:, t, :], y_tm[:, t, :], stat[:, t:t + 1], gate_b[:, int(t == 4), :], ALU.mult, ALU.mult)
                dve.wait_ge(x_reload.sem, x_reload.at(layer, 1))
                fence()
                add(x_tm, x_tm, y_tm).then_inc(x_new.sem, x_new.step)


def layouts(x):
    f = lambda n: np.ascontiguousarray(np.asarray(x[n]))
    A = np.ascontiguousarray

    def blocks(w):
        *lead, k, n = w.shape
        w = w.reshape(*lead, k // 128, 128, n // 128, 128)
        w = np.moveaxis(w, (-2, -3), (len(lead), len(lead) + 1))
        return w.reshape(*lead, n // 128, 128, k)

    w_in = f("w_in")
    sections = [w_in[..., 0:2048], w_in[..., 2064:4112], w_in[..., 4112:6160], w_in[..., 6160:8208]]
    w4 = np.stack([s.reshape(DEPTH, D, 4, HEADS, 128).transpose(0, 1, 3, 2, 4).reshape(DEPTH, D, 2048) for s in sections], 1)
    w_merge = blocks(f("w_merge").reshape(DEPTH, D, 4, D).transpose(0, 2, 1, 3))
    w_branch = blocks(f("w_branch"))
    vec = lambda v: v.reshape(DEPTH, -1, 128).transpose(2, 0, 1)
    rows = lambda v: np.broadcast_to(v.reshape(1, DEPTH, -1), (128, DEPTH, v.size // DEPTH))
    ff = lambda v: np.concatenate([v, np.zeros_like(v)], 1).T.reshape(128, DEPTH, 1)
    lam_init = np.array([0.8 - 0.6 * math.exp(-0.3 * i) for i in range(DEPTH)], np.float32)
    vecs = np.concatenate([
        vec(f("g_pre")), vec(f("g_post")), vec(f("b_mod")), vec(f("gdn_norm")), vec(f("diff_norm")),
        ff(f("hy_b1")), ff(f("hy_b2")), np.broadcast_to(lam_init.reshape(1, DEPTH, 1), (128, DEPTH, 1)),
        rows(f("gdn_dt_bias")), rows(f("gdn_a_log")), vec(f("b_merge"))], 2)
    conv = lambda n: f(n).reshape(DEPTH, 3, 3, HEADS, 128).transpose(4, 0, 3, 2, 1).reshape(128, DEPTH, HEADS, 9)
    skip = f("hy_skip").reshape(DEPTH, 2, HEADS, 128).transpose(3, 0, 2, 1)
    small = np.concatenate([conv("gdn_conv"), conv("hy_conv"), skip], 3)
    w12 = np.zeros((DEPTH, HY_FF, 2 * HY_FF), np.float32)
    w12[:, :HY_EMB, :HY_FF] = f("hy_w1")
    w12[:, :, HY_FF:] = f("hy_w2")
    w3 = np.concatenate([f("hy_w3"), f("hy_b3")[:, None, :]], 1).reshape(DEPTH, 65, 2, HEADS, 128).transpose(0, 1, 3, 2, 4)
    decay = f("hy_decay").reshape(DEPTH, 1, 2, HEADS, 128).transpose(0, 1, 3, 2, 4)
    cond = np.stack([f("c")[0], f("c_ctx")], -1).reshape(KT, 128, 2).transpose(1, 0, 2)
    state = f("state_gdn")[0].transpose(0, 2, 3, 1, 4)
    nat, diff = f("cache_nat_kv")[0], f("cache_diff_kv")[0]
    q, k = np.arange(GRID_W)[:, None], np.arange(GRID_W)[None, :]
    start = np.clip(q - WIN_C // 2, 0, GRID_W - WIN_C)
    inside = (k >= start) & (k < start + WIN_C)
    offset = np.where(inside, k - q + WIN_C - 1, 0)
    rpb = f("nat_rpb")
    table = np.where(inside, rpb[..., offset], np.float32(-1e30)).astype(rpb.dtype)
    half = lambda a: table[:, :, a:a + 14].transpose(0, 1, 3, 2, 4)
    bias = np.concatenate([half(1), half(0)], 2)
    return {
        "w_mod": blocks(f("w_mod")), "w_in": blocks(w4), "w_out": blocks(f("w_out")),
        "w_mb": A(np.concatenate([w_merge, w_branch], -1)),
        "x_sample": f("x_sample")[0], "x_prompt": f("x_prompt")[0],
        "vecs": A(vecs.reshape(128, -1)), "small": A(small.reshape(128, -1)), "w12": w12,
        "w3": A(w3.reshape(DEPTH, 65, 1024)), "decay": A(decay.reshape(DEPTH, 1, 1024)),
        "cond": A(cond.reshape(128, 16)), "state": A(state.reshape(DEPTH, HEADS, 128, 256)),
        "lam": f("diff_lam").reshape(DEPTH, 1, 256),
        "ab_w": A(w_in[..., 2048:2064].reshape(DEPTH, KT, 128, 16).transpose(0, 2, 1, 3).reshape(DEPTH, 128, 128)),
        "nat_kT": A(nat[:, 0].transpose(0, 1, 3, 2)), "nat_v": A(nat[:, 1]),
        "diff_kT": A(diff[:, 0].transpose(0, 1, 3, 2)), "diff_v": A(diff[:, 1]),
        "bias": A(bias.reshape(DEPTH, HEADS, 128, BIAS_W)),
    }


def constants():
    r, c = np.arange(128)[:, None], np.arange(128)[None, :]
    F = np.float32
    out = {"ident": (r == c).astype(F), "ones": np.ones((128, 128), F),
           "tri": np.concatenate([r <= c, r >= c], 1).astype(F), "strict": np.concatenate([r > c, r < c], 1).astype(F)}
    level = []
    for s in range(LEVELS):
        lower = ((r >> (s + 1)) == (c >> (s + 1))) & (((r >> s) & 1) == 1) & (((c >> s) & 1) == 0)
        level += [lower, lower.T, lower]
    out["level"] = np.concatenate(level, 1).astype(F)
    out["swap"] = ((r ^ 32) == c).astype(F)
    p = np.arange(128)
    out["dist"] = np.stack([-np.abs(p + 128 * t - SAMPLE // 2) / SAMPLE for t in range(4)] + [-np.abs(p - PROMPT // 2) / PROMPT], 1).astype(F)
    feats = []
    for n in (SAMPLE, PROMPT):
        t = np.arange(n, dtype=np.float64) / n
        ang = 2 * math.pi * t[:, None] * np.arange(1, BANDS + 1)
        feats.append(np.concatenate([t[:, None], np.cos(ang), np.sin(ang)], 1).T)
    out["feat"] = np.concatenate(feats, 1).astype(F)
    for name, n in (("s", SAMPLE), ("p", PROMPT)):
        m = 3 * n // 2
        t, k = np.arange(n)[:, None], np.arange(m // 2)[None, :]
        w = 2 * math.pi * (k + 0.5) / m
        re, im = np.cos(w * t), -np.sin(w * t)
        ire, iim = 2 / m * np.cos(w * (t + n // 2)), -2 / m * np.sin(w * (t + n // 2))
        if name == "s":
            fw = np.concatenate([re, im], 1).reshape(4, 128, 6, 128).transpose(1, 0, 2, 3)
            iv = np.concatenate([ire.T, iim.T], 0).reshape(6, 128, n).transpose(1, 0, 2)
        else:
            z = np.zeros((n, 128 - m // 2))
            fw = np.stack([np.concatenate([re, z], 1), np.concatenate([im, z], 1)], 1)
            iv = np.stack([np.concatenate([ire, z], 1).T, np.concatenate([iim, z], 1).T], 1)
        out[f"F_{name}"] = fw.reshape(128, -1).astype(F)
        out[f"Fi_{name}"] = iv.reshape(128, -1).astype(F)
    nf = 16
    inv = 10000.0 ** (-np.arange(nf) / nf)
    t = np.arange(SAMPLE)
    ang = np.concatenate([(t // GRID_W)[:, None] * inv, (t % GRID_W)[:, None] * inv], 1).T
    out["cos"] = np.concatenate([np.cos(ang)] * 4, 0).astype(F)
    out["sin"] = np.concatenate([-np.sin(ang), np.sin(ang)] * 2, 0).astype(F)
    return {k: np.ascontiguousarray(v) for k, v in out.items()}


def kernel(**inputs):
    import concourse.bacc as bacc
    from concourse.bass_utils import run_bass_kernel_spmd as run

    nc = bacc.Bacc("TRN2", target_bir_lowering=False, num_devices=1)
    arrays = {**layouts(inputs), **constants()}
    arrays = {f"in_{k}": np.ascontiguousarray(v) for k, v in arrays.items()}
    I = {k[3:]: nc.dram_tensor(k, v.shape, mybir.dt.from_np(v.dtype), kind="ExternalInput").ap() for k, v in arrays.items()}
    f32 = mybir.dt.float32
    shapes = {"x": (NT, D), "state": (DEPTH, HEADS, 128, 256), "nat": (DEPTH, 2, HEADS, 128, 128), "diff": (DEPTH, 2, HEADS, 128, 128)}
    O = {k: nc.dram_tensor(f"out_{k}", s, f32, kind="ExternalOutput").ap() for k, s in shapes.items()}
    program(nc, I, O)
    r = run(nc, [arrays], core_ids=[0]).results[0]
    state = r["out_state"].reshape(DEPTH, HEADS, 128, 2, 128).transpose(0, 3, 1, 2, 4)
    return (r["out_x"][None, SAMPLE:], r["out_x"][None, :SAMPLE], np.ascontiguousarray(state)[None],
            r["out_nat"][None], r["out_diff"][None])
```

```python
import concourse.bass as bass
from concourse import mybir
from contextlib import ExitStack
import math
import numpy as np

DEPTH, D, NT, SAMPLE, PROMPT = 2, 1024, 640, 512, 128
TILES, KT, HEADS, W = 5, 8, 4, 128
GRID_W, WIN_R, WIN_C = 64, 8, 16
BANDS, HY_EMB, HY_FF = 16, 33, 64
EPS = 1e-6
LEVELS = 7
SP1 = NT + 1
CONV_TILE = [0, 128, 256, 384, 513]
BIAS_W = 14 * GRID_W
RING, SPLITS = 2, 2
MOD_RING = 4
UNIT, MERGE_BLOCKS = 4, 12
MOD_BLOCKS, BRANCH_BLOCKS, OUT_BLOCKS = 24, HEADS * UNIT + MERGE_BLOCKS, 8
BRANCH_PROJ = HEADS * UNIT + 8
SPLIT_BLOCKS = 4 * BRANCH_BLOCKS + OUT_BLOCKS
RAW_BLOCKS = MOD_BLOCKS + SPLIT_BLOCKS
NSMALL = 20
V_PRE, V_POST, V_BMOD, V_GDN, V_DIFF, V_HB1, V_HB2, V_LAM, V_DT, V_ALOG, V_BMERGE, NVEC = (
    0, 8, 16, 40, 41, 42, 43, 44, 45, 53, 61, 93)
MAGIC = 1.5 * 2.0 ** 23


def program(nc, I, O):
    f32, f32r, u8 = mybir.dt.float32, mybir.dt.float32r, mybir.dt.uint8
    ALU, ACT, AX = mybir.AluOpType, mybir.ActivationFunctionType, mybir.AxisListType
    ctx = ExitStack()
    with ctx:
        def sb(name, shape, dt=f32):
            return ctx.enter_context(nc.sbuf_tensor(name, [shape[0], int(np.prod(shape[1:]))], dt))

        def view(t, *dims, at=0):
            n = int(np.prod(dims))
            names = "abcd"[:len(dims)]
            return t[:, at:at + n].rearrange(
                "p (" + " ".join(names) + ") -> p " + " ".join(names),
                **{x: d for x, d in zip(names[:-1], dims[:-1])}) if len(dims) > 1 else t[:, at:at + n]

        h_hi, h_lo = (sb(n, [128, KT, NT], f32r) for n in ("h_hi", "h_lo"))
        h_hi_v, h_lo_v = view(h_hi, KT, NT), view(h_lo, KT, NT)
        raw_t = sb("raw", [128, MOD_RING, KT, 128])
        raw = view(raw_t, MOD_RING, KT, 128)
        w_hi_t, w_lo_t = (sb(n, [128, SPLITS, KT, 128], f32r) for n in ("w_hi", "w_lo"))
        w_hi, w_lo = view(w_hi_t, SPLITS, KT, 128), view(w_lo_t, SPLITS, KT, 128)
        y_hi_t, y_lo_t = (sb(n, [128, HEADS, NT], f32r) for n in ("y_hi", "y_lo"))
        y_hi, y_lo = view(y_hi_t, HEADS, NT), view(y_lo_t, HEADS, NT)
        merged_t = sb("merged", [128, KT, NT])
        merged = view(merged_t, KT, NT)
        tmp640 = sb("tmp640", [128, NT])
        ident, ones = sb("ident", [128, 128]), sb("ones", [128, 128])
        tri_t, strict_t = sb("tri", [128, 2, 128]), sb("strict", [128, 2, 128])
        tri, strict = view(tri_t, 2, 128), view(strict_t, 2, 128)
        level_t, level_now = sb("level", [128, LEVELS, 384], u8), sb("level_now", [128, 384], u8)
        level, level_v = view(level_t, LEVELS, 384), view(level_now, 3, 128)
        swap = sb("swap", [128, 128])
        dist = sb("dist", [128, TILES])
        neg_half = sb("neg_half", [128, 16])
        small_t = sb("small", [128, DEPTH * HEADS, NSMALL])
        small = view(small_t, DEPTH * HEADS, NSMALL)
        vecs_t = sb("vecs", [128, DEPTH, NVEC])
        vecs = view(vecs_t, DEPTH, NVEC)
        cond_raw, cond = sb("cond_raw", [128, KT * 2]), sb("cond", [128, KT * 2])
        mod_t = sb("mod", [128, 24, 2])
        mod = view(mod_t, 24, 2)
        g_scale_t = sb("g_scale", [128, KT, 2])
        g_scale = view(g_scale_t, KT, 2)
        lam_in = sb("lam_in", [128, 256])
        lam_s = sb("lam_s", [128, 8])
        ab_w = sb("ab_w", [128, KT, 16])
        ab_w_hi, ab_w_lo = sb("ab_w_hi", [128, KT, 16], f32r), sb("ab_w_lo", [128, KT, 16], f32r)
        ab_s = sb("ab_s", [128, 10, 40])
        hid_t = sb("hid", [65, NT])
        gate_sg_t = sb("gate_sg", [128, 2, NT])
        gate_sg = view(gate_sg_t, 2, NT)
        exp_alog = sb("exp_alog", [128, 8])
        gate_post_t = sb("gate_post", [128, 2, KT])
        gate_post = view(gate_post_t, 2, KT)
        stat = sb("stat", [128, 64])

        AREA = 16800
        area = sb("area", [128, AREA])

        class Area:
            def __init__(self, at=0):
                self.at = at

            def take(self, *dims):
                n = int(np.prod(dims))
                v = view(area, *dims, at=self.at)
                self.at += n
                assert self.at <= AREA, self.at
                return v

        psum_a = [ctx.enter_context(nc.psum_tensor(f"proj{i}", [128, 1024], f32)) for i in range(2)]
        M = ctx.enter_context(nc.psum_tensor("mix", [128, 2048], f32))

        passed = {n: ctx.enter_context(nc.semaphore(f"passed_{n}")) for n in ("SP", "Pool", "PE", "Activation", "DVE")}

        class Signal:
            all = []

            def __init__(self, name, per_layer, first=0, step=1):
                self.sem = ctx.enter_context(nc.semaphore(name))
                self.per, self.step = per_layer, step
                self.first = max(first, 1) if step == 1 else 0
                Signal.all.append(self)

            def at(self, layer, n):
                return layer * (self.per * self.step) + n * self.step + self.first

        def held(eng):
            eng.sem_inc(passed[eng.engine.name], 1)

        def per_unit(name, k=1, step=1, first=0):
            return Signal(name, HEADS * k, step=step, first=first)

        raw_in = [Signal(f"raw_in{s}", MOD_BLOCKS // MOD_RING + (SPLIT_BLOCKS // RING if s < RING else 0), step=16)
                  for s in range(MOD_RING)]
        hi_ready = Signal("weight_hi_ready", SPLIT_BLOCKS, first=RING)
        lo_ready = Signal("weight_lo_ready", SPLIT_BLOCKS, first=RING)
        block_done = Signal("block_done", SPLIT_BLOCKS, first=SPLITS)
        proj_taken = Signal("proj_taken", 4 * BRANCH_PROJ + OUT_BLOCKS, first=2)
        mod_mm = Signal("mod_mm", MOD_BLOCKS, first=MOD_RING)
        exponent_set = Signal("exponent_set", 0)
        pad_zero = Signal("pad_zero", 1)
        level_cast = Signal("level_cast", 0)
        x_ss, y_ss = Signal("x_ss", 1), Signal("y_ss", 1)
        rope_in = [Signal(f"rope_in{i}", 1, step=16) for i in range(2)]
        consts_in = Signal("consts_in", 0, step=16)
        layer_in2 = [Signal(f"layer_in{i}", 1, step=16) for i in range(6)]
        cond_ready = Signal("cond_ready", 0)
        mod_ready = Signal("mod_ready", 1)
        mod_row, mod_t = Signal("mod_row", MOD_BLOCKS // 4), Signal("mod_t", 1)
        ab_split, ab_row, ab_t = Signal("ab_split", 1), Signal("ab_row", 1), Signal("ab_t", 1)
        x_in = Signal("x_in", 0, step=16)
        x_sq = Signal("x_sq", 1)
        x_rn = Signal("x_rn", 1)
        x_n = Signal("x_n", 1)
        xt_mm = Signal("xt_mm", KT)
        ht_raw = Signal("ht_raw", KT)
        h_ready = Signal("h_ready", KT)
        ab_mm = Signal("ab_mm", 1)
        ab_l = Signal("ab_l", 1)
        ab_v = Signal("ab_v", 3)
        gc_mm = Signal("gc_mm", 1)
        gc_e = Signal("gc_e", 1)
        ab_done = Signal("ab_done", 1)
        lam_v = Signal("lam_v", 2)
        lam_e = Signal("lam_e", 1)
        hid_mm = Signal("hid_mm", 2)
        hid_arg = Signal("hid_arg", 2)
        hid_sin = Signal("hid_sin", 2)
        dec_ready_l = Signal("decay_abs_ready", 1)
        A_conv, A_qkv = per_unit("A_conv", 3), per_unit("A_qkv")
        A_tr, A_tm, A_ss, A_rn = per_unit("A_tr"), per_unit("A_tm"), per_unit("A_ss", 2), per_unit("A_rn", 2)
        A_g1, A_rel, A_dec, A_kqn = per_unit("A_g1"), per_unit("A_rel", 2), per_unit("A_dec", 2), per_unit("A_kqn")
        A_kqt_mm, A_kqt, A_gram = per_unit("A_kqt_mm"), per_unit("A_kqt"), per_unit("A_gram")
        A_x0, A_lat = per_unit("A_x0"), per_unit("A_lat")
        A_q, A_qn, A_d = per_unit("A_q", 3 * (LEVELS - 1)), per_unit("A_qn", 3 * LEVELS), per_unit("A_d", 3 * LEVELS)
        A_x = per_unit("A_x", 3 * LEVELS, first=3)
        A_wt_mm, A_wt, A_s_in = per_unit("A_wt_mm"), per_unit("A_wt"), per_unit("A_s_in", step=16)
        A_va, A_vn, A_sb, A_su = per_unit("A_va", 5), per_unit("A_vn", 5), per_unit("A_sb", 5), per_unit("A_su", 5)
        A_s_out, A_stored = per_unit("A_s_out", step=16), per_unit("A_stored")
        A_o, A_ot, A_y = per_unit("A_o"), per_unit("A_ot"), per_unit("A_y")
        B_const = [Signal(f"B_const{i}", 1, step=16) for i in range(4)]
        B_conv = per_unit("B_conv", 3)
        B_win, B_filt_mm, B_filt = per_unit("B_win"), per_unit("B_filt_mm"), per_unit("B_filt")
        B_h_mm, B_h = per_unit("B_h_mm"), per_unit("B_h")
        B_tr, B_vt, B_u, B_y0, B_inv = (per_unit(n, 2) for n in ("B_tr", "B_vt", "B_u", "B_yf", "B_inv"))
        B_z1, B_y = per_unit("B_z1"), per_unit("B_y")
        def attention(n, dma, once, each):
            return {**{k: per_unit(f"{n}_{k}", step=16) for k in dma}, **{k: per_unit(f"{n}_{k}") for k in once},
                    **{k: per_unit(f"{n}_{k}", 5) for k in each}}

        C = attention("C", ("in0", "in1", "in2", "kv0", "kv1"), ("tr", "vt", "pv", "y", "stored"),
                      ("s", "mx", "p", "pn", "pt_mm", "pt"))
        Dd = attention("D", ("in0", "in1", "kv0", "kv1"), ("tr", "vt", "rope", "ss", "rn", "on", "ot", "y", "stored"),
                       ("s", "p", "pn", "pt_mm", "pt", "pv", "o"))
        Dd["mx"] = per_unit("D_mx", 10)
        br_mm, merged_step = Signal("branch_mm", 16), Signal("merged_step", 32, first=2)
        m_split = Signal("merged_split", KT)
        yt_mm, ytm = Signal("y_t", OUT_BLOCKS), Signal("y_tm", OUT_BLOCKS)
        gate_diag, gate_mm, gate_bc = Signal("gate_diag", 1), Signal("gate_mm", 1), Signal("gate_bc", 1)
        y_sq, y_rn, x_new = Signal("y_sq", 1), Signal("y_rn", 1), Signal("x_new", 1)
        x_back = Signal("x_back", 1, step=16)
        x_reload = Signal("x_reload", 1, step=16)
        x_out = Signal("x_out", 0, step=16)

        pre = Area()
        x_tm = pre.take(TILES, D)
        x_n_v = pre.take(TILES, D)
        feat = pre.take(NT)[0:HY_EMB]
        hy_w12 = pre.take(2 * HY_FF)[0:HY_FF]
        hid_tmp = pre.take(2, NT)[0:HY_FF]
        level_in = pre.take(LEVELS * 384)
        end = Area(TILES * D)
        y_tm = end.take(TILES, D)
        gate_b = end.take(2, D)
        y_cm = end.take(2, NT)
        diag = end.take(16, 128)
        a = Area()
        pad = a.take(643)
        A_c = a.take(3, SP1)
        A_L0 = a.at
        A_zb = a.take(NT)
        A_tmv = a.take(3, TILES, 128)
        kqn = a.take(TILES, 2, 128)
        kqT = a.take(TILES, 2, 128)
        g1 = a.take(2, TILES, 128)
        dec = a.take(2, TILES, 128)
        decT = a.take(2, TILES, 128)
        X = a.take(2, TILES, 128)
        XT = a.take(2, TILES, 128)
        Qn = a.take(2, TILES, 128)
        vn = a.take(2, 128)
        S = a.take(2, 128)
        S_out = a.take(2, 128)
        Rv = g1
        Rk = view(area, 2, TILES, 128, at=643)
        o_tm = view(area, TILES, 128, at=643 + 2 * NT)
        kd = view(area, 2, TILES, 128, at=A_L0 + NT)
        sq_a = view(area, 2 * NT, at=A_L0 + NT + 3 * NT + 4 * NT + 6 * NT)
        b_ = Area(643)
        F_s, F_p = b_.take(4, 6, 128), b_.take(2, 128)
        Fi_s, Fi_p = b_.take(6, 512), b_.take(2, 128)
        B_c = b_.take(3, SP1)
        B_gb = b_.take(SP1)
        Hf = b_.take(8, 2, 128)
        w3, dec_abs = b_.take(HEADS, 256), b_.take(HEADS, 256)
        B_over = b_.at
        filt, win = b_.take(TILES, 256), b_.take(TILES, 256)
        bo = Area(B_over)
        vt_b, Yf, z1 = bo.take(TILES, 128), bo.take(8, 128), bo.take(NT)
        t1, t2 = view(tmp640, 4, 128), view(gate_sg_t, 4, 128)
        c_ = Area()
        qT, kT, vT, gT = c_.take(NT), c_.take(NT), c_.take(NT), c_.take(NT)
        v_t = c_.take(TILES, 128)
        k_p = c_.take(128)
        ctx_k, ctx_v = c_.take(128), c_.take(128)
        bias = c_.take(BIAS_W)
        s_buf = c_.take(4, NT)
        PT = c_.take(TILES, 512)
        PTp = c_.take(128)
        d_o = c_.take(TILES, 128)
        d_sq = c_.take(NT)
        cosT, sinT = c_.take(512), c_.take(512)
        rope_tmp = c_.take(512)

        def raw_uses(n):
            return n // RING + (MOD_BLOCKS // MOD_RING + 1)

        def base(b):
            return b * BRANCH_BLOCKS

        def pbase(b):
            return b * BRANCH_PROJ

        D_scores = (psum_a[1][:, 0:NT], M[:, 1024:1024 + NT])

        AB_AT, GC_AT = 1664, 1792

        N_CONST = 10 * 16
        started = ctx.enter_context(nc.semaphore("started"))

        def start(eng):
            eng.wait_ge(started, 1)

        block = ctx.enter_context(nc.Block())

        @block.sync
        def _(sp):
            for s in Signal.all:
                if s.per and s.first:
                    sp.sem_inc(s.sem, s.first)
            sp.drain().then_inc(started, 1)
            start(sp)
            with sp.Fori(0, DEPTH) as layer:
                def load(slot, src):
                    sp.dma_start(raw[:, slot, :, :], src.rearrange("p (k c) -> p k c", k=KT)).then_inc(raw_in[slot].sem, raw_in[slot].step)

                sp.wait_ge(hi_ready.sem, hi_ready.at(layer, 0))
                held(sp)
                sp.wait_ge(lo_ready.sem, lo_ready.at(layer, 0))
                held(sp)
                with sp.Fori(0, MOD_BLOCKS // MOD_RING) as i:
                    for s in range(MOD_RING):
                        sp.wait_ge(mod_mm.sem, mod_mm.at(layer, i * MOD_RING + (s + 1 - MOD_RING)))
                        held(sp)
                        load(s, I["w_mod"][layer, i * MOD_RING + s, :, :])
                sp.wait_ge(mod_mm.sem, mod_mm.at(layer, MOD_BLOCKS - RING))
                held(sp)
                def stream(n, static, src):
                    sp.wait_ge(hi_ready.sem, hi_ready.at(layer, n - RING + 1))
                    held(sp)
                    sp.wait_ge(lo_ready.sem, lo_ready.at(layer, n - RING + 1))
                    held(sp)
                    load(static % RING, src)

                for b in range(4):
                    with sp.Fori(0, HEADS) as h:
                        for s in range(UNIT):
                            stream(h * UNIT + (base(b) + s), s, I["w_in"][layer, b, h * UNIT + s, :, :])
                    with sp.Fori(0, 2) as i:
                        for s in range(6):
                            stream(i * 6 + (base(b) + HEADS * UNIT + s), s, I["w_mb"][layer, b, i * 6 + s, :, :])
                with sp.Fori(0, OUT_BLOCKS // RING) as i:
                    for s in range(RING):
                        stream(i * RING + (base(4) + s), s, I["w_out"][layer, i * RING + s, :, :])

        @block.gpsimd
        def _(pool):
            P = nc.gpsimd
            start(pool)
            for dst, src in ((ident, I["ident"]), (ones, I["ones"]), (tri_t, I["tri"]), (strict_t, I["strict"]),
                             (level_in, I["level"]), (swap, I["swap"]), (dist, I["dist"]), (small_t, I["small"]),
                             (vecs_t, I["vecs"]), (cond_raw, I["cond"])):
                pool.dma_start(dst[:, :], src).then_inc(consts_in.sem, 16)
            P.memset(neg_half[:, :], -0.5).then_inc(exponent_set.sem, exponent_set.step)
            pool.dma_start(x_tm[:, 0:4, :], I["x_sample"].rearrange("(t p) d -> p t d", p=128)).then_inc(x_in.sem, x_in.step)
            pool.dma_start(x_tm[:, 4, :], I["x_prompt"]).then_inc(x_in.sem, x_in.step)
            pool.dma_start(O["x"][0:SAMPLE, :], I["x_sample"]).then_inc(x_out.sem, 16)
            pool.dma_start(O["x"][SAMPLE:NT, :], I["x_prompt"]).then_inc(x_out.sem, 16)
            pool.wait_ge(x_out.sem, 32)
            pool.wait_ge(consts_in.sem, N_CONST)
            pool.wait_ge(level_cast.sem, 1)
            pool.wait_ge(exponent_set.sem, 1)

            def power(layer, start_sig, n_wait, done_sig, cols):
                pool.wait_ge(start_sig.sem, start_sig.at(layer, n_wait))
                held(pool)
                P.tensor_tensor(stat[:, 0:cols], stat[:, 0:cols], neg_half[:, 0:cols], ALU.pow).then_inc(done_sig.sem, done_sig.step)

            with pool.Fori(0, DEPTH) as layer:
                pool.dma_start(lam_in[:, :], I["lam"][layer, :, :].to_broadcast([128, 256])).then_inc(layer_in2[0].sem, layer_in2[0].step)
                pool.dma_start(ab_w[:, :], I["ab_w"][layer, :, :]).then_inc(layer_in2[1].sem, layer_in2[1].step)
                pool.dma_start(hy_w12[0:HY_FF, :], I["w12"][layer, :, :]).then_inc(layer_in2[2].sem, layer_in2[2].step)
                pool.dma_start(feat[:, :], I["feat"]).then_inc(layer_in2[3].sem, layer_in2[3].step)
                power(layer, x_sq, 1, x_rn, 5)
                pool.wait_ge(h_ready.sem, h_ready.at(layer, KT))
                held(pool)
                pool.wait_ge(hid_sin.sem, hid_sin.at(layer, 2))
                held(pool)
                P.memset(pad, 0.0).then_inc(pad_zero.sem, pad_zero.step)
                with pool.Fori(0, HEADS) as h:
                    it = layer * HEADS + h
                    pool.wait_ge(A_su.sem, A_su.at(layer, h * 5))
                    held(pool)
                    pool.dma_start(S, I["state"][layer, h, :, :].rearrange("p (a b) -> p a b", a=2)).then_inc(A_s_in.sem, A_s_in.step)
                    power(layer, A_ss, h * 2 + 1, A_rn, 10)
                    pool.wait_ge(A_tm.sem, A_tm.at(layer, h + 1))
                    held(pool)
                    for dst in (X, XT):
                        for d in range(2):
                            last = P.tensor_copy(dst[:, d, :, :], ident[:, :].unsqueeze(1).to_broadcast([128, TILES, 128]))
                    last.then_inc(A_x0.sem, A_x0.step)
                    pool.wait_ge(A_su.sem, A_su.at(layer, h * 5 + 5))
                    held(pool)
                    pool.dma_start(O["state"][layer, h, :, :], S_out.rearrange("p a b -> p (a b)")).then_inc(A_s_out.sem, A_s_out.step)
                    power(layer, A_ss, h * 2 + 2, A_rn, 5)
                    pool.wait_ge(A_s_out.sem, A_s_out.at(layer, h + 1))
                    held(pool)
                    P.drain().then_inc(A_stored.sem, A_stored.step)
                pool.wait_ge(A_y.sem, A_y.at(layer, HEADS))
                held(pool)
                for i, (dst, src) in enumerate(((F_s, "F_s"), (F_p, "F_p"), (Fi_s, "Fi_s"), (Fi_p, "Fi_p"))):
                    pool.dma_start(dst, I[src].rearrange("p (a b) -> p a b", b=dst.shape[-1]) if len(dst.shape) == 3
                                                 else I[src].rearrange("p (a b c) -> p a b c", b=6, c=128)).then_inc(B_const[i].sem, B_const[i].step)
                pool.dma_start(w3[0:65], I["w3"][layer, :, :].rearrange("p (a b) -> p a b", a=4)).then_inc(layer_in2[4].sem, layer_in2[4].step)
                pool.dma_start(dec_abs, I["decay"][layer, :, :].rearrange("o (a b) -> o a b", a=4).to_broadcast([128, 4, 256])).then_inc(layer_in2[5].sem, layer_in2[5].step)
                pool.wait_ge(B_y.sem, B_y.at(layer, HEADS))
                held(pool)
                with pool.Fori(0, HEADS) as h:
                    pool.wait_ge(C["y"].sem, C["y"].at(layer, h))
                    held(pool)
                    pool.dma_start(ctx_k, I["nat_kT"][layer, h, :, :]).then_inc(C["in0"].sem, C["in0"].step)
                    pool.dma_start(ctx_v, I["nat_v"][layer, h, :, :]).then_inc(C["in1"].sem, C["in1"].step)
                    pool.dma_start(bias, I["bias"][layer, h, :, :]).then_inc(C["in2"].sem, C["in2"].step)
                    pool.wait_ge(C["vt"].sem, C["vt"].at(layer, h + 1))
                    held(pool)
                    pool.dma_start(O["nat"][layer, 0, h, :, :], k_p).then_inc(C["kv0"].sem, C["kv0"].step)
                    pool.dma_start(O["nat"][layer, 1, h, :, :], v_t[:, 4, :]).then_inc(C["kv1"].sem, C["kv1"].step)
                    pool.wait_ge(C["kv0"].sem, C["kv0"].at(layer, h + 1))
                    held(pool)
                    pool.wait_ge(C["kv1"].sem, C["kv1"].at(layer, h + 1))
                    held(pool)
                    P.drain().then_inc(C["stored"].sem, C["stored"].step)
                pool.wait_ge(C["y"].sem, C["y"].at(layer, HEADS))
                held(pool)
                pool.dma_start(cosT, I["cos"]).then_inc(rope_in[0].sem, rope_in[0].step)
                pool.dma_start(sinT, I["sin"]).then_inc(rope_in[1].sem, rope_in[1].step)
                with pool.Fori(0, HEADS) as h:
                    pool.wait_ge(Dd["y"].sem, Dd["y"].at(layer, h))
                    held(pool)
                    pool.dma_start(ctx_k, I["diff_kT"][layer, h, :, :]).then_inc(Dd["in0"].sem, Dd["in0"].step)
                    pool.dma_start(ctx_v, I["diff_v"][layer, h, :, :]).then_inc(Dd["in1"].sem, Dd["in1"].step)
                    pool.wait_ge(Dd["vt"].sem, Dd["vt"].at(layer, h + 1))
                    held(pool)
                    pool.dma_start(O["diff"][layer, 0, h, :, :], k_p).then_inc(Dd["kv0"].sem, Dd["kv0"].step)
                    pool.dma_start(O["diff"][layer, 1, h, :, :], v_t[:, 4, :]).then_inc(Dd["kv1"].sem, Dd["kv1"].step)
                    pool.wait_ge(Dd["kv0"].sem, Dd["kv0"].at(layer, h + 1))
                    held(pool)
                    pool.wait_ge(Dd["kv1"].sem, Dd["kv1"].at(layer, h + 1))
                    held(pool)
                    P.drain().then_inc(Dd["stored"].sem, Dd["stored"].step)
                    power(layer, Dd["ss"], h + 1, Dd["rn"], 5)
                pool.wait_ge(Dd["y"].sem, Dd["y"].at(layer, HEADS))
                held(pool)
                pool.dma_start(x_tm, O["x"].rearrange("(t p) d -> p t d", p=128)).then_inc(x_reload.sem, x_reload.step)
                power(layer, y_sq, 1, y_rn, 5)
                pool.wait_ge(x_new.sem, x_new.at(layer, 1))
                held(pool)
                pool.dma_start(O["x"].rearrange("(t p) d -> p t d", p=128), x_tm).then_inc(x_back.sem, x_back.step)
                pool.wait_ge(x_back.sem, x_back.at(layer, 1))
                held(pool)

        @block.tensor
        def _(pe):
            T = nc.tensor
            start(pe)
            pe.wait_ge(consts_in.sem, N_CONST)

            def mm(out, l, r, start=True, stop=True):
                return T.matmul(out, l, r, start=start, stop=stop)

            def tr(out, src):
                return T.transpose(out, src, ident[:, :])

            def product(static, act_hi, act_lo, kts, w0, out, part=None):
                s = static % SPLITS
                pairs = ((w_hi, act_hi), (w_hi, act_lo), (w_lo, act_hi))
                for k in part or range(kts):
                    for j, (w, t) in enumerate(pairs):
                        a, z = (k == 0 and j == 0), (k == kts - 1 and j == 2)
                        mm(out[:, 0:SAMPLE], w[:, s, w0 + k, :], t[:, k, 0:SAMPLE], a, z)
                        last = mm(out[:, SAMPLE:NT], w[:, s, w0 + k, :], t[:, k, SAMPLE:NT], a, z)
                return last

            def project(layer, n, p, static, pstatic, parts=None):
                pe.wait_ge(hi_ready.sem, hi_ready.at(layer, n + 1))
                pe.wait_ge(lo_ready.sem, lo_ready.at(layer, n + 1))
                pe.wait_ge(proj_taken.sem, proj_taken.at(layer, p - 1))
                args = (static, h_hi_v, h_lo_v, KT, 0, psum_a[pstatic % 2])
                if parts is None:
                    product(*args).then_inc(block_done.sem, block_done.step)
                    return None

                def piece(i):
                    last = product(*args, part=range(i * KT // parts, (i + 1) * KT // parts))
                    if i == parts - 1:
                        last.then_inc(block_done.sem, block_done.step)
                return piece

            with pe.Fori(0, DEPTH) as layer:
                pe.wait_ge(cond_ready.sem, 1)
                pe.wait_ge(ytm.sem, ytm.at(layer, 0))
                held(pe)
                with pe.Fori(0, MOD_BLOCKS // 8) as i:
                    for g in range(2):
                        for s in range(4):
                            pe.wait_ge(raw_in[s].sem, raw_in[s].at(layer, i * 2 + (g + 1)))
                            for k in range(KT):
                                last = mm(M[0:2, 512 * g + 128 * s:512 * g + 128 * s + 128], cond[:, 2 * k:2 * k + 2],
                                          raw[:, s, k, :], k == 0, k == KT - 1)
                            last.then_inc(mod_mm.sem, mod_mm.step)
                        pe.wait_ge(mod_row.sem, mod_row.at(layer, i * 2 + (g + 1)))
                        for s in range(4):
                            last = mm(M[:, bass.ds(i * 16 + (1536 + 8 * g + 2 * s), 2)], gate_sg[0:2, g, 128 * s:128 * s + 128], ident[0:2, 0:2])
                pe.drain().then_inc(mod_t.sem, mod_t.step)
                for i in (2, 3):
                    pe.wait_ge(layer_in2[i].sem, layer_in2[i].at(layer, 1))
                pe.wait_ge(mod_ready.sem, mod_ready.at(layer, 1))
                pe.wait_ge(x_n.sem, x_n.at(layer, 1))
                for k in range(KT):
                    at = 1024 * (k % 2)
                    if k >= 2:
                        pe.wait_ge(ht_raw.sem, ht_raw.at(layer, k - 1))
                    for t in range(TILES):
                        last = tr(M[:, at + 128 * t:at + 128 * (t + 1)], x_n_v[:, t, 128 * k:128 * (k + 1)])
                    last.then_inc(xt_mm.sem, xt_mm.step)
                def hidden(j):
                    src = feat[0:HY_EMB, :] if j == 0 else hid_tmp[0:HY_FF, 0, :]
                    w = hy_w12[0:HY_EMB, 0:HY_FF] if j == 0 else hy_w12[0:HY_FF, HY_FF:2 * HY_FF]
                    mm(M[0:HY_FF, 0:SAMPLE], w, src[:, 0:SAMPLE])
                    mm(M[0:HY_FF, SAMPLE:NT], w, src[:, SAMPLE:NT]).then_inc(hid_mm.sem, hid_mm.step)

                pe.wait_ge(h_ready.sem, h_ready.at(layer, KT))
                held(pe)
                hidden(0)
                pe.wait_ge(ab_split.sem, ab_split.at(layer, 1))
                for k in range(KT):
                    cols = slice(16 * k, 16 * k + 16)
                    for j, (w, x) in enumerate(((ab_w_hi, h_hi_v), (ab_w_hi, h_lo_v), (ab_w_lo, h_hi_v))):
                        a, z = k == 0 and j == 0, k == KT - 1 and j == 2
                        mm(M[0:16, 1024:1024 + SAMPLE], w[:, cols], x[:, k, 0:SAMPLE], a, z)
                        last = mm(M[0:16, 1024 + SAMPLE:1024 + NT], w[:, cols], x[:, k, SAMPLE:NT], a, z)
                last.then_inc(ab_mm.sem, ab_mm.step)
                piece = project(layer, 0, 0, 0, 0, 4)
                piece(0)
                pe.wait_ge(ab_row.sem, ab_row.at(layer, 1))
                for t in range(TILES):
                    last = mm(M[:, AB_AT + 16 * t:AB_AT + 16 * t + 16], tmp640[0:16, 128 * t:128 * t + 128], ident[0:16, 0:16])
                last.then_inc(ab_t.sem, ab_t.step)
                piece(1)
                piece(2)
                pe.wait_ge(hid_sin.sem, hid_sin.at(layer, 1))
                held(pe)
                hidden(1)
                piece(3)
                pe.wait_ge(ab_v.sem, ab_v.at(layer, 2))
                g = ab_s[:, 0:40]
                for d in range(2):
                    mm(M[:, GC_AT + 20 * d:GC_AT + 20 * d + 20], tri[:, d, :], ab_s[:, 20 * d:20 * d + 20])
                mm(M[:, GC_AT + 64:GC_AT + 104], ones[:, :], g).then_inc(gc_mm.sem, gc_mm.step)
                project(layer, 1, 1, 1, 1)

                def unit(b, h, j, parts=None):
                    return project(layer, h * UNIT + (base(b) + j), h * UNIT + (pbase(b) + j), j, j, parts)

                pe.wait_ge(ab_done.sem, ab_done.at(layer, 1))
                held(pe)
                with pe.Fori(0, HEADS) as h:
                    unit(0, h, 2)
                    unit(0, h, 3)
                    pe.wait_ge(A_y.sem, A_y.at(layer, h))
                    pe.wait_ge(A_qkv.sem, A_qkv.at(layer, h + 1))
                    for w in range(3):
                        for t in range(TILES):
                            col = 512 * w + 128 * t if t < 4 else 1536 + 128 * w
                            last = tr(M[:, col:col + 128], A_c[:, w, CONV_TILE[t]:CONV_TILE[t] + 128])
                    last.then_inc(A_tr.sem, A_tr.step)
                    piece = unit(0, h, 4, 4)
                    piece(0)
                    pe.wait_ge(A_tm.sem, A_tm.at(layer, h + 1))
                    pe.wait_ge(A_g1.sem, A_g1.at(layer, h + 1))
                    for d in range(2):
                        if d:
                            pe.wait_ge(A_dec.sem, A_dec.at(layer, h * 2 + 1))
                        mm(M[:, 0:512], tri[:, d, :], g1[:, d, 0:4, :])
                        mm(M[:, 512:640], tri[:, d, :], g1[:, d, 4, :])
                        for t in range(TILES):
                            last = mm(M[:, 1024 + 128 * t:1152 + 128 * t], g1[:, d, t, :], tri[:, d, :])
                        last.then_inc(A_rel.sem, A_rel.step)
                        piece(d + 1)
                    pe.wait_ge(A_kqn.sem, A_kqn.at(layer, h + 1))
                    pe.wait_ge(A_dec.sem, A_dec.at(layer, h * 2 + 2))
                    for t in range(TILES):
                        for j in range(2):
                            last = tr(M[:, 256 * t + 128 * j:256 * t + 128 * j + 128], kqn[:, t, j, :])
                    last.then_inc(A_kqt_mm.sem, A_kqt_mm.step)
                    piece(3)
                    pe.wait_ge(A_kqt.sem, A_kqt.at(layer, h + 1))
                    for t in range(TILES):
                        last = mm(M[:, 256 * t:256 * t + 256], kqT[:, t, 0, :], kqT[:, t, :, :])
                    last.then_inc(A_gram.sem, A_gram.step)
                    pe.wait_ge(A_x0.sem, A_x0.at(layer, h + 1))
                    pe.wait_ge(A_lat.sem, A_lat.at(layer, h + 1))
                    held(pe)
                    groups = ([(0, t) for t in range(4)], [(1, t) for t in range(4)], [(0, 4), (1, 4)])
                    def level_products(e, kind="inner"):
                        if kind != "first":
                            for gi, grp in enumerate(groups):
                                pe.wait_ge(A_x.sem, A_x.at(layer, e + (gi + 1 - 3)))
                                for j, (d, t) in enumerate(grp):
                                    last = mm(M[:, 512 * gi + 128 * j:512 * gi + 128 * j + 128], dec[:, d, t, :], XT[:, d, t, :])
                                last.then_inc(A_q.sem, A_q.step)
                        for gi, grp in enumerate(groups):
                            pe.wait_ge(A_qn.sem, A_qn.at(layer, e + (1, 3, 3)[gi]))
                            if gi == 2 and kind == "inner":
                                pe.wait_ge(A_x.sem, A_x.at(layer, e + 1))
                            a0, b0 = ((1536, 0), (512, 1024), (1536, 1792))[gi]
                            if kind == "inner":
                                for j, (d, t) in enumerate(grp):
                                    mm(M[:, a0 + 128 * j:a0 + 128 * j + 128], Qn[:, d, t, :], X[:, d, t, :])
                            for j, (d, t) in enumerate(grp):
                                o = M[:, b0 + 128 * j:b0 + 128 * j + 128]
                                last = tr(o, Qn[:, d, t, :]) if kind == "first" else mm(o, X[:, d, t, :], Qn[:, d, t, :])
                            last.then_inc(A_d.sem, A_d.step)

                    level_products(h * (3 * LEVELS), "first")
                    pe.wait_ge(A_x.sem, A_x.at(layer, h * (3 * LEVELS) + 1))
                    held(pe)
                    with pe.Fori(1, LEVELS - 1) as lv:
                        level_products(h * (3 * LEVELS) + lv * 3)
                    level_products(h * (3 * LEVELS) + 3 * (LEVELS - 1), "last")
                    pe.wait_ge(A_x.sem, A_x.at(layer, h * (3 * LEVELS) + 3 * LEVELS))
                    for d in range(2):
                        for t in range(4):
                            last = mm(M[:, 512 * d + 128 * t:512 * d + 128 * t + 128], Rk[:, d, t, :], XT[:, d, t, :])
                    last.then_inc(A_wt_mm.sem, A_wt_mm.step)
                    pe.wait_ge(A_s_in.sem, A_s_in.at(layer, h + 1))
                    pe.wait_ge(A_wt.sem, A_wt.at(layer, h + 1))
                    piece = unit(0, h, 5, 4)
                    for n in range(5):
                        ts = (n, 3 - n) if n < 4 else (4, 4)
                        if n:
                            pe.wait_ge(A_su.sem, A_su.at(layer, h * 5 + n))
                        for d, t in enumerate(ts):
                            o = M[:, 1024 + 128 * d:1152 + 128 * d]
                            last = mm(o, XT[:, d, t, :], Rv[:, d, t, :], True, n == 4)
                            if n < 4:
                                mm(o, Qn[:, d, t, :], S[:, d, :], False, True)
                        if n < 4:
                            for d, t in enumerate(ts):
                                last = mm(M[:, 1280 + 128 * d:1408 + 128 * d], kqT[:, t, 1, :], S[:, d, :])
                        last.then_inc(A_va.sem, A_va.step)
                        pe.wait_ge(A_vn.sem, A_vn.at(layer, h * 5 + (n + 1)))
                        for d, t in enumerate(ts):
                            mm(M[:, 1536 + 128 * d:1664 + 128 * d], decT[:, d, t, :], vn[:, d, :])
                        for d, t in enumerate(ts):
                            last = mm(M[:, 1792 + 128 * d:1920 + 128 * d], kd[:, d, t, :], vn[:, d, :])
                        last.then_inc(A_sb.sem, A_sb.step)
                        if n < 4:
                            piece(n)
                    pe.wait_ge(A_o.sem, A_o.at(layer, h + 1))
                    for t in range(TILES):
                        last = tr(M[:, 128 * t:128 * t + 128], o_tm[:, t, :])
                    last.then_inc(A_ot.sem, A_ot.step)

                def merge(b, y_sig):
                    pe.wait_ge(y_sig.sem, y_sig.at(layer, HEADS))
                    held(pe)

                    def pair(i, q, ahead=True):
                        n = i * 6 + (base(b) + HEADS * UNIT + 3 * q)
                        p = i * 4 + (pbase(b) + HEADS * UNIT + 2 * q)
                        step = i * 4 + (8 * b + 2 * q)
                        pe.wait_ge(hi_ready.sem, hi_ready.at(layer, n + 3))
                        pe.wait_ge(lo_ready.sem, lo_ready.at(layer, n + 3))
                        for s in range(2):
                            pe.wait_ge(merged_step.sem, merged_step.at(layer, step + s - 1))
                            last = product(q, y_hi, y_lo, HEADS, HEADS * s, M[:, 1024 * s:1024 * s + NT])
                            last.then_inc(*((br_mm.sem, br_mm.step) if s == 0 else (block_done.sem, block_done.step)))
                        if ahead:
                            project(layer, n + 3, p + 2, q + 1, 0)
                            project(layer, n + 4, p + 3, q + 2, 1)

                    if b < 3:
                        with pe.Fori(0, 2) as i:
                            for q in range(2):
                                pair(i, q)
                    else:
                        for q in range(4):
                            pair(q // 2, q % 2, q < 3)

                merge(0, A_y)

                def dft(src_s, src_p, out_w, at):
                    for f in range(6):
                        o = at + (f + f // 3) * out_w
                        for t in range(4):
                            mm(M[:, o:o + out_w], F_s[:, t, f, :], src_s(t), t == 0, t == 3)
                    for j in range(2):
                        o = at + (3 + 4 * j) * out_w
                        last = mm(M[:, o:o + out_w], F_p[:, j, :], src_p)
                    return last

                for i in range(4):
                    pe.wait_ge(B_const[i].sem, B_const[i].at(layer, 1))
                pe.wait_ge(layer_in2[4].sem, layer_in2[4].at(layer, 1))
                held(pe)
                with pe.Fori(0, HEADS) as h:
                    unit(1, h, 2)
                    pe.wait_ge(B_y.sem, B_y.at(layer, h))
                    pe.wait_ge(merged_step.sem, merged_step.at(layer, 8))
                    for t in range(TILES):
                        last = mm(M[:, 256 * t:256 * t + 256], hid_t[:, 128 * t:128 * t + 128], w3[0:65, h, :])
                    last.then_inc(B_filt_mm.sem, B_filt_mm.step)
                    piece = unit(1, h, 3, 2)
                    piece(0)
                    pe.wait_ge(B_filt.sem, B_filt.at(layer, h + 1))
                    dft(lambda t: filt[:, t, :], filt[:, 4, :], 256, 0).then_inc(B_h_mm.sem, B_h_mm.step)
                    piece(1)
                    pe.wait_ge(B_h.sem, B_h.at(layer, h + 1))
                    for r in range(2):
                        if r == 0:
                            pe.wait_ge(B_conv.sem, B_conv.at(layer, h * 3 + 1))
                            src = [B_c[:, 0, x:x + 128] for x in CONV_TILE]
                        else:
                            pe.wait_ge(B_z1.sem, B_z1.at(layer, h + 1))
                            src = [z1[:, 128 * t:128 * t + 128] for t in range(TILES)]
                        for t in range(TILES):
                            last = tr(M[:, 1024 + 128 * t:1152 + 128 * t], src[t])
                        last.then_inc(B_tr.sem, B_tr.step)
                        pe.wait_ge(B_vt.sem, B_vt.at(layer, h * 2 + (r + 1)))
                        dft(lambda t: vt_b[:, t, :], vt_b[:, 4, :], 128, 1024).then_inc(B_u.sem, B_u.step)
                        unit(1, h, 4 + r)
                        pe.wait_ge(B_y0.sem, B_y0.at(layer, h * 2 + (r + 1)))
                        for f in range(6):
                            mm(M[:, 0:512], Yf[:, f + f // 3, :], Fi_s[:, f, :], f == 0, f == 5)
                        for j in range(2):
                            last = mm(M[:, 512:640], Yf[:, 3 + 4 * j, :], Fi_p[:, j, :], j == 0, j == 1)
                        last.then_inc(B_inv.sem, B_inv.step)
                merge(1, B_y)

                with pe.Fori(0, HEADS) as h:
                    unit(2, h, 2)
                    pe.wait_ge(C["y"].sem, C["y"].at(layer, h))
                    pe.wait_ge(merged_step.sem, merged_step.at(layer, 16))
                    pe.wait_ge(proj_taken.sem, proj_taken.at(layer, h * UNIT + (pbase(2) + 3)))
                    for t in range(TILES):
                        tr(M[:, 1024 + 128 * t:1152 + 128 * t], vT[:, 128 * t:128 * t + 128])
                    tr(M[:, 1664:1792], kT[:, SAMPLE:NT]).then_inc(C["tr"].sem, C["tr"].step)
                    for i in range(3):
                        pe.wait_ge(C[f"in{i}"].sem, C[f"in{i}"].at(layer, h + 1))

                    def scores(m):
                        if m:
                            pe.wait_ge(C["mx"].sem, C["mx"].at(layer, h * 5 + m))
                        q = qT[:, 128 * m:128 * m + 128]
                        if m < 4:
                            mm(M[:, 0:512], q, kT[:, 0:SAMPLE])
                            mm(M[:, 512:640], q, ctx_k).then_inc(C["s"].sem, C["s"].step)
                        else:
                            mm(M[:, 512:640], q, kT[:, SAMPLE:NT]).then_inc(C["s"].sem, C["s"].step)

                    scores(0)
                    unit(2, h, 3)
                    pe.wait_ge(C["vt"].sem, C["vt"].at(layer, h + 1))
                    for m in range(5):
                        if m < 4:
                            scores(m + 1)
                        if m < 4:
                            if m % 2 == 0:
                                piece = unit(2, h, 4 + m // 2, 2)
                            piece(m % 2)
                        pe.wait_ge(C["pn"].sem, C["pn"].at(layer, h * 5 + (m + 1)))
                        if m:
                            pe.wait_ge(C["pt"].sem, C["pt"].at(layer, h * 5 + m))
                        for t in range(0 if m < 4 else 4, TILES):
                            last = tr(M[:, 1024 + 128 * t:1152 + 128 * t], s_buf[:, m % 2, 128 * t:128 * t + 128])
                        last.then_inc(C["pt_mm"].sem, C["pt_mm"].step)
                    pe.wait_ge(C["pt"].sem, C["pt"].at(layer, h * 5 + 5))
                    pe.wait_ge(C["mx"].sem, C["mx"].at(layer, h * 5 + 5))
                    for t in range(TILES):
                        mm(M[:, 0:512], v_t[:, t, :] if t < 4 else ctx_v, PT[:, t, :], t == 0, t == 4)
                    mm(M[:, 512:640], v_t[:, 4, :], PTp).then_inc(C["pv"].sem, C["pv"].step)
                merge(2, C["y"])

                with pe.Fori(0, HEADS) as h:
                    unit(3, h, 2)
                    pe.wait_ge(Dd["y"].sem, Dd["y"].at(layer, h))
                    pe.wait_ge(merged_step.sem, merged_step.at(layer, 24))
                    pe.wait_ge(proj_taken.sem, proj_taken.at(layer, h * UNIT + (pbase(3) + 3)))
                    mm(M[:, 0:512], swap[:, :], qT[:, 0:SAMPLE])
                    mm(M[:, 512:1024], swap[:, :], kT[:, 0:SAMPLE])
                    for t in range(TILES):
                        tr(M[:, 1024 + 128 * t:1152 + 128 * t], vT[:, 128 * t:128 * t + 128])
                    tr(M[:, 1664:1792], kT[:, SAMPLE:NT]).then_inc(Dd["tr"].sem, Dd["tr"].step)
                    for i in range(2):
                        pe.wait_ge(Dd[f"in{i}"].sem, Dd[f"in{i}"].at(layer, h + 1))
                    unit(3, h, 3)
                    pe.wait_ge(proj_taken.sem, proj_taken.at(layer, h * UNIT + (pbase(3) + 4)))
                    pe.wait_ge(Dd["rope"].sem, Dd["rope"].at(layer, h + 1))
                    pe.wait_ge(Dd["vt"].sem, Dd["vt"].at(layer, h + 1))

                    def scores(m):
                        if m:
                            pe.wait_ge(Dd["p"].sem, Dd["p"].at(layer, h * 5 + m))
                        for i in range(2):
                            rows = slice(64 * i, 64 * i + 64)
                            q = qT[rows, 128 * m:128 * m + 128]
                            if m < 4:
                                mm(D_scores[i][:, 0:SAMPLE], q, kT[rows, 0:SAMPLE])
                            last = mm(D_scores[i][:, SAMPLE:NT], q, ctx_k[rows, :] if m < 4 else kT[rows, SAMPLE:NT])
                        last.then_inc(Dd["s"].sem, Dd["s"].step)

                    scores(0)
                    piece = unit(3, h, 4, 4)
                    for m in range(5):
                        if m < 4:
                            scores(m + 1)
                            piece(m)
                        pe.wait_ge(Dd["pn"].sem, Dd["pn"].at(layer, h * 5 + (m + 1)))
                        if m:
                            pe.wait_ge(Dd["o"].sem, Dd["o"].at(layer, h * 5 + m))
                        first = 0 if m < 4 else 4
                        for t in range(first, TILES):
                            last = tr(M[:, 128 * t:128 * t + 128], s_buf[:, 2 * (m % 2), 128 * t:128 * t + 128])
                        last.then_inc(Dd["pt_mm"].sem, Dd["pt_mm"].step)
                        pe.wait_ge(Dd["pt"].sem, Dd["pt"].at(layer, h * 5 + (m + 1)))
                        for t in range(first, TILES):
                            v = ctx_v if (t == 4 and m < 4) else v_t[:, t, :]
                            last = mm(M[:, NT:NT + 128], PT[:, t, 0:128], v, t == first, t == 4)
                        last.then_inc(Dd["pv"].sem, Dd["pv"].step)
                    pe.wait_ge(Dd["p"].sem, Dd["p"].at(layer, h * 5 + 5))
                    unit(3, h, 5)
                    pe.wait_ge(Dd["on"].sem, Dd["on"].at(layer, h + 1))
                    for t in range(TILES):
                        last = tr(M[:, 128 * t:128 * t + 128], d_o[:, t, :])
                    last.then_inc(Dd["ot"].sem, Dd["ot"].step)
                merge(3, Dd["y"])

                def back(n):
                    pe.wait_ge(proj_taken.sem, proj_taken.at(layer, pbase(4) + n + 1))
                    if n == 0:
                        pe.wait_ge(merged_step.sem, merged_step.at(layer, 32))
                    if n >= 2:
                        pe.wait_ge(ytm.sem, ytm.at(layer, n - 1))
                    for t in range(TILES):
                        last = tr(M[:, 1024 * (n % 2) + 128 * t:1024 * (n % 2) + 128 * t + 128],
                                  y_cm[:, n % 2, 128 * t:128 * t + 128])
                    last.then_inc(yt_mm.sem, yt_mm.step)

                pe.wait_ge(gate_diag.sem, gate_diag.at(layer, 1))
                pe.wait_ge(proj_taken.sem, proj_taken.at(layer, pbase(4)))
                for n in range(4):
                    last = mm(psum_a[n // 2][:, 512 * (n % 2):512 * (n % 2) + 512], ones[:, :], diag[:, 4 * n:4 * n + 4, :])
                last.then_inc(gate_mm.sem, gate_mm.step)
                pe.wait_ge(m_split.sem, m_split.at(layer, KT))
                pe.wait_ge(gate_bc.sem, gate_bc.at(layer, 1))
                for n in range(OUT_BLOCKS):
                    project(layer, base(4) + n, pbase(4) + n, n, n)
                    if n:
                        back(n - 1)
                back(OUT_BLOCKS - 1)

        @block.scalar
        def _(act):
            A = nc.scalar
            start(act)
            act.wait_ge(consts_in.sem, N_CONST)
            A.activation(cond[:, :], cond_raw[:, :], ACT.Silu).then_inc(cond_ready.sem, cond_ready.step)

            def copy(out, x, scale=1.0):
                return A.activation(out, x, ACT.Copy, scale=scale)

            def split_hi(layer, n, static):
                r, s = static % RING, static % SPLITS
                act.wait_ge(raw_in[r].sem, raw_in[r].at(layer, raw_uses(n)))
                act.wait_ge(block_done.sem, block_done.at(layer, n - SPLITS + 1))
                copy(w_hi[:, s, :, :], raw[:, r, :, :]).then_inc(hi_ready.sem, hi_ready.step)

            def taken(instruction):
                instruction.then_inc(proj_taken.sem, proj_taken.step)

            act.wait_ge(x_in.sem, 2 * x_in.step)
            with act.Fori(0, DEPTH) as layer:
                def rows(g):
                    act.wait_ge(mod_mm.sem, mod_mm.at(layer, 4 * g + 4))
                    copy(gate_sg[0:2, g % 2, 0:512], M[0:2, 512 * (g % 2):512 * (g % 2) + 512]).then_inc(mod_row.sem, mod_row.step)

                for g in range(3):
                    rows(g)
                act.wait_ge(x_new.sem, x_new.at(layer, 0))
                for t in range(TILES):
                    last = A.activation(x_n_v[:, t, :], x_tm[:, t, :], ACT.Square, accum_out=stat[:, t:t + 1])
                last.then_inc(x_ss.sem, x_ss.step)
                for g in range(3, MOD_BLOCKS // 4):
                    rows(g)
                act.wait_ge(lam_v.sem, lam_v.at(layer, 1))
                A.activation(lam_s[:, 2:4], lam_s[:, 0:2], ACT.Exp).then_inc(lam_e.sem, lam_e.step)
                act.wait_ge(mod_ready.sem, mod_ready.at(layer, 1))
                for k in range(KT):
                    at = 1024 * (k % 2)
                    act.wait_ge(xt_mm.sem, xt_mm.at(layer, k + 1))
                    if k >= 2:
                        act.wait_ge(h_ready.sem, h_ready.at(layer, k - 1))
                    A.activation(gate_sg[:, k % 2, 0:SAMPLE], M[:, at:at + SAMPLE], ACT.Identity,
                                 scale=g_scale[:, k, 0:1], bias=mod[:, k, 0:1])
                    A.activation(gate_sg[:, k % 2, SAMPLE:NT], M[:, at + SAMPLE:at + NT], ACT.Identity,
                                           scale=g_scale[:, k, 1:2], bias=mod[:, k, 1:2]).then_inc(ht_raw.sem, ht_raw.step)
                    if k in (2, 4):
                        split_hi(layer, k // 2 - 1, k // 2 - 1)
                def sine(j):
                    act.wait_ge(hid_arg.sem, hid_arg.at(layer, j + 1))
                    out = hid_tmp[0:HY_FF, 0, :] if j == 0 else hid_t[0:HY_FF, :]
                    A.activation(out, hid_tmp[0:HY_FF, 0, :], ACT.Sin).then_inc(hid_sin.sem, hid_sin.step)

                sine(0)
                ab = lambda i: ab_s[:, 40 * i:40 * i + 40]
                act.wait_ge(ab_v.sem, ab_v.at(layer, 1))
                A.activation(ab(9), ab(7), ACT.Exp, scale=-1.0)
                A.activation(exp_alog[:, :], vecs[:, layer, V_ALOG:V_ALOG + 8], ACT.Exp)
                A.activation(ab(8), ab(8), ACT.Exp, scale=-1.0)
                A.drain()
                A.activation(ab(8), ab(8), ACT.Ln, bias=1.0).then_inc(ab_l.sem, ab_l.step)
                sine(1)
                act.wait_ge(ab_v.sem, ab_v.at(layer, 3))
                A.activation(ab(2), ab(8), ACT.Exp)
                A.activation(ab(3), ab(3), ACT.Exp)
                A.activation(ab(4), ab(7), ACT.Exp).then_inc(gc_e.sem, gc_e.step)
                split_hi(layer, 2, 2)
                split_hi(layer, 3, 3)

                act.wait_ge(pad_zero.sem, pad_zero.at(layer, 1))

                def to_pad(conv, h, j, p):
                    act.wait_ge(conv.sem, conv.at(layer, h * 3 + j))
                    copy(pad[:, 1:1 + SAMPLE], p[:, 0:SAMPLE])
                    taken(copy(pad[:, 2 + SAMPLE:2 + NT], p[:, SAMPLE:NT]))

                def unit_hi(b, h, j):
                    split_hi(layer, h * UNIT + (base(b) + j), j)

                def head_block(b, h, j):
                    if j >= 2:
                        unit_hi(b, h, j + 2)
                    act.wait_ge(block_done.sem, block_done.at(layer, h * UNIT + (base(b) + j + 1)))
                    return psum_a[j % 2]

                with act.Fori(0, HEADS) as h:
                    for j in range(3):
                        to_pad(A_conv, h, j, head_block(0, h, j))
                    act.wait_ge(A_conv.sem, A_conv.at(layer, h * 3 + 3))
                    A.activation(A_c, A_c, ACT.Silu).then_inc(A_qkv.sem, A_qkv.step)
                    p = head_block(0, h, 3)
                    act.wait_ge(A_y.sem, A_y.at(layer, h))
                    taken(A.activation(A_zb, p[:, 0:NT], ACT.Silu))
                    act.wait_ge(A_tr.sem, A_tr.at(layer, h + 1))
                    copy(A_tmv[:, :, 0:4, :], M[:, 0:1536].rearrange("p (w t c) -> p w t c", w=3, t=4))
                    copy(A_tmv[:, :, 4, :], M[:, 1536:1920].rearrange("p (w c) -> p w c", w=3)).then_inc(A_tm.sem, A_tm.step)
                    for d in range(2):
                        act.wait_ge(A_rel.sem, A_rel.at(layer, h * 2 + (d + 1)))
                        A.activation(dec[:, d, :, :], M[:, 0:NT].rearrange("p (t c) -> p t c", t=5), ACT.Exp)
                        A.activation(decT[:, d, :, :], M[:, 1024:1024 + NT].rearrange("p (t c) -> p t c", t=5), ACT.Exp).then_inc(A_dec.sem, A_dec.step)
                    act.wait_ge(A_kqt_mm.sem, A_kqt_mm.at(layer, h + 1))
                    copy(kqT, M[:, 0:1280].rearrange("p (t j c) -> p t j c", t=5, j=2)).then_inc(A_kqt.sem, A_kqt.step)
                    unit_hi(0, h, 6)
                    act.wait_ge(A_lat.sem, A_lat.at(layer, h + 1))
                    groups = ((slice(0, 1), slice(0, 4)), (slice(1, 2), slice(0, 4)), (slice(0, 2), slice(4, 5)))
                    for d, t in groups:
                        copy(Qn[:, d, t, :], dec[:, d, t, :], -1.0).then_inc(A_qn.sem, A_qn.step)
                    with act.Fori(1, LEVELS) as lv:
                        for gi, (d, t) in enumerate(groups):
                            act.wait_ge(A_q.sem, A_q.at(layer, h * (3 * (LEVELS - 1)) + lv * 3 + (gi - 2)))
                            src = M[:, 512 * gi:512 * gi + (512 if gi < 2 else 256)].rearrange("p (d t c) -> p d t c", c=128, d=1 if gi < 2 else 2)
                            copy(Qn[:, d, t, :], src, -1.0).then_inc(A_qn.sem, A_qn.step)
                    act.wait_ge(A_wt_mm.sem, A_wt_mm.at(layer, h + 1))
                    copy(Qn[:, :, 0:4, :], M[:, 0:1024].rearrange("p (d t c) -> p d t c", d=2, t=4), -1.0).then_inc(A_wt.sem, A_wt.step)
                    for n in range(5):
                        act.wait_ge(A_va.sem, A_va.at(layer, h * 5 + (n + 1)))
                        copy(vn, M[:, 1024:1280].rearrange("p (d c) -> p d c", d=2)).then_inc(A_vn.sem, A_vn.step)
                    unit_hi(0, h, 7)

                def merge(b):
                    def pair(i, q, ahead=True):
                        n = i * 6 + (base(b) + HEADS * UNIT + 3 * q)
                        step = i * 4 + (8 * b + 2 * q)
                        for s in range(2):
                            act.wait_ge(block_done.sem, block_done.at(layer, n + s + 1))
                            act.wait_ge(merged_step.sem, merged_step.at(layer, step + s - 1))
                            taken(A.activation(gate_sg[:, s, :], psum_a[s][:, 0:NT], ACT.Sigmoid,
                                               bias=vecs[:, layer, bass.ds(i * 4 + (V_BMERGE + 8 * b + 2 * q + s), 1)]))
                        for j in range(4, 7 if ahead else 5):
                            split_hi(layer, n + j, q + j)

                    if b == 1:
                        act.wait_ge(B_y.sem, B_y.at(layer, HEADS))
                    if b < 3:
                        with act.Fori(0, 2) as i:
                            for q in range(2):
                                pair(i, q)
                    else:
                        for q in range(4):
                            pair(q // 2, q % 2, q < 3)

                merge(0)

                act.wait_ge(dec_ready_l.sem, dec_ready_l.at(layer, 1))
                with act.Fori(0, HEADS) as h:
                    to_pad(B_conv, h, 0, head_block(1, h, 0))
                    act.wait_ge(B_y.sem, B_y.at(layer, h))
                    for t in range(TILES):
                        last = A.activation(win[:, t, :], dec_abs[:, h, :], ACT.Exp, scale=dist[:, t:t + 1])
                    last.then_inc(B_win.sem, B_win.step)
                    for j in range(1, 3):
                        to_pad(B_conv, h, j, head_block(1, h, j))
                    act.wait_ge(B_h_mm.sem, B_h_mm.at(layer, h + 1))
                    copy(Hf, M[:, 0:2048].rearrange("p (f o c) -> p f o c", f=8, o=2)).then_inc(B_h.sem, B_h.step)
                    p = head_block(1, h, 3)
                    for r in range(2):
                        act.wait_ge(B_tr.sem, B_tr.at(layer, h * 2 + (r + 1)))
                        copy(vt_b, M[:, 1024:1664].rearrange("p (t c) -> p t c", t=5)).then_inc(B_vt.sem, B_vt.step)
                        if r == 0:
                            A.activation(B_gb[:, 0:SAMPLE + 1], p[:, 0:SAMPLE + 1], ACT.Silu)
                            A.drain()
                            taken(A.activation(B_gb[:, SAMPLE + 1:SP1], p[:, SAMPLE:NT], ACT.Silu))
                        unit_hi(1, h, 6 + r)
                merge(1)

                def evacuate(b, X_, h):
                    for j, dst in enumerate((qT, kT, vT)):
                        taken(copy(dst, head_block(b, h, j)[:, 0:NT], (128.0 if b == 2 else 64.0) ** -0.5 if j == 0 else 1.0))
                    act.wait_ge(X_["tr"].sem, X_["tr"].at(layer, h + 1))
                    act.wait_ge(X_["stored"].sem, X_["stored"].at(layer, h))
                    copy(v_t, M[:, 1024:1664].rearrange("p (t c) -> p t c", t=5))
                    copy(k_p, M[:, 1664:1792]).then_inc(X_["vt"].sem, X_["vt"].step)

                def gate(b, X_, h):
                    p = head_block(b, h, 3)
                    act.wait_ge(X_["y"].sem, X_["y"].at(layer, h))
                    taken(A.activation(gT, p[:, 0:NT], ACT.Silu))

                with act.Fori(0, HEADS) as h:
                    evacuate(2, C, h)

                    def probs(m):
                        act.wait_ge(C["mx"].sem, C["mx"].at(layer, h * 5 + (m + 1)))
                        cols = slice(0 if m < 4 else SAMPLE, NT)
                        A.activation(s_buf[:, m % 2, cols], s_buf[:, m % 2, cols], ACT.Exp, bias=stat[:, m:m + 1],
                                               accum_out=stat[:, 8 + m:9 + m]).then_inc(C["p"].sem, C["p"].step)

                    probs(0)
                    gate(2, C, h)
                    for m in range(5):
                        if m < 4:
                            probs(m + 1)
                        act.wait_ge(C["pt_mm"].sem, C["pt_mm"].at(layer, h * 5 + (m + 1)))
                        if m < 4:
                            copy(PT[:, :, 128 * m:128 * m + 128], M[:, 1024:1664].rearrange("p (t c) -> p t c", t=5)).then_inc(C["pt"].sem, C["pt"].step)
                        else:
                            copy(PTp, M[:, 1536:1664]).then_inc(C["pt"].sem, C["pt"].step)
                        if m in (1, 3):
                            unit_hi(2, h, 6 + m // 2)
                merge(2)
                act.wait_ge(C["stored"].sem, C["stored"].at(layer, HEADS))
                with act.Fori(0, HEADS) as h:
                    evacuate(3, Dd, h)
                    gate(3, Dd, h)

                    def probs(m):
                        if m >= 2:
                            act.wait_ge(Dd["pt_mm"].sem, Dd["pt_mm"].at(layer, h * 5 + (m - 1)))
                        cols = slice(0 if m < 4 else SAMPLE, NT)
                        for i in range(2):
                            act.wait_ge(Dd["mx"].sem, Dd["mx"].at(layer, h * 10 + (2 * m + i + 1)))
                            last = A.activation(s_buf[:, 2 * (m % 2) + i, cols], D_scores[i][:, cols], ACT.Exp,
                                                bias=stat[:, 2 * m + i:2 * m + i + 1], accum_out=stat[:, 16 + 2 * m + i:17 + 2 * m + i])
                        last.then_inc(Dd["p"].sem, Dd["p"].step)

                    probs(0)
                    for m in range(5):
                        act.wait_ge(Dd["pt_mm"].sem, Dd["pt_mm"].at(layer, h * 5 + (m + 1)))
                        if m:
                            act.wait_ge(Dd["pv"].sem, Dd["pv"].at(layer, h * 5 + m))
                        f = 0 if m < 4 else 4
                        copy(PT[:, f:TILES, 0:128], M[:, 128 * f:NT].rearrange("p (t c) -> p t c", c=128)).then_inc(Dd["pt"].sem, Dd["pt"].step)
                        if m < 4:
                            probs(m + 1)
                    unit_hi(3, h, 6)
                    unit_hi(3, h, 7)
                merge(3)

                act.wait_ge(gate_mm.sem, gate_mm.at(layer, 1))
                copy(gate_b[:, 0, :], psum_a[0][:, :])
                copy(gate_b[:, 1, :], psum_a[1][:, :]).then_inc(gate_bc.sem, gate_bc.step)
                for n in range(OUT_BLOCKS):
                    act.wait_ge(block_done.sem, block_done.at(layer, base(4) + n + 1))
                    if n >= 2:
                        act.wait_ge(yt_mm.sem, yt_mm.at(layer, n - 1))
                    taken(copy(y_cm[:, n % 2, :], psum_a[n % 2][:, 0:NT]))
                    if n < OUT_BLOCKS - 2:
                        split_hi(layer, base(4) + n + 2, n + 2)
                act.wait_ge(ytm.sem, ytm.at(layer, OUT_BLOCKS))
                held(act)
                for t in range(TILES):
                    A.drain()
                    last = A.activation(psum_a[0][:, :], y_tm[:, t, :], ACT.Square, accum_out=stat[:, t:t + 1])
                last.then_inc(y_ss.sem, y_ss.step)

        @block.vector
        def _(dve):
            V = nc.vector
            V.memset(hid_t[64:65, :], 1.0)
            start(dve)
            dve.wait_ge(consts_in.sem, N_CONST)
            V.tensor_copy(level_t[:, :], level_in).then_inc(level_cast.sem, level_cast.step)

            def tt(out, a_, b_, op):
                return V.tensor_tensor(out, a_, b_, op)

            def mul(out, a_, b_):
                return tt(out, a_, b_, ALU.mult)

            def add(out, a_, b_):
                return tt(out, a_, b_, ALU.add)

            def fence():
                held(dve)
                dve.drain()

            def over(v, *shape):
                return v.to_broadcast([128, *shape])

            def per_tile(cols):
                return over(cols.unsqueeze(2), TILES, 128)

            def all_tiles(mask):
                return over(mask.unsqueeze(1), TILES, 128)

            def split_lo(layer, n, static):
                r, s = static % RING, static % SPLITS
                dve.wait_ge(raw_in[r].sem, raw_in[r].at(layer, raw_uses(n)))
                dve.wait_ge(hi_ready.sem, hi_ready.at(layer, n + 1))
                tt(w_lo[:, s, :, :], raw[:, r, :, :], w_hi[:, s, :, :].bitcast(f32), ALU.subtract).then_inc(lo_ready.sem, lo_ready.step)

            def split_y(h, sig):
                fence()
                V.tensor_copy(y_hi[:, h, :], tmp640[:, :])
                fence()
                tt(y_lo[:, h, :], tmp640[:, :], y_hi[:, h, :].bitcast(f32), ALU.subtract).then_inc(sig.sem, sig.step)

            def unit_lo(layer, b, h, j):
                split_lo(layer, h * UNIT + (base(b) + j), j)

            def rms(layer, tile, sq, ss, rn, n_ss, done):
                mul(sq, tile, tile)
                fence()
                V.tensor_reduce(stat[:, 0:5], sq, AX.X, ALU.add)
                fence()
                V.tensor_scalar(stat[:, 0:5], stat[:, 0:5], 1.0 / 128, EPS, ALU.mult, ALU.add).then_inc(ss.sem, ss.step)
                dve.wait_ge(rn.sem, rn.at(layer, n_ss))
                mul(tile, tile, per_tile(stat[:, 0:5])).then_inc(done.sem, done.step)

            with dve.Fori(0, DEPTH) as layer:
                vec = lambda c, n=1: vecs[:, layer, c:c + n]
                dve.wait_ge(layer_in2[0].sem, layer_in2[0].at(layer, 1))
                lv4 = lam_in[:, :].rearrange("p (a b c) -> p a b c", a=2, b=2)
                mul(tmp640[:, 0:128].rearrange("p (a c) -> p a c", a=2), lv4[:, :, 0, :], lv4[:, :, 1, :])
                fence()
                V.tensor_reduce(lam_s[:, 0:2], tmp640[:, 0:128].rearrange("p (a c) -> p a c", a=2), AX.X, ALU.add).then_inc(lam_v.sem, lam_v.step)
                dve.wait_ge(x_ss.sem, x_ss.at(layer, 1))
                V.tensor_scalar(stat[:, 0:5], stat[:, 0:5], 1.0 / D, EPS, ALU.mult, ALU.add).then_inc(x_sq.sem, x_sq.step)
                dve.wait_ge(x_rn.sem, x_rn.at(layer, 1))
                for t in range(TILES):
                    last = V.tensor_scalar(x_n_v[:, t, :], x_tm[:, t, :], stat[:, t:t + 1], None, ALU.mult)
                last.then_inc(x_n.sem, x_n.step)
                dve.wait_ge(lam_e.sem, lam_e.at(layer, 1))
                tt(lam_s[:, 4:5], lam_s[:, 3:4], lam_s[:, 2:3], ALU.subtract)
                V.tensor_scalar(lam_s[:, 5:6], vec(V_LAM), -1.0, 1.0, ALU.mult, ALU.add)
                fence()
                tt(lam_s[:, 4:5], lam_s[:, 4:5], vec(V_LAM), ALU.subtract)
                mul(lam_s[:, 5:6], lam_s[:, 5:6], vec(V_DIFF)).then_inc(lam_v.sem, lam_v.step)
                dve.wait_ge(mod_t.sem, mod_t.at(layer, 1))
                add(mod, M[:, 1536:1584].rearrange("p (k g) -> p k g", g=2), over(vec(V_BMOD, 24).unsqueeze(2), 24, 2))
                fence()
                V.scalar_tensor_tensor(g_scale, mod[:, 8:16, :], 1.0, over(vec(V_PRE, 8).unsqueeze(2), 8, 2), ALU.add, ALU.mult)
                mul(gate_post, mod[:, 16:24, :].rearrange("p k g -> p g k"), over(vec(V_POST, 8).unsqueeze(1), 2, 8)).then_inc(mod_ready.sem, mod_ready.step)
                dve.wait_ge(layer_in2[1].sem, layer_in2[1].at(layer, 1))
                V.tensor_copy(ab_w_hi[:, :], ab_w[:, :])
                fence()
                tt(ab_w_lo[:, :], ab_w[:, :], ab_w_hi[:, :].bitcast(f32), ALU.subtract).then_inc(ab_split.sem, ab_split.step)
                for k in range(KT):
                    dve.wait_ge(ht_raw.sem, ht_raw.at(layer, k + 1))
                    V.tensor_copy(h_hi_v[:, k, :], gate_sg[:, k % 2, :])
                    fence()
                    tt(h_lo_v[:, k, :], gate_sg[:, k % 2, :], h_hi_v[:, k, :].bitcast(f32), ALU.subtract).then_inc(h_ready.sem, h_ready.step)
                    if k in (3, 5):
                        split_lo(layer, k // 2 - 1, k // 2 - 1)
                x, turns = hid_tmp[0:HY_FF, 0, :], tmp640[0:HY_FF, :]

                def argument(j):
                    dve.wait_ge(hid_mm.sem, hid_mm.at(layer, j + 1))
                    V.tensor_scalar(x, M[0:HY_FF, 0:NT], vecs[0:HY_FF, layer, V_HB1 + j:V_HB1 + j + 1], None, ALU.add)
                    fence()
                    V.tensor_scalar(turns, x, 1.0 / (2 * math.pi), MAGIC, ALU.mult, ALU.add)
                    fence()
                    V.tensor_scalar(turns, turns, MAGIC, None, ALU.subtract)
                    fence()
                    V.scalar_tensor_tensor(x, turns, -6.28125, x, ALU.mult, ALU.add)
                    fence()
                    V.scalar_tensor_tensor(x, turns, -(2 * math.pi - 6.28125), x, ALU.mult, ALU.add)
                    fence()
                    V.tensor_scalar(x, x, 3.1415925, -3.1415925, ALU.min, ALU.max).then_inc(hid_arg.sem, hid_arg.step)

                argument(0)
                ab = lambda i: ab_s[:, 40 * i:40 * i + 40]
                dht = lambda v: v.rearrange("p (d h t) -> p d h t", d=2, h=4)
                dve.wait_ge(ab_mm.sem, ab_mm.at(layer, 1))
                fence()
                V.tensor_copy(tmp640[0:16, :], M[0:16, 1024:1024 + NT]).then_inc(ab_row.sem, ab_row.step)
                dve.wait_ge(ab_t.sem, ab_t.at(layer, 1))
                src = M[:, AB_AT:AB_AT + 80].rearrange("p (t d k h) -> p k d h t", t=5, d=2, k=2)
                for d in range(2):
                    add(dht(ab(6))[:, d], src[:, 0, d], over(vecs[:, layer, V_DT + 4 * d:V_DT + 4 * d + 4].unsqueeze(2), 4, 5))
                    V.tensor_copy(dht(ab(7))[:, d], src[:, 1, d])
                fence()
                V.scalar_tensor_tensor(ab(8), ab(6), -1.0, ab(6), ALU.mult, ALU.max).then_inc(ab_v.sem, ab_v.step)
                dve.wait_ge(ab_l.sem, ab_l.at(layer, 1))
                V.scalar_tensor_tensor(ab(6), ab(6), 0.0, ab(8), ALU.max, ALU.add)
                V.tensor_scalar(ab(9), ab(9), 1.0, None, ALU.add)
                fence()
                V.reciprocal(ab(1), ab(9))
                V.scalar_tensor_tensor(ab(0).rearrange("p (a t) -> p a t", t=5), ab(6).rearrange("p (a t) -> p a t", t=5), -1.0,
                                               over(exp_alog[:, :].unsqueeze(2), 8, 5), ALU.mult, ALU.mult).then_inc(ab_v.sem, ab_v.step)
                argument(1)
                dve.wait_ge(gc_mm.sem, gc_mm.at(layer, 1))
                V.tensor_copy(ab(8), M[:, GC_AT:GC_AT + 40])
                V.tensor_copy(ab(7), M[:, GC_AT + 64:GC_AT + 104])
                fence()
                tt(ab(3), ab(7), ab(8), ALU.subtract).then_inc(ab_v.sem, ab_v.step)
                dve.wait_ge(gc_e.sem, gc_e.at(layer, 1))
                mul(ab(5), ab(1), ab(2)).then_inc(ab_done.sem, ab_done.step)
                split_lo(layer, 2, 2)
                split_lo(layer, 3, 3)

                def convolve(out, h, first, sig):
                    w = lambda i: small[:, layer * HEADS + h, first + i:first + i + 1]
                    V.tensor_scalar(out, pad[:, 1:1 + SP1], w(1), None, ALU.mult)
                    fence()
                    V.scalar_tensor_tensor(out, pad[:, 0:SP1], w(0), out, ALU.mult, ALU.add)
                    fence()
                    V.scalar_tensor_tensor(out, pad[:, 2:2 + SP1], w(2), out, ALU.mult, ALU.add).then_inc(sig.sem, sig.step)

                with dve.Fori(0, HEADS) as h:
                    def col(i, d, t=None):
                        if t is None:
                            return ab_s[:, bass.ds(h * 5 + (40 * i + 20 * d), 5)]
                        return ab_s[:, bass.ds(h * 5 + (40 * i + 20 * d + t), 1)]

                    for j in range(3):
                        if j == 2:
                            unit_lo(layer, 0, h, 4)
                        dve.wait_ge(proj_taken.sem, proj_taken.at(layer, h * UNIT + (pbase(0) + j + 1)))
                        convolve(A_c[:, j, :], h, 3 * j, A_conv)
                    for d in range(2):
                        last = mul(g1[:, d, :, :], per_tile(col(0, d)), all_tiles(strict[:, d, :]))
                    last.then_inc(A_g1.sem, A_g1.step)
                    unit_lo(layer, 0, h, 5)
                    dve.wait_ge(A_tm.sem, A_tm.at(layer, h + 1))
                    mul(sq_a.rearrange("p (a c) -> p a c", c=128), A_tmv[:, 0:2, :, :].rearrange("p w t c -> p (w t) c"),
                        A_tmv[:, 0:2, :, :].rearrange("p w t c -> p (w t) c"))
                    fence()
                    V.tensor_reduce(stat[:, 0:10], sq_a.rearrange("p (a c) -> p a c", c=128), AX.X, ALU.add)
                    fence()
                    V.tensor_scalar(stat[:, 0:10], stat[:, 0:10], EPS, None, ALU.add).then_inc(A_ss.sem, A_ss.step)
                    def decays(d):
                        dve.wait_ge(A_dec.sem, A_dec.at(layer, h * 2 + (d + 1)))
                        mul(dec[:, d, :, :], dec[:, d, :, :], all_tiles(strict[:, d, :]))
                        mul(decT[:, d, :, :], decT[:, d, :, :], all_tiles(tri[:, d, :]))
                        fence()
                        mul(dec[:, d, :, :], dec[:, d, :, :], per_tile(col(1, d)))

                    decays(0)
                    dve.wait_ge(A_rn.sem, A_rn.at(layer, h * 2 + 1))
                    V.tensor_scalar(stat[:, 0:5], stat[:, 0:5], 128.0 ** -0.5, None, ALU.mult)
                    mul(kqn[:, :, 0, :], A_tmv[:, 1, :, :], per_tile(stat[:, 5:10]))
                    fence()
                    mul(kqn[:, :, 1, :], A_tmv[:, 0, :, :], per_tile(stat[:, 0:5])).then_inc(A_kqn.sem, A_kqn.step)
                    decays(1)
                    for d in range(2):
                        mul(Rk[:, d, :, :], kqn[:, :, 0, :], per_tile(col(5, d)))
                        mul(kd[:, d, :, :], kqn[:, :, 0, :], per_tile(col(3, d)))
                    for d in range(2):
                        mul(Rv[:, d, :, :], A_tmv[:, 2, :, :], per_tile(col(1, d)))
                    V.memset(o_tm, 0.0)
                    fence()
                    dve.wait_ge(A_gram.sem, A_gram.at(layer, h + 1))
                    gram = M[:, 0:1280].rearrange("p (t j c) -> p t j c", t=5, j=2)
                    for d in range(2):
                        mul(dec[:, d, :, :], dec[:, d, :, :], gram[:, :, 0, :])
                        last = mul(decT[:, d, :, :], decT[:, d, :, :], gram[:, :, 1, :])
                    last.then_inc(A_lat.sem, A_lat.step)
                    unit_lo(layer, 0, h, 6)
                    def update(lv, kind="inner"):
                        e = h * (3 * LEVELS) + lv * 3
                        fence()
                        V.tensor_copy(level_now[:, :], level[:, lv, :])
                        fence()
                        lower, upper = (over(level_v[:, i, :].unsqueeze(1), 4, 128) for i in range(2))
                        quad = lambda at: M[:, at:at + 512].rearrange("p (t c) -> p t c", c=128)
                        pair = lambda at: M[:, at:at + 256].rearrange("p (t c) -> p t c", c=128)
                        first = kind == "first"
                        jobs = (((X[:, 0, 0:4, :], lower, Qn[:, 0, 0:4, :] if first else quad(1536)), (XT[:, 0, 0:4, :], upper, quad(0))),
                                ((X[:, 1, 0:4, :], upper, Qn[:, 1, 0:4, :] if first else quad(512)), (XT[:, 1, 0:4, :], lower, quad(1024))),
                                ((X[:, :, 4, :], level_v[:, 0:2, :], Qn[:, :, 4, :] if first else pair(1536)),
                                 (XT[:, :, 4, :], level_v[:, 1:3, :], pair(1792))))
                        for gi, job in enumerate(jobs):
                            dve.wait_ge(A_d.sem, A_d.at(layer, e + (gi + 1)))
                            held(dve)
                            for out, mask, data in job[1:] if kind == "last" else job:
                                last = V.copy_predicated(out, mask, data)
                            last.then_inc(A_x.sem, A_x.step)

                    dve.wait_ge(A_x0.sem, A_x0.at(layer, h + 1))
                    update(0, "first")
                    with dve.Fori(1, LEVELS - 1) as lv:
                        update(lv)
                    update(LEVELS - 1, "last")
                    for n in range(5):
                        ts = (n, 3 - n) if n < 4 else (4, 4)
                        dve.wait_ge(A_sb.sem, A_sb.at(layer, h * 5 + (n + 1)))
                        fence()
                        oa = [M[:, 1536 + 128 * d:1664 + 128 * d] for d in range(2)]
                        if n < 4:
                            for d, t in enumerate(ts):
                                V.scalar_tensor_tensor(S[:, d, :], S[:, d, :], col(4, d, t), M[:, 1792 + 128 * d:1920 + 128 * d], ALU.mult, ALU.add)
                                V.scalar_tensor_tensor(o_tm[:, t, :], M[:, 1280 + 128 * d:1408 + 128 * d], col(2, d, t), o_tm[:, t, :], ALU.mult, ALU.add)
                            fence()
                            for d, t in enumerate(ts):
                                last = add(o_tm[:, t, :], o_tm[:, t, :], oa[d])
                        else:
                            dve.wait_ge(A_stored.sem, A_stored.at(layer, h))
                            V.tensor_copy(S_out, M[:, 1792:2048].rearrange("p (d c) -> p d c", d=2))
                            V.tensor_copy(o_tm[:, 4, :], oa[0])
                            fence()
                            last = add(o_tm[:, 4, :], o_tm[:, 4, :], oa[1])
                        last.then_inc(A_su.sem, A_su.step)
                    fence()
                    rms(layer, o_tm, sq_a[:, 0:NT].rearrange("p (t c) -> p t c", t=5), A_ss, A_rn, h * 2 + 2, A_o)
                    dve.wait_ge(A_ot.sem, A_ot.at(layer, h + 1))
                    fence()
                    V.scalar_tensor_tensor(tmp640[:, :], M[:, 0:NT], vec(V_GDN), A_zb, ALU.mult, ALU.mult)
                    split_y(h, A_y)
                    unit_lo(layer, 0, h, 7)

                def split_merged(k):
                    fence()
                    V.tensor_copy(h_hi_v[:, k, :], merged[:, k, :])
                    fence()
                    tt(h_lo_v[:, k, :], merged[:, k, :], h_hi_v[:, k, :].bitcast(f32), ALU.subtract).then_inc(m_split.sem, m_split.step)

                def merge(b):
                    def pair(i, q, ahead=True):
                        n = i * 6 + (base(b) + HEADS * UNIT + 3 * q)
                        p = i * 4 + (pbase(b) + HEADS * UNIT + 2 * q)
                        if not ahead:
                            dve.wait_ge(block_done.sem, block_done.at(layer, n + 2))
                            for k in range(KT - 2):
                                split_merged(k)
                        for s in range(2):
                            if s == 0:
                                dve.wait_ge(br_mm.sem, br_mm.at(layer, i * 2 + (4 * b + q + 1)))
                            else:
                                dve.wait_ge(block_done.sem, block_done.at(layer, n + 3))
                            dve.wait_ge(proj_taken.sem, proj_taken.at(layer, p + s + 1))
                            br, out = M[:, 1024 * s:1024 * s + NT], merged[:, i * 4 + (2 * q + s), :]
                            if b == 0:
                                last = mul(out, gate_sg[:, s, :], br)
                            else:
                                fence()
                                mul(tmp640[:, :], gate_sg[:, s, :], br)
                                fence()
                                last = add(out, out, tmp640[:, :])
                            last.then_inc(merged_step.sem, merged_step.step)
                            if not ahead:
                                split_merged(KT - 2 + s)
                            if s == 0:
                                split_lo(layer, n + 4, q + 4)
                        if ahead:
                            split_lo(layer, n + 5, q + 5)
                            split_lo(layer, n + 6, q + 6)

                    if b < 3:
                        with dve.Fori(0, 2) as i:
                            for q in range(2):
                                pair(i, q)
                    else:
                        for q in range(4):
                            pair(q // 2, q % 2, q < 3)

                merge(0)

                dve.wait_ge(layer_in2[5].sem, layer_in2[5].at(layer, 1))
                V.scalar_tensor_tensor(dec_abs, dec_abs, -1.0, dec_abs, ALU.mult, ALU.max).then_inc(dec_ready_l.sem, dec_ready_l.step)
                parts = ((slice(0, SAMPLE), slice(0, SAMPLE)), (slice(SAMPLE, NT), slice(SAMPLE + 1, SP1)))
                with dve.Fori(0, HEADS) as h:
                    skip = lambda r: small[:, layer * HEADS + h, 18 + r:19 + r]
                    for j in range(4):
                        if j >= 2:
                            unit_lo(layer, 1, h, j + 2)
                        if j < 3:
                            dve.wait_ge(proj_taken.sem, proj_taken.at(layer, h * UNIT + (pbase(1) + j + 1)))
                            convolve(B_c[:, j, :], h, 9 + 3 * j, B_conv)
                        if j == 0:
                            dve.wait_ge(B_win.sem, B_win.at(layer, h + 1))
                            dve.wait_ge(B_filt_mm.sem, B_filt_mm.at(layer, h + 1))
                            fence()
                            mul(filt, M[:, 0:1280].rearrange("p (t c) -> p t c", t=5), win).then_inc(B_filt.sem, B_filt.step)
                    re, im = (M[:, x:x + 512].rearrange("p (f c) -> p f c", f=4) for x in (1024, 1536))
                    for r in range(2):
                        dve.wait_ge(B_u.sem, B_u.at(layer, h * 2 + (r + 1)))
                        Hr, Hi = Hf[:, 0:4, r, :], Hf[:, 4:8, r, :]
                        fence()
                        mul(t1, re, Hr)
                        mul(t2, im, Hi)
                        fence()
                        tt(Yf[:, 0:4, :], t1, t2, ALU.subtract)
                        fence()
                        mul(t1, re, Hi)
                        mul(t2, im, Hr)
                        fence()
                        add(Yf[:, 4:8, :], t1, t2).then_inc(B_y0.sem, B_y0.step)
                        if r == 0:
                            dve.wait_ge(proj_taken.sem, proj_taken.at(layer, h * UNIT + (pbase(1) + 4)))
                            mul(B_c[:, 2, :], B_c[:, 2, :], B_gb)
                        dve.wait_ge(B_inv.sem, B_inv.at(layer, h * 2 + (r + 1)))
                        if r == 0:
                            for o, c in parts:
                                V.scalar_tensor_tensor(z1[:, o], B_c[:, 0, c], skip(0), M[:, o], ALU.mult, ALU.add)
                            fence()
                            for o, c in parts:
                                last = mul(z1[:, o], z1[:, o], B_c[:, 1, c])
                            last.then_inc(B_z1.sem, B_z1.step)
                            unit_lo(layer, 1, h, 6)
                        else:
                            fence()
                            V.scalar_tensor_tensor(tmp640[:, :], z1, skip(1), M[:, 0:NT], ALU.mult, ALU.add)
                            fence()
                            for o, c in parts:
                                mul(tmp640[:, o], tmp640[:, o], B_c[:, 2, c])
                            split_y(h, B_y)
                            unit_lo(layer, 1, h, 7)
                merge(1)

                with dve.Fori(0, HEADS) as h:
                    unit_lo(layer, 2, h, 4)
                    dve.wait_ge(C["in2"].sem, C["in2"].at(layer, h + 1))

                    def logits(m):
                        dve.wait_ge(C["s"].sem, C["s"].at(layer, h * 5 + (m + 1)))
                        if m >= 2:
                            dve.wait_ge(C["pt_mm"].sem, C["pt_mm"].at(layer, h * 5 + (m - 1)))
                        s = s_buf[:, m % 2, :]
                        if m < 4:
                            add(s[:, 0:SAMPLE], M[:, 0:SAMPLE], bias[:, (6 - 2 * m) * GRID_W:(6 - 2 * m) * GRID_W + SAMPLE])
                        V.tensor_copy(s[:, SAMPLE:NT], M[:, SAMPLE:NT])
                        fence()
                        V.tensor_reduce(stat[:, m:m + 1], s if m < 4 else s[:, SAMPLE:NT], AX.X, ALU.max, negate=True).then_inc(C["mx"].sem, C["mx"].step)

                    logits(0)
                    unit_lo(layer, 2, h, 5)
                    for m in range(5):
                        if m < 4:
                            logits(m + 1)
                        dve.wait_ge(C["p"].sem, C["p"].at(layer, h * 5 + (m + 1)))
                        V.reciprocal(stat[:, 16 + m:17 + m], stat[:, 8 + m:9 + m])
                        fence()
                        cols = slice(0 if m < 4 else SAMPLE, NT)
                        V.tensor_scalar(s_buf[:, m % 2, cols], s_buf[:, m % 2, cols], stat[:, 16 + m:17 + m], None, ALU.mult).then_inc(C["pn"].sem, C["pn"].step)
                        if m in (2, 4):
                            unit_lo(layer, 2, h, 5 + m // 2)
                    dve.wait_ge(C["pv"].sem, C["pv"].at(layer, h + 1))
                    fence()
                    mul(tmp640[:, :], M[:, 0:NT], gT)
                    split_y(h, C["y"])
                merge(2)

                with dve.Fori(0, HEADS) as h:
                    unit_lo(layer, 3, h, 4)
                    dve.wait_ge(rope_in[0].sem, rope_in[0].at(layer, 1))
                    dve.wait_ge(rope_in[1].sem, rope_in[1].at(layer, 1))
                    dve.wait_ge(Dd["tr"].sem, Dd["tr"].at(layer, h + 1))
                    for i, x_ in enumerate((qT, kT)):
                        mul(rope_tmp, M[:, 512 * i:512 * i + 512], sinT)
                        mul(x_[:, 0:SAMPLE], x_[:, 0:SAMPLE], cosT)
                        fence()
                        last = add(x_[:, 0:SAMPLE], x_[:, 0:SAMPLE], rope_tmp)
                        if i == 0:
                            fence()
                    last.then_inc(Dd["rope"].sem, Dd["rope"].step)
                    unit_lo(layer, 3, h, 5)

                    def maxima(m):
                        dve.wait_ge(Dd["s"].sem, Dd["s"].at(layer, h * 5 + (m + 1)))
                        first = 0 if m < 4 else SAMPLE
                        for i in range(2):
                            V.tensor_reduce(stat[:, 2 * m + i:2 * m + i + 1], D_scores[i][:, first:NT], AX.X, ALU.max,
                                            negate=True).then_inc(Dd["mx"].sem, Dd["mx"].step)

                    def weigh(m):
                        dve.wait_ge(Dd["pv"].sem, Dd["pv"].at(layer, h * 5 + (m + 1)))
                        V.tensor_scalar(d_o[:, m, :], M[:, NT:NT + 128], stat[:, 32 + 2 * m:33 + 2 * m], None, ALU.mult).then_inc(Dd["o"].sem, Dd["o"].step)

                    maxima(0)
                    for m in range(5):
                        dve.wait_ge(Dd["p"].sem, Dd["p"].at(layer, h * 5 + (m + 1)))
                        first = 0 if m < 4 else SAMPLE
                        sums, rec = stat[:, 16 + 2 * m:18 + 2 * m], stat[:, 32 + 2 * m:34 + 2 * m]
                        p0, p1 = s_buf[:, 2 * (m % 2), first:NT], s_buf[:, 2 * (m % 2) + 1, first:NT]
                        V.reciprocal(rec, sums)
                        fence()
                        V.scalar_tensor_tensor(stat[:, 48 + m:49 + m], sums[:, 0:1], rec[:, 1:2], lam_s[:, 4:5], ALU.mult, ALU.mult)
                        fence()
                        V.scalar_tensor_tensor(p0, p1, stat[:, 48 + m:49 + m], p0, ALU.mult, ALU.add).then_inc(Dd["pn"].sem, Dd["pn"].step)
                        if m:
                            weigh(m - 1)
                        if m < 4:
                            maxima(m + 1)
                    weigh(4)
                    fence()
                    rms(layer, d_o, d_sq.rearrange("p (t c) -> p t c", t=5), Dd["ss"], Dd["rn"], h + 1, Dd["on"])
                    unit_lo(layer, 3, h, 6)
                    dve.wait_ge(Dd["ot"].sem, Dd["ot"].at(layer, h + 1))
                    fence()
                    V.scalar_tensor_tensor(tmp640[:, :], M[:, 0:NT], lam_s[:, 5:6], gT, ALU.mult, ALU.mult)
                    split_y(h, Dd["y"])
                    unit_lo(layer, 3, h, 7)
                mul(diag, over(ident[:, :].unsqueeze(1), 16, 128),
                    over(gate_post_t[:, :].unsqueeze(2), 16, 128)).then_inc(gate_diag.sem, gate_diag.step)
                merge(3)

                for n in range(OUT_BLOCKS):
                    if n < OUT_BLOCKS - 2:
                        split_lo(layer, base(4) + n + 2, n + 2)
                    dve.wait_ge(yt_mm.sem, yt_mm.at(layer, n + 1))
                    V.tensor_copy(y_tm[:, :, 128 * n:128 * n + 128],
                                         M[:, 1024 * (n % 2):1024 * (n % 2) + NT].rearrange("p (t c) -> p t c", t=5)).then_inc(ytm.sem, ytm.step)
                dve.wait_ge(y_ss.sem, y_ss.at(layer, 1))
                V.tensor_scalar(stat[:, 0:5], stat[:, 0:5], 1.0 / D, EPS, ALU.mult, ALU.add).then_inc(y_sq.sem, y_sq.step)
                dve.wait_ge(y_rn.sem, y_rn.at(layer, 1))
                dve.wait_ge(gate_bc.sem, gate_bc.at(layer, 1))
                for t in range(TILES):
                    V.scalar_tensor_tensor(y_tm[:, t, :], y_tm[:, t, :], stat[:, t:t + 1], gate_b[:, int(t == 4), :], ALU.mult, ALU.mult)
                dve.wait_ge(x_reload.sem, x_reload.at(layer, 1))
                fence()
                add(x_tm, x_tm, y_tm).then_inc(x_new.sem, x_new.step)


def layouts(x):
    f = lambda n: np.ascontiguousarray(np.asarray(x[n]))
    A = np.ascontiguousarray

    def blocks(w):
        *lead, k, n = w.shape
        w = w.reshape(*lead, k // 128, 128, n // 128, 128)
        w = np.moveaxis(w, (-2, -3), (len(lead), len(lead) + 1))
        return w.reshape(*lead, n // 128, 128, k)

    w_in = f("w_in")
    sections = [w_in[..., 0:2048], w_in[..., 2064:4112], w_in[..., 4112:6160], w_in[..., 6160:8208]]
    w4 = np.stack([s.reshape(DEPTH, D, 4, HEADS, 128).transpose(0, 1, 3, 2, 4).reshape(DEPTH, D, 2048) for s in sections], 1)
    w_gate = blocks(f("w_merge").reshape(DEPTH, D, 4, D).transpose(0, 2, 1, 3)).reshape(DEPTH, 4, 4, 2, 128, D)
    w_branch = blocks(f("w_branch")).reshape(DEPTH, 4, 4, 2, 128, D // 2).transpose(0, 1, 2, 4, 3, 5).reshape(DEPTH, 4, 4, 1, 128, D)
    vec = lambda v: v.reshape(DEPTH, -1, 128).transpose(2, 0, 1)
    rows = lambda v: np.broadcast_to(v.reshape(1, DEPTH, -1), (128, DEPTH, v.size // DEPTH))
    ff = lambda v: np.concatenate([v, np.zeros_like(v)], 1).T.reshape(128, DEPTH, 1)
    lam_init = np.array([0.8 - 0.6 * math.exp(-0.3 * i) for i in range(DEPTH)], np.float32)
    vecs = np.concatenate([
        vec(f("g_pre")), vec(f("g_post")), vec(f("b_mod")), vec(f("gdn_norm")), vec(f("diff_norm")),
        ff(f("hy_b1")), ff(f("hy_b2")), np.broadcast_to(lam_init.reshape(1, DEPTH, 1), (128, DEPTH, 1)),
        rows(f("gdn_dt_bias")), rows(f("gdn_a_log")), vec(f("b_merge"))], 2)
    conv = lambda n: f(n).reshape(DEPTH, 3, 3, HEADS, 128).transpose(4, 0, 3, 2, 1).reshape(128, DEPTH, HEADS, 9)
    skip = f("hy_skip").reshape(DEPTH, 2, HEADS, 128).transpose(3, 0, 2, 1)
    small = np.concatenate([conv("gdn_conv"), conv("hy_conv"), skip], 3)
    w12 = np.zeros((DEPTH, HY_FF, 2 * HY_FF), np.float32)
    w12[:, :HY_EMB, :HY_FF] = f("hy_w1")
    w12[:, :, HY_FF:] = f("hy_w2")
    w3 = np.concatenate([f("hy_w3"), f("hy_b3")[:, None, :]], 1).reshape(DEPTH, 65, 2, HEADS, 128).transpose(0, 1, 3, 2, 4)
    decay = f("hy_decay").reshape(DEPTH, 1, 2, HEADS, 128).transpose(0, 1, 3, 2, 4)
    cond = np.stack([f("c")[0], f("c_ctx")], -1).reshape(KT, 128, 2).transpose(1, 0, 2)
    state = f("state_gdn")[0].transpose(0, 2, 3, 1, 4)
    nat, diff = f("cache_nat_kv")[0], f("cache_diff_kv")[0]
    q, k = np.arange(GRID_W)[:, None], np.arange(GRID_W)[None, :]
    start = np.clip(q - WIN_C // 2, 0, GRID_W - WIN_C)
    inside = (k >= start) & (k < start + WIN_C)
    offset = np.where(inside, k - q + WIN_C - 1, 0)
    rpb = f("nat_rpb")
    table = np.where(inside, rpb[..., offset], np.float32(-1e30)).astype(rpb.dtype)
    half = lambda a: table[:, :, a:a + 14].transpose(0, 1, 3, 2, 4)
    bias = np.concatenate([half(1), half(0)], 2)
    return {
        "w_mod": blocks(f("w_mod")), "w_in": blocks(w4), "w_out": blocks(f("w_out")),
        "w_mb": A(np.concatenate([w_gate, w_branch], 3).reshape(DEPTH, 4, MERGE_BLOCKS, 128, D)),
        "x_sample": f("x_sample")[0], "x_prompt": f("x_prompt")[0],
        "vecs": A(vecs.reshape(128, -1)), "small": A(small.reshape(128, -1)), "w12": w12,
        "w3": A(w3.reshape(DEPTH, 65, 1024)), "decay": A(decay.reshape(DEPTH, 1, 1024)),
        "cond": A(cond.reshape(128, 16)), "state": A(state.reshape(DEPTH, HEADS, 128, 256)),
        "lam": f("diff_lam").reshape(DEPTH, 1, 256),
        "ab_w": A(w_in[..., 2048:2064].reshape(DEPTH, KT, 128, 16).transpose(0, 2, 1, 3).reshape(DEPTH, 128, 128)),
        "nat_kT": A(nat[:, 0].transpose(0, 1, 3, 2)), "nat_v": A(nat[:, 1]),
        "diff_kT": A(diff[:, 0].transpose(0, 1, 3, 2)), "diff_v": A(diff[:, 1]),
        "bias": A(bias.reshape(DEPTH, HEADS, 128, BIAS_W)),
    }


def constants():
    r, c = np.arange(128)[:, None], np.arange(128)[None, :]
    F = np.float32
    out = {"ident": (r == c).astype(F), "ones": np.ones((128, 128), F),
           "tri": np.concatenate([r <= c, r >= c], 1).astype(F), "strict": np.concatenate([r > c, r < c], 1).astype(F)}
    level = []
    for s in range(LEVELS):
        lower = ((r >> (s + 1)) == (c >> (s + 1))) & (((r >> s) & 1) == 1) & (((c >> s) & 1) == 0)
        level += [lower, lower.T, lower]
    out["level"] = np.concatenate(level, 1).astype(F)
    out["swap"] = ((r ^ 32) == c).astype(F)
    p = np.arange(128)
    out["dist"] = np.stack([-np.abs(p + 128 * t - SAMPLE // 2) / SAMPLE for t in range(4)] + [-np.abs(p - PROMPT // 2) / PROMPT], 1).astype(F)
    feats = []
    for n in (SAMPLE, PROMPT):
        t = np.arange(n, dtype=np.float64) / n
        ang = 2 * math.pi * t[:, None] * np.arange(1, BANDS + 1)
        feats.append(np.concatenate([t[:, None], np.cos(ang), np.sin(ang)], 1).T)
    out["feat"] = np.concatenate(feats, 1).astype(F)
    for name, n in (("s", SAMPLE), ("p", PROMPT)):
        m = 3 * n // 2
        t, k = np.arange(n)[:, None], np.arange(m // 2)[None, :]
        w = 2 * math.pi * (k + 0.5) / m
        re, im = np.cos(w * t), -np.sin(w * t)
        ire, iim = 2 / m * np.cos(w * (t + n // 2)), -2 / m * np.sin(w * (t + n // 2))
        if name == "s":
            fw = np.concatenate([re, im], 1).reshape(4, 128, 6, 128).transpose(1, 0, 2, 3)
            iv = np.concatenate([ire.T, iim.T], 0).reshape(6, 128, n).transpose(1, 0, 2)
        else:
            z = np.zeros((n, 128 - m // 2))
            fw = np.stack([np.concatenate([re, z], 1), np.concatenate([im, z], 1)], 1)
            iv = np.stack([np.concatenate([ire, z], 1).T, np.concatenate([iim, z], 1).T], 1)
        out[f"F_{name}"] = fw.reshape(128, -1).astype(F)
        out[f"Fi_{name}"] = iv.reshape(128, -1).astype(F)
    nf = 16
    inv = 10000.0 ** (-np.arange(nf) / nf)
    t = np.arange(SAMPLE)
    ang = np.concatenate([(t // GRID_W)[:, None] * inv, (t % GRID_W)[:, None] * inv], 1).T
    out["cos"] = np.concatenate([np.cos(ang)] * 4, 0).astype(F)
    out["sin"] = np.concatenate([-np.sin(ang), np.sin(ang)] * 2, 0).astype(F)
    return {k: np.ascontiguousarray(v) for k, v in out.items()}


def kernel(**inputs):
    import concourse.bacc as bacc
    from concourse.bass_utils import run_bass_kernel_spmd as run

    nc = bacc.Bacc("TRN2", target_bir_lowering=False, num_devices=1)
    arrays = {**layouts(inputs), **constants()}
    arrays = {f"in_{k}": np.ascontiguousarray(v) for k, v in arrays.items()}
    I = {k[3:]: nc.dram_tensor(k, v.shape, mybir.dt.from_np(v.dtype), kind="ExternalInput").ap() for k, v in arrays.items()}
    f32 = mybir.dt.float32
    shapes = {"x": (NT, D), "state": (DEPTH, HEADS, 128, 256), "nat": (DEPTH, 2, HEADS, 128, 128), "diff": (DEPTH, 2, HEADS, 128, 128)}
    O = {k: nc.dram_tensor(f"out_{k}", s, f32, kind="ExternalOutput").ap() for k, s in shapes.items()}
    program(nc, I, O)
    r = run(nc, [arrays], core_ids=[0]).results[0]
    state = r["out_state"].reshape(DEPTH, HEADS, 128, 2, 128).transpose(0, 3, 1, 2, 4)
    return (r["out_x"][None, SAMPLE:], r["out_x"][None, :SAMPLE], np.ascontiguousarray(state)[None],
            r["out_nat"][None], r["out_diff"][None])
```
